# Optimizing a Trainium2 kernel written in Bass

```python
import jax, jax.numpy as jnp
from jax import lax
import numpy as np
import math
import jax
import jax.numpy as jnp

D_MODEL = 1024
BATCH = 1
SEQ = 256
DEPTH = 2

CHUNK = 64
BRANCH_W = 512
N_BRANCH = 3
EPS = 1e-6
SG_BLOCK = 128
SG_GROUPS = 4
SG_GROUP_W = BRANCH_W // SG_GROUPS
MLA_HEADS = 8
MLA_NOPE = 64
MLA_ROPE = 32
MLA_QK = MLA_NOPE + MLA_ROPE
MLA_V = 64
MLA_Q_RANK = 256
MLA_KV_RANK = 128
ROPE_THETA = 10000.0
Q_BLOCK = 128
GLA_HEADS = 4
GLA_DK = 64
GLA_DV = 128
GLA_GATE_RANK = 16
GLA_TAU = 16.0

SPLITS = (BRANCH_W, BRANCH_W, BRANCH_W,
          MLA_Q_RANK, MLA_KV_RANK, MLA_ROPE, MLA_HEADS * MLA_V,
          GLA_HEADS * GLA_DK, GLA_HEADS * GLA_DK, GLA_HEADS * GLA_DV,
          GLA_GATE_RANK, GLA_HEADS * GLA_DV,
          N_BRANCH * D_MODEL)
IN_COLS = sum(SPLITS)


def _rmsnorm(x, g):
    x32 = x.astype(jnp.float32)
    y = x32 * lax.rsqrt(jnp.mean(x32 * x32, axis=-1, keepdims=True) + EPS)
    return (y * g.astype(jnp.float32)).astype(x.dtype)

def _layernorm(x, g, b):
    x32 = x.astype(jnp.float32)
    mu = jnp.mean(x32, axis=-1, keepdims=True)
    xc = x32 - mu
    y = xc * lax.rsqrt(jnp.mean(xc * xc, axis=-1, keepdims=True) + EPS)
    return (y * g.astype(jnp.float32) + b.astype(jnp.float32)).astype(x.dtype)

def _split_cols(proj):
    idx = np.cumsum(np.array(SPLITS))[:-1].tolist()
    return jnp.split(proj, idx, axis=-1)

def _rope_tables(positions):
    half = MLA_ROPE // 2
    inv = 1.0 / (ROPE_THETA ** (jnp.arange(half, dtype=jnp.float32) * 2.0 / MLA_ROPE))
    ang = positions.astype(jnp.float32)[..., None] * inv
    return jnp.cos(ang)[:, :, None, :], jnp.sin(ang)[:, :, None, :]

def _apply_rope(x, cos, sin):
    half = MLA_ROPE // 2
    x32 = x.astype(jnp.float32)
    x1, x2 = x32[..., :half], x32[..., half:]
    return jnp.concatenate([x1 * cos - x2 * sin, x1 * sin + x2 * cos], axis=-1).astype(x.dtype)

def _spatial_gating(u, v, z, ln_g, ln_b, w_s, b_s):
    bn, s, _ = u.shape
    u = jax.nn.gelu(u)
    v = _layernorm(jax.nn.gelu(v), ln_g, ln_b)
    nb = s // SG_BLOCK
    vb = v.reshape(bn, nb, SG_BLOCK, SG_GROUPS, SG_GROUP_W)
    cid = jnp.arange(SG_BLOCK) // CHUNK
    mask = cid[:, None] >= cid[None, :]
    w = jnp.where(mask[None], w_s, jnp.zeros_like(w_s))
    sv = jnp.einsum('gij,bnjgc->bnigc', w, vb) + b_s.T[None, None, :, :, None]
    return u * sv.reshape(bn, s, BRANCH_W) * jax.nn.silu(z)

def _chunk_causal_attention(q, k, v):
    bn, s, h, dq = q.shape
    dv = v.shape[-1]
    nb = s // Q_BLOCK
    scale = dq ** -0.5
    qb = q.reshape(bn, nb, Q_BLOCK, h, dq).transpose(1, 0, 3, 2, 4)
    kh = k.transpose(0, 2, 1, 3)
    vh = v.transpose(0, 2, 1, 3)
    k_chunk = jnp.arange(s) // CHUNK

    def one_block(args):
        qblk, bi = args
        sc = jnp.einsum('bhqd,bhkd->bhqk', qblk, kh).astype(jnp.float32) * scale
        q_chunk = (bi * Q_BLOCK + jnp.arange(Q_BLOCK)) // CHUNK
        mask = k_chunk[None, :] <= q_chunk[:, None]
        sc = jnp.where(mask, sc, -jnp.inf)
        p = jax.nn.softmax(sc, axis=-1)
        return jnp.einsum('bhqk,bhkd->bhqd', p.astype(vh.dtype), vh)

    out = lax.map(one_block, (qb, jnp.arange(nb)))
    return out.transpose(1, 0, 3, 2, 4).reshape(bn, s, h, dv)

def _mla(c_q, c_kv, k_r, z, cq_g, ckv_g, w_uq, w_ukv, q_g, k_g, cos, sin):
    bn, s, _ = c_q.shape
    q = (_rmsnorm(c_q, cq_g) @ w_uq).reshape(bn, s, MLA_HEADS, MLA_QK)
    kv = (_rmsnorm(c_kv, ckv_g) @ w_ukv).reshape(bn, s, MLA_HEADS, MLA_NOPE + MLA_V)
    k_nope, v = kv[..., :MLA_NOPE], kv[..., MLA_NOPE:]
    k_rope = jnp.broadcast_to(k_r[:, :, None, :], (bn, s, MLA_HEADS, MLA_ROPE))
    k = jnp.concatenate([k_nope, k_rope], axis=-1)
    q = _rmsnorm(q, q_g)
    k = _rmsnorm(k, k_g)
    q = jnp.concatenate([q[..., :MLA_NOPE], _apply_rope(q[..., MLA_NOPE:], cos, sin)], axis=-1)
    k = jnp.concatenate([k[..., :MLA_NOPE], _apply_rope(k[..., MLA_NOPE:], cos, sin)], axis=-1)
    o = _chunk_causal_attention(q, k, v)
    return o.reshape(bn, s, MLA_HEADS * MLA_V) * jax.nn.silu(z)

def _gla(q, k, v, g_lr, z, w_gu, b_gu, o_g):
    bn, s, _ = q.shape
    n = s // CHUNK
    f32 = jnp.float32
    qc = q.astype(f32).reshape(bn, n, CHUNK, GLA_HEADS, GLA_DK) * (GLA_DK ** -0.5)
    kc = k.astype(f32).reshape(bn, n, CHUNK, GLA_HEADS, GLA_DK)
    vc = v.astype(f32).reshape(bn, n, CHUNK, GLA_HEADS, GLA_DV)
    log_a = jax.nn.log_sigmoid((g_lr @ w_gu + b_gu).astype(f32)) / GLA_TAU
    log_a = log_a.reshape(bn, n, CHUNK, GLA_HEADS, GLA_DK)
    b = jnp.cumsum(log_a, axis=2)
    b_last = b[:, :, -1]
    q_t = qc * jnp.exp(b)
    k_t = kc * jnp.exp(-b)
    k_s = kc * jnp.exp(b_last[:, :, None] - b)
    causal = jnp.tril(jnp.ones((CHUNK, CHUNK), dtype=bool))
    att = jnp.einsum('bnihd,bnjhd->bnhij', q_t, k_t)
    att = jnp.where(causal, att, 0.0)
    o_intra = jnp.einsum('bnhij,bnjhe->bnihe', att, vc)

    def step(state, xs):
        q_i, k_i, v_i, dec = xs
        o_i = jnp.einsum('bihd,bhde->bihe', q_i, state)
        new_state = dec[..., None] * state + jnp.einsum('bjhd,bjhe->bhde', k_i, v_i)
        return new_state, o_i

    s0 = jnp.zeros((bn, GLA_HEADS, GLA_DK, GLA_DV), f32)
    xs = (jnp.moveaxis(q_t, 1, 0), jnp.moveaxis(k_s, 1, 0), jnp.moveaxis(vc, 1, 0), jnp.moveaxis(jnp.exp(b_last), 1, 0))
    _, o_inter = lax.scan(step, s0, xs)
    o = (o_intra + jnp.moveaxis(o_inter, 0, 1)).reshape(bn, s, GLA_HEADS, GLA_DV)
    o = _rmsnorm(o, o_g).reshape(bn, s, GLA_HEADS * GLA_DV).astype(z.dtype)
    return o * jax.nn.silu(z)

def first_inputs(seed: int = 0) -> dict:
    key = jax.random.key(seed)
    ks = jax.random.split(key, 24)
    f32 = jnp.float32
    nrm = lambda k, shp, sc: jax.random.normal(k, shp, f32) * sc
    gain = lambda k, shp: 1.0 + 0.02 * jax.random.normal(k, shp, f32)
    x = jax.random.normal(ks[0], (BATCH, SEQ, D_MODEL), f32)
    offset = jax.random.randint(ks[1], (BATCH, 1), 0, 4096, dtype=jnp.int32)
    positions = offset + jnp.arange(SEQ, dtype=jnp.int32)[None, :]
    return {
        'x': x,
        'positions': positions,
        'norm_g': gain(ks[2], (DEPTH, D_MODEL)),
        'w_in': nrm(ks[3], (DEPTH, D_MODEL, IN_COLS), D_MODEL ** -0.5),
        'b_gate': nrm(ks[4], (DEPTH, N_BRANCH * D_MODEL), 0.1),
        'sg_ln_g': gain(ks[5], (DEPTH, BRANCH_W)),
        'sg_ln_b': nrm(ks[6], (DEPTH, BRANCH_W), 0.02),
        'sg_w': nrm(ks[7], (DEPTH, SG_GROUPS, SG_BLOCK, SG_BLOCK), SG_BLOCK ** -0.5),
        'sg_b': gain(ks[8], (DEPTH, SG_GROUPS, SG_BLOCK)),
        'mla_cq_g': gain(ks[9], (DEPTH, MLA_Q_RANK)),
        'mla_ckv_g': gain(ks[10], (DEPTH, MLA_KV_RANK)),
        'mla_w_uq': nrm(ks[11], (DEPTH, MLA_Q_RANK, MLA_HEADS * MLA_QK), MLA_Q_RANK ** -0.5),
        'mla_w_ukv': nrm(ks[12], (DEPTH, MLA_KV_RANK, MLA_HEADS * (MLA_NOPE + MLA_V)), MLA_KV_RANK ** -0.5),
        'mla_q_g': gain(ks[13], (DEPTH, MLA_QK)),
        'mla_k_g': gain(ks[14], (DEPTH, MLA_QK)),
        'gla_w_gate': nrm(ks[15], (DEPTH, GLA_GATE_RANK, GLA_HEADS * GLA_DK), GLA_GATE_RANK ** -0.5),
        'gla_b_gate': nrm(ks[16], (DEPTH, GLA_HEADS * GLA_DK), 0.1),
        'gla_o_g': gain(ks[17], (DEPTH, GLA_DV)),
        'w_branch': nrm(ks[18], (DEPTH, N_BRANCH, BRANCH_W, D_MODEL), BRANCH_W ** -0.5),
        'w_out': nrm(ks[19], (DEPTH, D_MODEL, D_MODEL), D_MODEL ** -0.5),
    }

def first_block(x, positions, norm_g, w_in, b_gate, sg_ln_g, sg_ln_b, sg_w, sg_b, mla_cq_g, mla_ckv_g,
              mla_w_uq, mla_w_ukv, mla_q_g, mla_k_g, gla_w_gate, gla_b_gate, gla_o_g, w_branch, w_out):
    bn, s, d = x.shape
    cos, sin = _rope_tables(positions)
    for l in range(DEPTH):
        h = _rmsnorm(x, norm_g[l])
        (u_a, v_a, z_a, c_q, c_kv, k_r, z_b, q_c, k_c, v_c, g_c, z_c, gate_logits) = _split_cols(h @ w_in[l])
        y_a = _spatial_gating(u_a, v_a, z_a, sg_ln_g[l], sg_ln_b[l], sg_w[l], sg_b[l])
        y_b = _mla(c_q, c_kv, k_r, z_b, mla_cq_g[l], mla_ckv_g[l], mla_w_uq[l], mla_w_ukv[l],
                   mla_q_g[l], mla_k_g[l], cos, sin)
        y_c = _gla(q_c, k_c, v_c, g_c, z_c, gla_w_gate[l], gla_b_gate[l], gla_o_g[l])
        gates = jax.nn.sigmoid(gate_logits + b_gate[l]).reshape(bn, s, N_BRANCH, d)
        merged = (gates[:, :, 0] * (y_a @ w_branch[l, 0])
                  + gates[:, :, 1] * (y_b @ w_branch[l, 1])
                  + gates[:, :, 2] * (y_c @ w_branch[l, 2]))
        x = x + merged @ w_out[l]
    return x


DEPTH_2 = 1

HEAD_DIM = 64
GRID_W = 64
N_MEM = 256
NA_HEADS = 6
NA_WIN_ROWS = 8
NA_WIN_COLS = 16
ML_HEADS = 4
ML_CHUNK = 64
GDN_HEADS = 6
GDN_CHUNK = 64
CONV_K = 5
N_DIR = 2
XA_HEADS = 4
XA_HEAD_DIM = D_MODEL // XA_HEADS
D_FF = 4 * D_MODEL
NA_WIDTH = NA_HEADS * HEAD_DIM
ML_WIDTH = ML_HEADS * HEAD_DIM
GDN_WIDTH = GDN_HEADS * HEAD_DIM
D_MIX = NA_WIDTH + ML_WIDTH + GDN_WIDTH
IN_SIZES = (NA_WIDTH, NA_WIDTH, NA_WIDTH,
            ML_WIDTH, ML_WIDTH, ML_WIDTH, ML_WIDTH, N_DIR * ML_HEADS, N_DIR * ML_HEADS,
            GDN_WIDTH, GDN_WIDTH, GDN_WIDTH, GDN_WIDTH, N_DIR * GDN_HEADS, N_DIR * GDN_HEADS)
IN_OFFSETS = tuple(int(o) for o in np.cumsum(IN_SIZES)[:-1])
P_IN = int(sum(IN_SIZES))


def rmsnorm(x, w):
    xf = x.astype(jnp.float32)
    y = xf * lax.rsqrt(jnp.mean(xf * xf, axis=-1, keepdims=True) + EPS)
    return (y * w.astype(jnp.float32)).astype(x.dtype)

def head_rms(t):
    return t * lax.rsqrt(jnp.mean(t * t, axis=-1, keepdims=True) + EPS)

def l2norm(t):
    return t * lax.rsqrt(jnp.sum(t * t, axis=-1, keepdims=True) + EPS)

def neighbourhood_attention(q, k, v, rel_bias):
    b, s, h, dh = q.shape
    rows = s // GRID_W
    wr = min(NA_WIN_ROWS, rows)
    wc = NA_WIN_COLS
    qg = (q * dh ** -0.5).reshape(b, rows, GRID_W, h, dh)
    kg = k.reshape(b, rows, GRID_W, h, dh)
    vg = v.reshape(b, rows, GRID_W, h, dh)
    cols = jnp.arange(GRID_W)
    col_idx = jnp.clip(cols - wc // 2, 0, GRID_W - wc)[:, None] + jnp.arange(wc)[None, :]
    dc = col_idx - cols[:, None] + (NA_WIN_COLS - 1)

    def row_block(args):
        q_r, r = args
        r0 = jnp.clip(r - wr // 2, 0, rows - wr)
        k_win = lax.dynamic_slice_in_dim(kg, r0, wr, axis=1)[:, :, col_idx]
        v_win = lax.dynamic_slice_in_dim(vg, r0, wr, axis=1)[:, :, col_idx]
        dr = r0 + jnp.arange(wr) - r + (NA_WIN_ROWS - 1)
        bias = rel_bias[:, dr[None, :, None], dc[:, None, :]]
        logits = jnp.einsum('bqhd,brqchd->bhqrc', q_r, k_win).astype(jnp.float32) + bias.astype(jnp.float32)
        p = jax.nn.softmax(logits.reshape(b, h, GRID_W, wr * wc), axis=-1).reshape(logits.shape)
        return jnp.einsum('bhqrc,brqchd->bqhd', p.astype(v.dtype), v_win)

    out = lax.map(row_block, (jnp.moveaxis(qg, 1, 0), jnp.arange(rows)))
    return jnp.moveaxis(out, 0, 1).reshape(b, s, h * dh)

def mlstm_direction(q, k, v, ig, f_pre):
    b, h, s, d = q.shape
    L = ML_CHUNK
    nc = s // L
    q = q.reshape(b, h, nc, L, d)
    k = k.reshape(b, h, nc, L, d) * d ** -0.5
    v = v.reshape(b, h, nc, L, d)
    ig = ig.reshape(b, h, nc, L)
    bcum = jnp.cumsum(jax.nn.log_sigmoid(f_pre).reshape(b, h, nc, L), axis=-1)
    b_last = bcum[..., -1]
    w = b_last[..., None] - bcum + ig
    m_loc = jnp.max(w, axis=-1)
    wexp = jnp.exp(w - m_loc[..., None])
    c_loc = jnp.einsum('bhnl,bhnld,bhnle->nbhde', wexp, k, v)
    n_loc = jnp.einsum('bhnl,bhnld->nbhd', wexp, k)

    def step(carry, xs):
        c, n, m = carry
        c_l, n_l, m_l, bl = xs
        m_new = jnp.maximum(bl + m, m_l)
        a = jnp.exp(bl + m - m_new)
        g = jnp.exp(m_l - m_new)
        c_new = a[..., None, None] * c + g[..., None, None] * c_l
        n_new = a[..., None] * n + g[..., None] * n_l
        return (c_new, n_new, m_new), (c, n, m)

    init = (jnp.zeros((b, h, d, d), jnp.float32), jnp.zeros((b, h, d), jnp.float32), jnp.zeros((b, h), jnp.float32))
    _, (c_prev, n_prev, m_prev) = lax.scan(
        step, init, (c_loc, n_loc, jnp.moveaxis(m_loc, -1, 0), jnp.moveaxis(b_last, -1, 0)))
    c_prev = jnp.moveaxis(c_prev, 0, 2)
    n_prev = jnp.moveaxis(n_prev, 0, 2)
    m_prev = jnp.moveaxis(m_prev, 0, -1)
    causal = jnp.tril(jnp.ones((L, L), dtype=bool))
    dmat = jnp.where(causal, bcum[..., :, None] - bcum[..., None, :] + ig[..., None, :], -jnp.inf)
    inter = bcum + m_prev[..., None]
    m_t = jnp.maximum(jnp.max(dmat, axis=-1), inter)
    s_intra = jnp.einsum('bhnld,bhnsd->bhnls', q, k) * jnp.exp(dmat - m_t[..., None])
    a_inter = jnp.exp(inter - m_t)
    num = a_inter[..., None] * jnp.einsum('bhnld,bhnde->bhnle', q, c_prev) + jnp.einsum('bhnls,bhnse->bhnle', s_intra, v)
    den = a_inter * jnp.einsum('bhnld,bhnd->bhnl', q, n_prev) + jnp.sum(s_intra, axis=-1)
    out = num / jnp.maximum(jnp.abs(den), jnp.exp(-m_t))[..., None]
    return out.reshape(b, h, s, d)

def mlstm_mixer(q, k, v, o_pre, i_pre, f_pre, i_bias, f_bias, norm_w):
    b, s, _ = q.shape

    def heads(t):
        return t.reshape(b, s, ML_HEADS, HEAD_DIM).transpose(0, 2, 1, 3).astype(jnp.float32)

    qh, kh, vh = heads(q), heads(k), heads(v)
    ig = (i_pre.reshape(b, s, N_DIR, ML_HEADS).astype(jnp.float32) + i_bias.astype(jnp.float32)).transpose(2, 0, 3, 1)
    fg = (f_pre.reshape(b, s, N_DIR, ML_HEADS).astype(jnp.float32) + f_bias.astype(jnp.float32)).transpose(2, 0, 3, 1)
    h_fwd = mlstm_direction(qh, kh, vh, ig[0], fg[0])
    h_bwd = jnp.flip(mlstm_direction(jnp.flip(qh, 2), jnp.flip(kh, 2), jnp.flip(vh, 2),
                                     jnp.flip(ig[1], 2), jnp.flip(fg[1], 2)), 2)
    hs = head_rms((h_fwd + h_bwd).transpose(0, 2, 1, 3)).reshape(b, s, ML_WIDTH)
    out = hs * norm_w.astype(jnp.float32) * jax.nn.sigmoid(o_pre.astype(jnp.float32))
    return out.astype(q.dtype)

def centred_depthwise_conv(x, w):
    c = x.shape[-1]
    return lax.conv_general_dilated(
        x, w[:, None, :].astype(x.dtype), window_strides=(1,),
        padding=[(CONV_K // 2, CONV_K // 2)],
        dimension_numbers=('NWC', 'WIO', 'NWC'), feature_group_count=c)

def gdn_direction(q, k, v, g, beta):
    b, h, s, dk = q.shape
    dv = v.shape[-1]
    L = GDN_CHUNK
    nc = s // L
    q = (q * dk ** -0.5).reshape(b, h, nc, L, dk)
    k = k.reshape(b, h, nc, L, dk)
    v = v.reshape(b, h, nc, L, dv)
    beta = beta.reshape(b, h, nc, L)
    gc = jnp.cumsum(g.reshape(b, h, nc, L), axis=-1)
    incl = jnp.tril(jnp.ones((L, L), dtype=bool))
    strict = jnp.tril(jnp.ones((L, L), dtype=bool), -1)
    diff = gc[..., :, None] - gc[..., None, :]
    lmask = jnp.where(incl, jnp.exp(jnp.where(incl, diff, 0.0)), 0.0)
    kb = k * beta[..., None]
    a = jnp.where(strict, jnp.einsum('bhnld,bhnsd->bhnls', kb, k) * lmask, 0.0)
    eye = jnp.eye(L, dtype=jnp.float32)
    t = lax.linalg.triangular_solve(a + eye, jnp.broadcast_to(eye, a.shape),
                                    left_side=True, lower=True, unit_diagonal=True)
    u = jnp.einsum('bhnls,bhnse->bhnle', t, v * beta[..., None])
    wk = jnp.einsum('bhnls,bhnsd->bhnld', t, kb * jnp.exp(gc)[..., None])
    attn = jnp.where(incl, jnp.einsum('bhnld,bhnsd->bhnls', q, k) * lmask, 0.0)
    q_dec = q * jnp.exp(gc)[..., None]
    g_last = gc[..., -1]
    k_state = k * jnp.exp(g_last[..., None] - gc)[..., None]

    def step(state, xs):
        u_c, w_c, a_c, qd_c, ks_c, gl_c = xs
        v_new = u_c - jnp.einsum('bhld,bhde->bhle', w_c, state)
        o = jnp.einsum('bhld,bhde->bhle', qd_c, state) + jnp.einsum('bhls,bhse->bhle', a_c, v_new)
        state = state * jnp.exp(gl_c)[..., None, None] + jnp.einsum('bhld,bhle->bhde', ks_c, v_new)
        return state, o

    xs = tuple(jnp.moveaxis(t_, 2, 0) for t_ in (u, wk, attn, q_dec, k_state, g_last))
    _, o = lax.scan(step, jnp.zeros((b, h, dk, dv), jnp.float32), xs)
    return jnp.moveaxis(o, 0, 2).reshape(b, h, s, dv)

def gated_deltanet_mixer(q, k, v, z, beta_pre, alpha_pre, conv_w, a_log, dt_bias, norm_w):
    b, s, _ = q.shape
    qkv = jax.nn.silu(centred_depthwise_conv(jnp.concatenate([q, k, v], axis=-1), conv_w))
    qc, kc, vc = jnp.split(qkv, 3, axis=-1)

    def heads(t):
        return t.reshape(b, s, GDN_HEADS, HEAD_DIM).transpose(0, 2, 1, 3).astype(jnp.float32)

    qh, kh, vh = l2norm(heads(qc)), l2norm(heads(kc)), heads(vc)
    beta = jax.nn.sigmoid(beta_pre.reshape(b, s, N_DIR, GDN_HEADS).astype(jnp.float32)).transpose(2, 0, 3, 1)
    g = (-jnp.exp(a_log.astype(jnp.float32)) * jax.nn.softplus(
        alpha_pre.reshape(b, s, N_DIR, GDN_HEADS).astype(jnp.float32) + dt_bias.astype(jnp.float32))).transpose(2, 0, 3, 1)
    o_fwd = gdn_direction(qh, kh, vh, g[0], beta[0])
    o_bwd = jnp.flip(gdn_direction(jnp.flip(qh, 2), jnp.flip(kh, 2), jnp.flip(vh, 2),
                                   jnp.flip(g[1], 2), jnp.flip(beta[1], 2)), 2)
    o = head_rms((o_fwd + o_bwd).transpose(0, 2, 1, 3)).reshape(b, s, GDN_WIDTH)
    o = o * norm_w.astype(jnp.float32) * jax.nn.silu(z.astype(jnp.float32))
    return o.astype(z.dtype)

def memory_cross_attention(h, mem_n, w_q, w_kv, w_o):
    b, s, _ = h.shape
    m = mem_n.shape[1]
    q = (h @ w_q).reshape(b, s, XA_HEADS, XA_HEAD_DIM)
    kk, vv = jnp.split(mem_n @ w_kv, 2, axis=-1)
    kk = kk.reshape(b, m, XA_HEADS, XA_HEAD_DIM)
    vv = vv.reshape(b, m, XA_HEADS, XA_HEAD_DIM)
    logits = jnp.einsum('bshd,bmhd->bhsm', q, kk).astype(jnp.float32) * XA_HEAD_DIM ** -0.5
    p = jax.nn.softmax(logits, axis=-1)
    o = jnp.einsum('bhsm,bmhd->bshd', p.astype(vv.dtype), vv).reshape(b, s, XA_HEADS * XA_HEAD_DIM)
    return o @ w_o

def second_inputs(seed: int = 0) -> dict:
    key = jax.random.key(seed)
    ks = jax.random.split(key, 24)
    f32 = jnp.float32

    def nrm(k, shape, scale):
        return jax.random.normal(k, shape, f32) * scale

    def gain(k, shape):
        return 1.0 + 0.02 * jax.random.normal(k, shape, f32)

    dt = jnp.exp(jax.random.uniform(ks[12], (DEPTH_2, N_DIR, GDN_HEADS), f32, math.log(1e-3), math.log(1e-1)))
    return {
        'x': nrm(ks[0], (BATCH, SEQ, D_MODEL), 1.0),
        'mem': nrm(ks[1], (BATCH, N_MEM, D_MODEL), 1.0),
        'norm_mix_w': gain(ks[2], (DEPTH_2, D_MODEL)),
        'w_in': nrm(ks[3], (DEPTH_2, D_MODEL, P_IN), D_MODEL ** -0.5),
        'na_rel_bias': nrm(ks[4], (DEPTH_2, NA_HEADS, 2 * NA_WIN_ROWS - 1, 2 * NA_WIN_COLS - 1), 0.02),
        'ml_i_bias': nrm(ks[5], (DEPTH_2, N_DIR, ML_HEADS), 0.1),
        'ml_f_bias': 3.0 + 3.0 * jax.random.uniform(ks[6], (DEPTH_2, N_DIR, ML_HEADS), f32),
        'ml_norm_w': gain(ks[7], (DEPTH_2, ML_WIDTH)),
        'gdn_conv_w': nrm(ks[8], (DEPTH_2, CONV_K, 3 * GDN_WIDTH), CONV_K ** -0.5),
        'gdn_a_log': jnp.log(jax.random.uniform(ks[9], (DEPTH_2, N_DIR, GDN_HEADS), f32, 1.0, 16.0)),
        'gdn_dt_bias': dt + jnp.log(-jnp.expm1(-dt)),
        'gdn_norm_w': gain(ks[10], (DEPTH_2, GDN_WIDTH)),
        'w_out': nrm(ks[11], (DEPTH_2, D_MIX, D_MODEL), D_MIX ** -0.5),
        'norm_xa_w': gain(ks[13], (DEPTH_2, D_MODEL)),
        'norm_mem_w': gain(ks[14], (DEPTH_2, D_MODEL)),
        'w_xq': nrm(ks[15], (DEPTH_2, D_MODEL, XA_HEADS * XA_HEAD_DIM), D_MODEL ** -0.5),
        'w_xkv': nrm(ks[16], (DEPTH_2, D_MODEL, 2 * XA_HEADS * XA_HEAD_DIM), D_MODEL ** -0.5),
        'w_xo': nrm(ks[17], (DEPTH_2, XA_HEADS * XA_HEAD_DIM, D_MODEL), (XA_HEADS * XA_HEAD_DIM) ** -0.5),
        'norm_ffn_w': gain(ks[18], (DEPTH_2, D_MODEL)),
        'w_ff1': nrm(ks[19], (DEPTH_2, D_MODEL, D_FF), D_MODEL ** -0.5),
        'w_ff2': nrm(ks[20], (DEPTH_2, D_FF, D_MODEL), D_FF ** -0.5),
        'norm_out_w': gain(ks[21], (D_MODEL,)),
    }

def second_block(x, mem, norm_mix_w, w_in, na_rel_bias, ml_i_bias, ml_f_bias, ml_norm_w,
              gdn_conv_w, gdn_a_log, gdn_dt_bias, gdn_norm_w, w_out, norm_xa_w, norm_mem_w,
              w_xq, w_xkv, w_xo, norm_ffn_w, w_ff1, w_ff2, norm_out_w):
    b, s, _ = x.shape
    for l in range(DEPTH_2):
        h = rmsnorm(x, norm_mix_w[l])
        (na_q, na_k, na_v, ml_q, ml_k, ml_v, ml_o, ml_i, ml_f,
         gd_q, gd_k, gd_v, gd_z, gd_b, gd_a) = jnp.split(h @ w_in[l], IN_OFFSETS, axis=-1)
        y_na = neighbourhood_attention(na_q.reshape(b, s, NA_HEADS, HEAD_DIM),
                                       na_k.reshape(b, s, NA_HEADS, HEAD_DIM),
                                       na_v.reshape(b, s, NA_HEADS, HEAD_DIM), na_rel_bias[l])
        y_ml = mlstm_mixer(ml_q, ml_k, ml_v, ml_o, ml_i, ml_f, ml_i_bias[l], ml_f_bias[l], ml_norm_w[l])
        y_gd = gated_deltanet_mixer(gd_q, gd_k, gd_v, gd_z, gd_b, gd_a, gdn_conv_w[l],
                                    gdn_a_log[l], gdn_dt_bias[l], gdn_norm_w[l])
        x = x + jnp.concatenate([y_na, y_ml, y_gd], axis=-1) @ w_out[l]
        x = x + memory_cross_attention(rmsnorm(x, norm_xa_w[l]), rmsnorm(mem, norm_mem_w[l]),
                                       w_xq[l], w_xkv[l], w_xo[l])
        h = rmsnorm(x, norm_ffn_w[l])
        x = x + jnp.square(jax.nn.relu(h @ w_ff1[l])) @ w_ff2[l]
    return rmsnorm(x, norm_out_w)


def setup_inputs(seed=0):
    out = dict(first_inputs(seed))
    for name, value in second_inputs(seed + 1).items():
        if name != "x":
            out[name + "_2"] = value
    return out


def reference(
    x, positions, norm_g, w_in, b_gate, sg_ln_g, sg_ln_b, sg_w, sg_b, mla_cq_g, mla_ckv_g,
    mla_w_uq, mla_w_ukv, mla_q_g, mla_k_g, gla_w_gate, gla_b_gate, gla_o_g, w_branch, w_out,
    mem_2, norm_mix_w_2, w_in_2, na_rel_bias_2, ml_i_bias_2, ml_f_bias_2, ml_norm_w_2,
    gdn_conv_w_2, gdn_a_log_2, gdn_dt_bias_2, gdn_norm_w_2, w_out_2, norm_xa_w_2, norm_mem_w_2,
    w_xq_2, w_xkv_2, w_xo_2, norm_ffn_w_2, w_ff1_2, w_ff2_2, norm_out_w_2,
):
    x = first_block(
        x, positions, norm_g, w_in, b_gate, sg_ln_g, sg_ln_b, sg_w, sg_b, mla_cq_g, mla_ckv_g,
        mla_w_uq, mla_w_ukv, mla_q_g, mla_k_g, gla_w_gate, gla_b_gate, gla_o_g, w_branch, w_out,
    )
    return second_block(
        x, mem_2, norm_mix_w_2, w_in_2, na_rel_bias_2, ml_i_bias_2, ml_f_bias_2, ml_norm_w_2,
        gdn_conv_w_2, gdn_a_log_2, gdn_dt_bias_2, gdn_norm_w_2, w_out_2, norm_xa_w_2,
        norm_mem_w_2, w_xq_2, w_xkv_2, w_xo_2, norm_ffn_w_2, w_ff1_2, w_ff2_2, norm_out_w_2,
    )


_drawn_inputs = setup_inputs


def setup_inputs(seed=0):
    import zlib

    import numpy as np

    out = dict(_drawn_inputs(seed))
    spreads = {}
    factors = {'sg_ln_g': 8.0,
     'sg_ln_b': 8.0,
     'sg_b': 7.864,
     'mla_cq_g': 8.0,
     'mla_ckv_g': 8.0,
     'mla_q_g': 8.0,
     'mla_k_g': 8.0,
     'gla_o_g': 5.069,
     'norm_mix_w_2': 3.162,
     'na_rel_bias_2': 8.0,
     'ml_i_bias_2': 64.0,
     'ml_norm_w_2': 28.445,
     'gdn_norm_w_2': 8.0,
     'norm_xa_w_2': 8.0,
     'norm_mem_w_2': 8.0,
     'norm_ffn_w_2': 11.812,
     'norm_out_w_2': 8.13}
    for name, (base, spread) in spreads.items():
        noise = np.random.default_rng([zlib.crc32(name.encode()), seed]).standard_normal(out[name].shape)
        drawn = base * np.exp(spread * noise) if base else spread * noise
        out[name] = jnp.asarray(drawn.astype(out[name].dtype))
    for name, factor in factors.items():
        out[name] = (out[name] * factor).astype(out[name].dtype)
    return out
```

```python
from contextlib import ExitStack

import numpy as np
import concourse.bass as bass
from concourse import mybir
from concourse.alu_op_type import AluOpType as ALU

F32 = mybir.dt.float32
I32 = mybir.dt.int32
I8 = mybir.dt.int8
ACT = mybir.ActivationFunctionType
X = mybir.AxisListType.X

P = 128
S = 256
T = S // P
D = 1024
KD = D // P
BANK = 512
EPS = 1e-6
NEG = -1e30
DEPTH = 2
CH = 64

COL_U, COL_V, COL_Z = 0, 512, 1024
COL_CQ, COL_CKV, COL_KR, COL_ZB = 1536, 1792, 1920, 1952
COL_QC, COL_KC, COL_VC, COL_GC, COL_ZC, COL_GATE = 2464, 2720, 2976, 3488, 3504, 4016
MH, MQK, NOPE, ROPE = 8, 96, 64, 32
HALF = ROPE // 2
THETA = 10000.0
GH, GDK, GDV, GRANK, GTAU = 4, 64, 128, 16, 16.0
GELU_C = float(np.sqrt(2.0 / np.pi))
SLOTS1 = [(COL_CQ, 416, 1), (COL_ZB, 512, 1), (COL_U, 512, 1), (COL_V, 512, 1), (COL_Z, 512, 1),
          (COL_QC, 512, 1), (COL_GC, 528, 2), (COL_VC, 512, 1)]
NGATE = 6
BRANCHES = (1, 0, 2)
SC = [(0, 0, 8), (1, 0, 4), (1, 4, 4)]
TWO_PI = 2.0 * np.pi
PI_A = 6.28125
PI_B = float(np.float32(np.round((TWO_PI - PI_A) * 2.0 ** 22) / 2.0 ** 22))
PI_C = float(np.float32(TWO_PI - PI_A - PI_B))
ROUND = float(1.5 * 2 ** 23)

NH, HD, GW = 6, 64, 64
MLH = 4
GNH = 6
TAPS = 5
C_MLQ, C_MLK, C_MLV, C_MLO, C_MLI, C_MLF = 1152, 1408, 1664, 1920, 2176, 2184
C_GDQ, C_GDZ = 2192, 3344
SHIFT = C_GDZ - C_GDQ
K_GDZ, K_GDB, K_GDA = C_GDQ, C_GDQ + 384, C_GDQ + 396
SLOTS2 = [(C_GDQ, 512), (C_GDQ + 512, 512), (C_GDQ + 1024, 128)]
SLOTS2T = [(2048, 144, 2048), (C_GDZ, 408, K_GDZ), (0, 512, 0), (512, 512, 512), (1024, 512, 1024), (1536, 512, 1536)]
XH, XD = 4, 256
FF = 4096
SLOT_W = KD * 528
RING = 3

R_NORM, R_MIX, R_XA, R_MEM, R_FFN, R_CQ, R_CKV, R_SGB, R_CONV, R_END = 0, 16, 24, 32, 40, 48, 52, 54, 62, 107


def bc(ap, pos, n):
    dims = [list(d) for d in ap.ap]
    dims.insert(pos, [0, n])
    return bass.AP(tensor=ap.tensor, offset=ap.offset, ap=dims)


def build(nc, A, out):
    ctx = ExitStack()
    with ctx:
        def sb(name, shape, dt=F32):
            return ctx.enter_context(nc.sbuf_tensor(name, shape, dt))

        sems = {}
        made = {}

        def ev(name):
            if name not in sems:
                sems[name] = ctx.enter_context(nc.semaphore(name))
            return sems[name]

        def done(eng, ins, name):
            if isinstance(name, tuple):
                sem, value = name
            else:
                made[name] = made.get(name, 0) + 1
                sem, value = ev(name), made[name]
            ins.then_inc(sem, 1)
            eng.wait_ge(sem, value)

        x = sb("x", [P, T, D])
        xn = sb("xn", [P, T * D])
        hT = sb("hT", [P, KD, S])
        ring = sb("ring", [P, RING, SLOT_W])
        proj_all = sb("proj", [P, T * COL_GATE])
        arena = sb("arena", [P, 23488])
        tiny = sb("tiny", [P, 544])
        ident = sb("ident", [P, P])
        blk = sb("blk", [P, P])
        causal = sb("causal", [P, 2, P])
        ones = sb("ones", [P, P])
        sel = sb("sel", [6, 6, P])
        cols = sb("cols", [P, R_END])
        rin = sb("rin", [P, 32])
        rout = sb("rout", [P, 32])
        mhalf = sb("mhalf", [P, 32])
        ssq = sb("ssq", [P, 32])
        posi = sb("posi", [P, T], I32)
        posf = sb("posf", [P, T])
        freq = sb("freq", [P, HALF])
        trig = sb("trig", [P, 2, T, HALF])
        stat_all = sb("stat_all", [P, 24])
        smax = sb("smax", [P, 16])
        ssum = sb("ssum", [P, 16])
        stat = sb("stat", [P, T, 8])
        gdec = sb("gdec", [P, 4])
        level = sb("level", [P, 2, 6, P], I8)
        psum = ctx.enter_context(nc.psum_tensor("psum", [P, 8, BANK], F32))

        def at(where, off, *shape):
            n = int(np.prod(shape))
            ap = where[:, off:off + n]
            if len(shape) == 1:
                return ap
            names = "abcde"[:len(shape)]
            return ap.rearrange("p (%s) -> p %s" % (" ".join(names), " ".join(names)),
                                **dict(zip(names[1:], shape[1:])))

        proj = at(proj_all, 0, T, COL_GATE)
        gate = at(arena, 0, T, 3 * D)
        RA, RB, RC, PB = 6144, 9216, 13312, 17408
        qk = at(arena, RA, T, 2 * MH, MQK)
        sc = at(arena, RA, 3, 1024)
        qkT = at(arena, RB, 2 * MH, S)
        pT = at(arena, RB, 3, MH, P)
        tmp = at(arena, RC, 3072)
        mv = at(arena, RC + 3072, T, MH * NOPE)
        yT = at(arena, RB, 3, 4, S)
        sgw = at(arena, PB, 4, P)
        sgwT = at(arena, PB + 512, 4, P)
        ln_g = at(arena, PB + 1024, 512)
        ln_b = at(arena, PB + 1536, 512)
        wuq = at(arena, PB + 2048, 2, MH * MQK)
        wukv = at(arena, PB + 3584, 1024)
        qk_g = at(arena, PB + 4608, 2, MQK)
        o_g = at(arena, PB + 4800, GDV)
        wgu = at(arena, PB + 4928, 256)
        bgu = at(arena, PB + 5184, 256)
        bgate = at(arena, PB + 5440, 512)
        rows = at(arena, PB + 5952, P)
        N_LAYER_DMA = 11
        N_ROWS_DMA = 9
        N_SECOND_DMA = 30
        merged = at(arena, RA, T, D)
        ang, ang1, ang2 = at(arena, 0, T, HALF), at(arena, 0, T * HALF), at(arena, 64, T * HALF)
        cn = at(xn, 0, T, 384)
        cT = at(xn, 768, 3, S)
        glrT = at(xn, 0, S)
        gl_la = at(xn, 1024, T, 256)
        gl_b = at(xn, 1536, T, 256)
        gl_qk = at(arena, RA, T, 512)
        gl_ks = at(arena, RA + 1024, T, 256)
        gl_e = at(arena, RA + 1536, T, 256)
        gl_st = at(arena, RA + 2048, 3, 2, P)
        gl_e2 = at(xn, 512, T, 256)
        gl_qkT = at(arena, RB, 4, S)
        gl_att = at(arena, RB + 1024, T, 4, P)
        gl_o = at(arena, RC, T, 512)
        gl_sq = at(arena, RC + 1024, T, 512)

        proj2 = at(proj_all, 0, T, 2600)
        gd = at(proj_all, 5200, T, 1152)
        gd_th = at(proj_all, 5200, 9, S)
        nstrict = at(proj_all, 7504, 2, P)
        first = at(proj_all, 7760, 2, 64)
        mirror = at(proj_all, 7888, P)
        conv = at(arena, 20352, 9, S)
        PC = 22656
        ml_w, gd_w = at(arena, PC, 256), at(arena, PC + 256, 384)
        if_b, dt_b, a_log = at(arena, PC + 640, 16), at(arena, PC + 656, 12), at(arena, PC + 668, 12)
        na_s = at(arena, 0, T, 2, 3, S)
        na_pT = at(arena, 3072, 24, P)
        na_T = at(arena, 6144, 6, S)
        na_raw = at(arena, 7680, T, NH, S)
        ml_row = at(arena, 7680, 2, 2, S)
        ml_max = at(arena, 8704, 3, 2, S)
        ml_T = at(arena, 10752, 4, S)
        ml_v = at(arena, 11776, T, MLH, HD + 1)
        ml_k = at(arena, 12296, T, 2, MLH, HD)
        ml_p = at(arena, 13320, T, 2, MLH, P)
        zt = at(arena, 15368, T, 384)
        ot = at(arena, 16136, T, 256)
        ml_c = at(arena, 16648, 2, 4, 2, HD + 1)
        ml_n = at(arena, 17688, T, 2, MLH, HD + 1)
        gd_kb = at(arena, 0, T, 2, GNH, HD)
        gd_kbe = at(arena, 1536, T, 2, GNH, HD)
        gd_ks = at(arena, 3072, T, 2, GNH, HD)
        gd_vb = at(arena, 4608, T, 2, GNH, HD)
        gd_T = at(arena, 6144, 6, S)
        gd_kbT = at(arena, 7680, T, 2, 3, P)
        gd_x = at(arena, 7680, 4, 3, P)
        gd_a = at(arena, 9216, T, 2, GNH, P)
        gd_att = at(arena, 12288, T, 2, GNH, P)
        gd_inv = [at(arena, 19584, T, 2, GNH, P), at(arena, 16512, T, 2, GNH, P)]
        gd_u = at(arena, 0, T, 2, GNH, HD)
        gd_wk = at(arena, 19584, T, 2, 3, P)
        gd_vn = at(arena, 21120, T, 2, GNH, HD)
        gd_st = at(arena, 9216, 4, 2, 3, HD)
        gd_o = at(arena, 10752, T, 2, GNH, HD)
        y2 = at(xn, 0, T, D)
        na_mask = at(tiny, 0, GW)
        ml_if = at(tiny, 64, T, 16)
        sp = at(tiny, 96, T, 20)
        spl = at(tiny, 136, T, 20)
        cum = at(tiny, 176, 80)
        ml_b, ml_bl = at(tiny, 176, T, 8), at(tiny, 192, T, 8)
        gd_c, gd_cl = at(tiny, 208, T, 12), at(tiny, 232, T, 12)
        ml_g = at(tiny, 256, T, 8)
        ml_m = at(tiny, 272, 2, 5)
        ml_col = at(tiny, 284, 3, T, 8)
        ml_e = at(tiny, 332, 4, T, 8)
        ml_dec = at(tiny, 396, 4, 2, 2)
        beta = at(tiny, 412, T, 12)
        gd_g = at(tiny, 436, T, 12)
        gd_e = at(tiny, 460, 3, T, 12)
        rc_ = at(tiny, 256, 16)
        gd_dec = at(stat_all, 0, 4, 2, 3)
        mem = at(arena, 0, T, D)
        memT = at(arena, 2048, KD, S)
        xk_T = at(arena, 4096, KD, S)
        x_v = at(arena, 6144, T, D)
        xq_T = at(arena, 8192, KD, S)
        x_s = at(arena, 10240, T, XH, S)
        x_pT = at(arena, 12288, T, XH, S)
        x_oT = at(arena, 14336, KD, S)
        out_g = at(arena, 16384, D)
        h1T = at(arena, 0, FF // P, S)

        bank_full = [ev(f"bank_full{b}") for b in range(8)]
        bank_free = [ev(f"bank_free{b}") for b in range(8)]
        uses = [0] * 8
        last = [None] * 8
        where = {}
        turn = [0]

        def open_bank(pe, name, n=1):
            if turn[0] % 8 + n > 8:
                turn[0] += 8 - turn[0] % 8
            b = turn[0] % 8
            turn[0] += n
            for lead, use in sorted({last[c] for c in range(b, b + n) if last[c]}):
                pe.wait_ge(bank_free[lead], use)
            uses[b] += 1
            for c in range(b, b + n):
                last[c] = (b, uses[b])
            assert name not in where, name
            where[name] = (b, uses[b])
            return bank_view(b, n)

        def bank_view(b, n):
            return psum[:, b, :] if n == 1 else psum[:, b:b + n, :].rearrange("p b n -> p (b n)")

        def filled(ins, name):
            ins.then_inc(bank_full[where[name][0]], 1)

        def full(eng, name, n=1):
            b, u = where[name]
            eng.wait_ge(bank_full[b], u)
            return bank_view(b, n)

        def copied(eng, *names):
            for b in sorted({where[n][0] for n in names}):
                eng.wait_ge(bank_free[b], max(where[n][1] for n in names if where[n][0] == b))

        def free(name):
            return bank_free[where[name][0]], where[name][1]

        slots = []
        release = []

        def slot_done(name):
            release.append((bank_full[where[name][0]], where[name][1]))

        def w_cols(w, c0, n):
            slots.append((w[:, c0:c0 + n].rearrange("(k p) n -> p k n", p=P), KD, n))

        def w_rows(w, r0):
            slots.append((w[r0:r0 + 4 * P, :].rearrange("(k p) n -> p k n", p=P), 4, D))

        for l in range(DEPTH):
            for c0, n, _ in SLOTS1:
                w_cols(A["w_in"][l], c0, n)
            for i in range(NGATE):
                w_cols(A["w_in"][l], COL_GATE + BANK * i, BANK)
            for i in BRANCHES:
                w_rows(A["w_branch"][l, i], 0)
            for i in range(2):
                w_rows(A["w_out"][l], 4 * P * i)
        for c0, n in SLOTS2:
            w_cols(A["w_in_2"][0], c0, n)
        for c0, n, _ in SLOTS2T:
            w_cols(A["w_in_2"][0], c0, n)
        for i in range(2):
            w_rows(A["w_out_2"][0], 4 * P * i)
        for i in range(4):
            w_cols(A["w_xkv_2"][0], BANK * i, BANK)
        for i in range(2):
            w_cols(A["w_xq_2"][0], BANK * i, BANK)
        for i in range(2):
            w_rows(A["w_xo_2"][0], 4 * P * i)
        for i in range(8):
            w_cols(A["w_ff1_2"][0], BANK * i, BANK)
        for i in range(8):
            w_rows(A["w_ff2_2"][0], 4 * P * i)


        block = ctx.enter_context(nc.Block())

        @block.tensor
        def _(pe):
            mm = nc.tensor.matmul
            turn_ = nc.tensor.transpose
            used = [0]

            def take_slot():
                k = used[0]
                used[0] += 1
                pe.wait_ge(ev(f"ring_full{k % RING}"), 16 * (k // RING + 1))
                _, kd, n = slots[k]
                return ring[:, k % RING, 0:kd * n].rearrange("p (k n) -> p k n", n=n)

            def norm_T(i):
                for t in range(T):
                    pe.wait_ge(ev("xn_ready"), T * i + t + 1)
                    for h in range(2):
                        b = open_bank(pe, ("xT", i, t, h))
                        for k in range(4):
                            c = t * D + (4 * h + k) * P
                            m = turn_(b[:, k * P:(k + 1) * P], xn[:, c:c + P], ident[:, :])
                        filled(m, ("xT", i, t, h))
                copied(pe, *[("xT", i, t, h) for t in range(T) for h in range(2)])

            def gemm_cols(tag, lhs, parts=1, bias=None):
                w = take_slot()
                n = w.shape[2] // parts
                for t in range(T):
                    for q in range(parts):
                        b = open_bank(pe, (*tag, t, q))
                        for k in range(KD):
                            m = mm(b[:, 0:n], lhs[:, k, t * P:(t + 1) * P], w[:, k, q * n:(q + 1) * n],
                                   start=(k == 0), stop=(k == KD - 1 and bias is None))
                        if bias is not None:
                            m = mm(b[:, 0:n], sel[:, bias, :], bgate[0:6, :], start=False, stop=True)
                        filled(m, (*tag, t, q))
                slot_done((*tag, T - 1, parts - 1))

            def gemm_rows(tag, lhs, parts=2):
                banks = [open_bank(pe, (*tag, t, h)) for t in range(T) for h in range(2)]
                for part in range(parts):
                    w = take_slot()
                    for t in range(T):
                        for h in range(2):
                            for k in range(4):
                                m = mm(banks[2 * t + h], lhs[:, 4 * part + k, t * P:(t + 1) * P], w[:, k, h * BANK:(h + 1) * BANK],
                                       start=(part == 0 and k == 0), stop=(part == parts - 1 and k == 3))
                            if part == parts - 1:
                                filled(m, (*tag, t, h))
                    if part < parts - 1:
                        m.then_inc(ev("rows_used"), 1)
                        made["rows_used"] = made.get("rows_used", 0) + 1
                        release.append((ev("rows_used"), made["rows_used"]))
                slot_done((*tag, 1, 1))

            def gemm_T(tag, rhs, pairs):
                w = take_slot()
                for g in range(pairs):
                    b = open_bank(pe, (*tag, g))
                    for f in range(2):
                        for k in range(KD):
                            c = (2 * g + f) * P
                            m = mm(b[:, f * S:(f + 1) * S], w[:, k, c:c + P], rhs[:, k, :], start=(k == 0), stop=(k == KD - 1))
                    filled(m, (*tag, g))
                slot_done((*tag, pairs - 1))

            def rows_T(tag, src):
                for t in range(T):
                    for h in range(2):
                        b = open_bank(pe, (*tag, t, h))
                        for k in range(4):
                            m = turn_(b[:, k * P:(k + 1) * P], src[:, t, (4 * h + k) * P:(4 * h + k + 1) * P], ident[:, :])
                        filled(m, (*tag, t, h))
                copied(pe, *[(*tag, t, h) for t in range(T) for h in range(2)])

            pe.wait_ge(ev("const_ready"), 1)
            pe.wait_ge(ev("rows_in"), 16 * N_ROWS_DMA)
            b = open_bank(pe, "cols")
            filled(turn_(b[:, 0:R_END], rows[0:R_END, :], ident[0:R_END, 0:R_END]), "cols")

            for l in range(DEPTH):
                def p1(i):
                    gemm_cols(("p1", l, i), hT, parts=SLOTS1[i][2])

                def gates(i):
                    gemm_cols(("gate", l, i), hT, bias=i)

                norm_T(l)
                p1(0)
                p1(1)
                p1(2)
                pe.wait_ge(ev("cn_ready"), l + 1)
                for t in range(T):
                    b = open_bank(pe, ("cT", l, t))
                    for k in range(3):
                        m = turn_(b[:, k * P:(k + 1) * P], cn[:, t, k * P:(k + 1) * P], ident[:, :])
                    filled(m, ("cT", l, t))
                copied(pe, ("cT", l, 0), ("cT", l, 1))
                pe.wait_ge(ev("layer_in"), 16 * N_LAYER_DMA * (l + 1))
                for t in range(T):
                    for h in range(2):
                        b = open_bank(pe, ("uq", l, t, h))
                        for k in range(2):
                            m = mm(b[:, 0:384], cT[:, k, t * P:(t + 1) * P], wuq[:, k, h * 384:(h + 1) * 384],
                                   start=(k == 0), stop=(k == 1))
                        filled(m, ("uq", l, t, h))
                        b = open_bank(pe, ("ukv", l, t, h))
                        filled(mm(b, cT[:, 2, t * P:(t + 1) * P], wukv[:, h * BANK:(h + 1) * BANK], start=True, stop=True),
                               ("ukv", l, t, h))
                p1(3)
                p1(4)
                p1(5)
                pe.wait_ge(ev("qk_ready"), l + 1)
                for t in range(T):
                    for g in range(4):
                        b = open_bank(pe, ("qkT", l, t, g))
                        for k in range(4):
                            m = turn_(b[0:MQK, k * P:(k + 1) * P], qk[:, t, 4 * g + k, :], ident[:, :])
                        filled(m, ("qkT", l, t, g))
                p1(6)
                p1(7)
                copied(pe, *[("qkT", l, t, g) for t in range(T) for g in range(4)])
                for j, (t, h0, hn) in enumerate(SC):
                    n = P * (t + 1)
                    b = open_bank(pe, ("sc", l, j), 2)
                    for h in range(hn):
                        m = mm(b[:, h * n:(h + 1) * n], qkT[0:MQK, h0 + h, t * P:(t + 1) * P], qkT[0:MQK, MH + h0 + h, 0:n],
                               start=True, stop=True)
                    filled(m, ("sc", l, j))
                b = open_bank(pe, ("glrT", l))
                copied(pe, ("p1", l, 6, 0, 0), ("p1", l, 6, 1, 0))
                for t in range(T):
                    m = turn_(b[0:GRANK, t * P:(t + 1) * P], proj[:, t, COL_GC:COL_GC + GRANK], ident[:, :])
                filled(m, ("glrT", l))
                pe.wait_ge(ev("const_ready"), 2)
                gates(0)
                copied(pe, ("glrT", l))
                b = open_bank(pe, ("gg", l))
                for t in range(T):
                    mm(b[:, t * 256:(t + 1) * 256], glrT[0:GRANK, t * P:(t + 1) * P], wgu[0:GRANK, :], start=True, stop=False)
                    m = mm(b[:, t * 256:(t + 1) * 256], ones[0:1, :], bgu[0:1, :], start=False, stop=True)
                filled(m, ("gg", l))
                for j in range(3):
                    pe.wait_ge(ev("p_ready"), 3 * l + j + 1)
                    for q in range(2):
                        b = open_bank(pe, ("pT", l, j, q))
                        for k in range(4):
                            m = turn_(b[:, k * P:(k + 1) * P], sc[:, j, (4 * q + k) * P:(4 * q + k + 1) * P], ident[:, :])
                        filled(m, ("pT", l, j, q))
                gates(1)
                copied(pe, *[("pT", l, j, q) for j in range(3) for q in range(2)])
                for t in range(T):
                    b = open_bank(pe, ("pv", l, t))
                    for h in range(MH):
                        for k in range(t + 1):
                            src = pT[:, 0, h, :] if t == 0 else pT[:, 1 + h // 4, 2 * (h % 4) + k, :]
                            m = mm(b[:, h * NOPE:(h + 1) * NOPE], src, mv[:, k, h * NOPE:(h + 1) * NOPE],
                                   start=(k == 0), stop=(k == t))
                    filled(m, ("pv", l, t))
                pe.wait_ge(ev("la_ready"), l + 1)
                for name, mat in (("gb", causal[:, 0, :]), ("gbl", blk[:, :])):
                    b = open_bank(pe, (name, l))
                    for t in range(T):
                        m = mm(b[:, t * 256:(t + 1) * 256], mat, gl_la[:, t, :], start=True, stop=True)
                    filled(m, (name, l))
                b = open_bank(pe, ("gdec", l), 2)
                for n in range(1, 3):
                    r = CH * (n % 2)
                    for pr in range(2):
                        c = BANK * (n - 1) + pr
                        m = mm(b[:, c:c + 1], gl_la[r:r + CH, n // 2, pr * P:(pr + 1) * P], ones[r:r + CH, 0:1],
                               start=True, stop=True)
                filled(m, ("gdec", l))
                gates(2)
                pe.wait_ge(ev("gqk_ready"), l + 1)
                for t in range(T):
                    b = open_bank(pe, ("gqkT", l, t))
                    for k in range(4):
                        m = turn_(b[:, k * P:(k + 1) * P], gl_qk[:, t, k * P:(k + 1) * P], ident[:, :])
                    filled(m, ("gqkT", l, t))
                copied(pe, ("p1", l, 7, 0, 0), ("p1", l, 7, 1, 0))
                b = open_bank(pe, ("gu", l), 2)
                for n in range(3):
                    r = CH * (n % 2)
                    for h in range(GH):
                        o = 64 * (h % 2)
                        c = (n % 2) * BANK + (n // 2) * 256 + (h // 2) * P
                        m = mm(b[o:o + 64, c:c + P], gl_ks[r:r + CH, n // 2, h * 64:(h + 1) * 64],
                               proj[r:r + CH, n // 2, COL_VC + h * P:COL_VC + (h + 1) * P], start=True, stop=True)
                filled(m, ("gu", l))
                gates(3)
                copied(pe, ("gqkT", l, 0), ("gqkT", l, 1))
                for t in range(T):
                    b = open_bank(pe, ("gatt", l, t), 2)
                    for h in range(GH):
                        o = 64 * (h % 2)
                        c = BANK * (h % 2) + (h // 2) * P
                        m = mm(b[:, c:c + P], gl_qkT[o:o + 64, 2 + h // 2, t * P:(t + 1) * P],
                               gl_qkT[o:o + 64, h // 2, t * P:(t + 1) * P], start=True, stop=True)
                    filled(m, ("gatt", l, t))
                b = open_bank(pe, ("sgT", l))
                for g in range(4):
                    m = turn_(b[:, g * P:(g + 1) * P], sgw[:, g, :], ident[:, :])
                filled(m, ("sgT", l))
                gates(4)
                pe.wait_ge(ev("vn_ready"), l + 1)
                copied(pe, ("sgT", l))
                for t in range(T):
                    b = open_bank(pe, ("sv", l, t))
                    for g in range(4):
                        m = mm(b[:, g * P:(g + 1) * P], sgwT[:, g, :], proj[:, t, COL_V + g * P:COL_V + (g + 1) * P],
                               start=True, stop=True)
                    filled(m, ("sv", l, t))
                copied(pe, ("gatt", l, 0), ("gatt", l, 1))
                copied(pe, ("gu", l))
                for t in range(T):
                    b = open_bank(pe, ("go", l, t), 2)
                    for h in range(GH):
                        o = 64 * (h % 2)
                        c = BANK * (h % 2) + (h // 2) * P
                        mm(b[:, c:c + P], gl_att[:, t, 2 * (h % 2) + h // 2, :], proj[:, t, COL_VC + h * P:COL_VC + (h + 1) * P],
                           start=True, stop=True, skip_group_check=True)
                        for n in range(max(1, 2 * t), 2 * t + 2):
                            r = CH * (n % 2)
                            m = mm(b[r:r + CH, c:c + P], gl_qkT[o:o + 64, h // 2, n * CH:(n + 1) * CH],
                                   gl_st[o:o + 64, n - 1, h // 2, :], start=False, stop=True, skip_group_check=True)
                    filled(m, ("go", l, t))
                gates(5)

                for i, c0 in enumerate((COL_ZB, COL_U, COL_ZC)):
                    if i == 1:
                        copied(pe, ("sv", l, 0), ("sv", l, 1))
                    else:
                        pe.wait_ge(ev(f"y{i}_ready"), l + 1)
                    for t in range(T):
                        b = open_bank(pe, ("yT", l, i, t))
                        for k in range(4):
                            m = turn_(b[:, k * P:(k + 1) * P], proj[:, t, c0 + k * P:c0 + (k + 1) * P], ident[:, :])
                        filled(m, ("yT", l, i, t))
                    w = take_slot()
                    copied(pe, ("yT", l, i, 0), ("yT", l, i, 1))
                    for t in range(T):
                        for h in range(2):
                            b = open_bank(pe, ("br", l, i, t, h))
                            for k in range(4):
                                m = mm(b, yT[:, i, k, t * P:(t + 1) * P], w[:, k, h * BANK:(h + 1) * BANK],
                                       start=(k == 0), stop=(k == 3))
                            filled(m, ("br", l, i, t, h))
                    slot_done(("br", l, i, T - 1, 1))
                pe.wait_ge(ev("merged_ready"), l + 1)
                rows_T(("mT", l), merged)
                gemm_rows(("wo", l), hT)

            def turns(name, pieces, rows_=P):
                b = open_bank(pe, name)
                for k, piece in enumerate(pieces):
                    m = turn_(b[0:rows_, k * P:(k + 1) * P], piece, ident[:, :])
                filled(m, name)

            def p2(i):
                gemm_cols(("p2", i), hT)

            norm_T(2)
            for i, (c0, n) in enumerate(SLOTS2):
                w = take_slot()
                for f in range(n // P):
                    b = open_bank(pe, ("cv", 4 * i + f))
                    for k in range(KD):
                        m = mm(b[:, 0:S], w[:, k, f * P:(f + 1) * P], hT[:, k, :], start=(k == 0), stop=(k == KD - 1))
                    filled(m, ("cv", 4 * i + f))
                slot_done(("cv", 4 * i + n // P - 1))
            p2(0)
            p2(1)
            pe.wait_ge(ev("lfg_ready"), 1)
            b = open_bank(pe, "cum")
            for t in range(T):
                for d in range(2):
                    mm(b[:, t * 8 + d * 4:t * 8 + d * 4 + 4], causal[:, d, :], sp[:, t, d * 4:d * 4 + 4], start=True, stop=True)
                    c = 32 + t * 12 + d * 6
                    mm(b[:, c:c + 6], causal[:, d, :], gd_g[:, t, d * 6:d * 6 + 6], start=True, stop=True)
                mm(b[:, 16 + t * 8:24 + t * 8], blk[:, :], sp[:, t, 0:8], start=True, stop=True)
                m = mm(b[:, 56 + t * 12:68 + t * 12], blk[:, :], gd_g[:, t, :], start=True, stop=True)
            filled(m, "cum")
            p2(2)
            pe.wait_ge(ev("second_in"), 16 * N_SECOND_DMA)
            pe.wait_ge(ev("second_const"), 1)
            for t in range(T):
                for r in range(3):
                    b = open_bank(pe, ("nab", t, r))
                    filled(mm(b, mirror[:, :], na_raw[:, t, 2 * r:2 * r + 2, :].rearrange("p h n -> p (h n)"), start=True, stop=True), ("nab", t, r))
            pe.wait_ge(ev("mlg_ready"), 1)
            copied(pe, "cum")
            b = open_bank(pe, "mlrow", 2)
            for q, src in enumerate((ml_g, ml_bl)):
                for d in range(2):
                    for t in range(T):
                        c = ((q * 2 + d) * 2 + t) * P
                        m = turn_(b[0:MLH, c:c + P], src[:, t, d * 4:d * 4 + 4], ident[:, :])
            filled(m, "mlrow")
            p2(3)
            for t in range(T):
                copied(pe, ("p2", 2, t, 0), ("p2", 3, t, 0))
                for q in range(2):
                    turns(("naT", t, q), [proj2[:, t, (3 * q + k) * P:(3 * q + k + 1) * P] for k in range(3)])
            p2(4)
            copied(pe, *[("naT", t, q) for t in range(T) for q in range(2)])
            for t in range(T):
                for z in range(2):
                    b = open_bank(pe, ("nas", t, z), 2)
                    o = 64 * z
                    for r in range(3):
                        m = mm(b[:, r * S:(r + 1) * S], na_T[o:o + 64, r, t * P:(t + 1) * P], na_T[o:o + 64, 3 + r, :],
                               start=True, stop=True)
                    filled(m, ("nas", t, z))
            p2(5)
            pe.wait_ge(ev("mlm_ready"), 1)
            b = open_bank(pe, "mlcol")
            for q in range(3):
                for t in range(T):
                    for d in range(2):
                        c = (q * 2 + t) * 8 + d * 4
                        m = turn_(b[:, c:c + 4], ml_max[0:MLH, q, d, t * P:(t + 1) * P], ident[0:MLH, 0:MLH])
            filled(m, "mlcol")
            for t in range(T):
                for d in range(2):
                    b = open_bank(pe, ("mrow", t, d))
                    for h in range(MLH):
                        m = mm(b[:, h * P:(h + 1) * P], sel[0:MLH, h, :], ml_max[0:MLH, 0, d, t * P:(t + 1) * P],
                               start=True, stop=True)
                    filled(m, ("mrow", t, d))
            for t in range(T):
                copied(pe, ("p2", 4, t, 0), ("p2", 5, t, 0))
                turns(("mlT", t), [proj2[:, t, C_MLQ + k * P:C_MLQ + (k + 1) * P] for k in range(4)])
            for t in range(T):
                for q in range(3):
                    pe.wait_ge(ev("conv_ready"), q + 1)
                    turns(("gT", t, q), [conv[:, 3 * q + k, t * P:(t + 1) * P] for k in range(3)])
            copied(pe, ("mlT", 0), ("mlT", 1))
            for t in range(T):
                b = open_bank(pe, ("mqk", t), 2)
                for h in range(MLH):
                    o, c = 64 * (h % 2), BANK * (h % 2) + (h // 2) * P
                    m = mm(b[:, c:c + P], ml_T[o:o + 64, 2 + h // 2, t * P:(t + 1) * P], ml_T[o:o + 64, h // 2, t * P:(t + 1) * P],
                           start=True, stop=True)
                filled(m, ("mqk", t))
            for t in range(T):
                pe.wait_ge(ev("nap_ready"), t + 1)
                for q in range(3):
                    flat = na_s[:, t, :, :, :].rearrange("p z r n -> p (z r n)")
                    turns(("napT", t, q), [flat[:, (4 * q + k) * P:(4 * q + k + 1) * P] for k in range(4)])
            pe.wait_ge(ev("mle_ready"), 1)
            b = open_bank(pe, "mldec")
            for n in range(4):
                for z in range(2):
                    m = mm(b[64 * z:64 * z + 64, n * 4:n * 4 + 4], first[:, n % 2, :], ml_e[:, 3, n // 2, z::2], start=True, stop=True)
            filled(m, "mldec")
            pe.wait_ge(ev("mlk_ready"), 1)
            for d in range(2):
                b = open_bank(pe, ("mu", d), 2)
                for j in range(3):
                    n = j if d == 0 else 3 - j
                    r = CH * (n % 2)
                    for h in range(MLH):
                        o, c = 64 * (h % 2), BANK * (j % 2) + (j // 2) * 130 + (h // 2) * 65
                        m = mm(b[o:o + 64, c:c + 65], ml_k[r:r + CH, n // 2, d, h, :], ml_v[r:r + CH, n // 2, h, :],
                               start=True, stop=True)
                filled(m, ("mu", d))
            copied(pe, *[("napT", t, q) for t in range(T) for q in range(3)])
            for t in range(T):
                b = open_bank(pe, ("napv", t))
                for h in range(NH):
                    for k in range(2):
                        i = ((t * 2 + h % 2) * 3 + h // 2) * 2 + k
                        m = mm(b[:, h * HD:(h + 1) * HD], na_pT[:, i, :], proj2[:, k, 768 + h * HD:768 + (h + 1) * HD],
                               start=(k == 0), stop=(k == 1))
                filled(m, ("napv", t))
            copied(pe, ("mu", 0), ("mu", 1))
            pe.wait_ge(ev("mlp_ready"), 1)
            for t in range(T):
                for d in range(2):
                    b = open_bank(pe, ("mint", t, d), 2)
                    for h in range(MLH):
                        o, c = 64 * (h % 2), BANK * (h % 2) + (h // 2) * 65
                        for n in (2 * t, 2 * t + 1):
                            j = n if d == 0 else 3 - n
                            r = CH * (n % 2)
                            m = mm(b[r:r + CH, c:c + 65], ml_T[o:o + 64, h // 2, n * CH:(n + 1) * CH], ml_c[o:o + 64, d, j, h // 2, :],
                                   start=True, stop=True)
                    filled(m, ("mint", t, d))
                    b = open_bank(pe, ("mia", t, d))
                    for h in range(MLH):
                        m = mm(b[:, h * 65:(h + 1) * 65], ml_p[:, t, d, h, :], ml_v[:, t, h, :], start=True, stop=True)
                    filled(m, ("mia", t, d))

            pe.wait_ge(ev("gdqk_ready"), 1)
            for t in range(T):
                for q in range(2):
                    turns(("gqT", t, q), [gd[:, t, (3 * q + k) * P:(3 * q + k + 1) * P] for k in range(3)])
            pe.wait_ge(ev("gdkb_ready"), 1)
            for t in range(T):
                for d in range(2):
                    flat = gd_kb[:, t, d, :, :].rearrange("p h n -> p (h n)")
                    turns(("gkT", t, d), [flat[:, k * P:(k + 1) * P] for k in range(3)])
            for t in range(T):
                for d in range(2):
                    for z in range(2):
                        b = open_bank(pe, ("gl", t, d, z))
                        for r in range(3):
                            c = d * 6 + 2 * r + z
                            m = mm(b[:, r * P:(r + 1) * P], gd_g[:, t, c:c + 1].to_broadcast([P, P]), causal[:, d, :],
                                   start=True, stop=True)
                        filled(m, ("gl", t, d, z))
            copied(pe, *[("gqT", t, q) for t in range(T) for q in range(2)], *[("gkT", t, d) for t in range(T) for d in range(2)])
            for t in range(T):
                for d in range(2):
                    for z in range(2):
                        o = 64 * z
                        b = open_bank(pe, ("kk", t, d, z))
                        for r in range(3):
                            m = mm(b[:, r * P:(r + 1) * P], gd_T[o:o + 64, 3 + r, t * P:(t + 1) * P], gd_kbT[o:o + 64, t, d, r, :],
                                   start=True, stop=True)
                        filled(m, ("kk", t, d, z))
            for t in range(T):
                for z in range(2):
                    o = 64 * z
                    b = open_bank(pe, ("kq", t, z))
                    for r in range(3):
                        m = mm(b[:, r * P:(r + 1) * P], gd_T[o:o + 64, 3 + r, t * P:(t + 1) * P], gd_T[o:o + 64, r, t * P:(t + 1) * P],
                               start=True, stop=True)
                    filled(m, ("kq", t, z))
            GROUPS = [(t, d, z) for t in range(T) for d in range(2) for z in range(2)]
            pe.wait_ge(ev("inv0_ready"), 1)
            for t, d, z in GROUPS:
                turns(("inv0", t, d, z), [gd_inv[1][:, t, d, 3 * z + r, :] for r in range(3)])
            for k in range(1, 6):
                def product(g):
                    t, d, z = g
                    copied(pe, ("inv0", *g) if k == 1 else ("ty", k - 1, *g))
                    b = open_bank(pe, ("tx", k, *g))
                    for r in range(3):
                        i = 3 * z + r
                        m = mm(b[:, r * P:(r + 1) * P], gd_a[:, t, d, i, :], gd_inv[0][:, t, d, i, :], start=True, stop=True)
                    filled(m, ("tx", k, *g))

                def update(n, g):
                    t, d, z = g
                    copied(pe, ("tx", k, *g))
                    if k > 1:
                        copied(pe, ("tz", k - 1, *g))
                    for kind in ("ty", "tz")[k == 5:]:
                        b = open_bank(pe, (kind, k, *g))
                        for r in range(3):
                            xr, rr = gd_x[:, n % 4, r, :], gd_inv[1][:, t, d, 3 * z + r, :]
                            if kind == "ty":
                                m = mm(b[:, r * P:(r + 1) * P], rr, xr, start=True, stop=True)
                            else:
                                m = mm(b[:, r * P:(r + 1) * P], xr, rr, start=True, stop=True)
                        filled(m, (kind, k, *g))

                for n, g in enumerate(GROUPS):
                    product(g)
                    if n >= 2:
                        update(n - 2, GROUPS[n - 2])
                for n in (6, 7):
                    update(n, GROUPS[n])
            b = open_bank(pe, "gdec2")
            for n in range(4):
                for z in range(2):
                    m = mm(b[64 * z:64 * z + 64, n * 6:n * 6 + 6], first[:, n % 2, :], gd_e[:, 2, n // 2, z::2], start=True, stop=True)
            filled(m, "gdec2")
            for t in range(T):
                for d in range(2):
                    copied(pe, ("tz", 5, t, d, 0), ("tz", 5, t, d, 1))
                    b = open_bank(pe, ("gu2", t, d))
                    for h in range(GNH):
                        m = mm(b[:, h * HD:(h + 1) * HD], gd_inv[1][:, t, d, 3 * (h % 2) + h // 2, :], gd_vb[:, t, d, h, :],
                               start=True, stop=True)
                    filled(m, ("gu2", t, d))
                    b = open_bank(pe, ("gw", t, d))
                    for h in range(GNH):
                        o, c = 64 * (h % 2), (h // 2) * P
                        m = mm(b[o:o + 64, c:c + P], gd_kbe[:, t, d, h, :], gd_inv[1][:, t, d, 3 * (h % 2) + h // 2, :],
                               start=True, stop=True)
                    filled(m, ("gw", t, d))
            copied(pe, *[(n, t, d) for n in ("gu2", "gw") for t in range(T) for d in range(2)])
            for j in range(4):
                for d in range(2):
                    n = j if d == 0 else 3 - j
                    t, r = n // 2, CH * (n % 2)
                    if j:
                        copied(pe, ("kv", j - 1, d))
                        b = open_bank(pe, ("ws", j, d), 2)
                        for h in range(GNH):
                            o, c = 64 * (h % 2), BANK * (h % 2) + (h // 2) * HD
                            m = mm(b[r:r + CH, c:c + HD], gd_wk[o:o + 64, t, d, h // 2, r:r + CH], gd_st[o:o + 64, j, d, h // 2, :],
                                   start=True, stop=True)
                        filled(m, ("ws", j, d))
                for d in range(2):
                    n = j if d == 0 else 3 - j
                    t, r = n // 2, CH * (n % 2)
                    if j < 3:
                        if j:
                            copied(pe, ("ws", j, d))
                        else:
                            pe.wait_ge(ev("vn0_ready"), d + 1)
                        b = open_bank(pe, ("kv", j, d))
                        for h in range(GNH):
                            o, c = 64 * (h % 2), (h // 2) * HD
                            m = mm(b[o:o + 64, c:c + HD], gd_ks[r:r + CH, t, d, h, :], gd_vn[r:r + CH, t, d, h, :],
                                   start=True, stop=True)
                        filled(m, ("kv", j, d))
            copied(pe, ("ws", 3, 0), ("ws", 3, 1))
            for t in range(T):
                for d in range(2):
                    b = open_bank(pe, ("oi", t, d), 2)
                    for h in range(GNH):
                        o, c = 64 * (h % 2), BANK * (h % 2) + (h // 2) * HD
                        for n in (2 * t, 2 * t + 1):
                            j = n if d == 0 else 3 - n
                            r = CH * (n % 2)
                            m = mm(b[r:r + CH, c:c + HD], gd_T[o:o + 64, h // 2, n * CH:(n + 1) * CH], gd_st[o:o + 64, j, d, h // 2, :],
                                   start=True, stop=True)
                    filled(m, ("oi", t, d))
                    b = open_bank(pe, ("oa", t, d))
                    for h in range(GNH):
                        m = mm(b[:, h * HD:(h + 1) * HD], gd_att[:, t, d, 3 * (h % 2) + h // 2, :], gd_vn[:, t, d, h, :],
                               start=True, stop=True)
                    filled(m, ("oa", t, d))
            pe.wait_ge(ev("mixed_ready"), 1)
            rows_T(("yT2",), y2)
            gemm_rows(("wo2",), hT)

            norm_T(3)
            for i in range(2):
                gemm_T(("xk", i), memT, 2)
            for i in range(2):
                gemm_cols(("xv", i), memT)
            norm_T(4)
            for i in range(2):
                gemm_T(("xq", i), hT, 2)
            copied(pe, *[(n, i, g) for n in ("xk", "xq") for i in range(2) for g in range(2)])
            for t in range(T):
                for g in range(2):
                    b = open_bank(pe, ("xs", t, g))
                    for h in range(2):
                        for k in range(2):
                            i = 2 * (2 * g + h) + k
                            m = mm(b[:, h * S:(h + 1) * S], xq_T[:, i, t * P:(t + 1) * P], xk_T[:, i, :], start=(k == 0), stop=(k == 1))
                    filled(m, ("xs", t, g))
            for t in range(T):
                pe.wait_ge(ev("xp_ready"), t + 1)
                for g in range(2):
                    turns(("xpT", t, g), [x_s[:, t, 2 * g + h, m_ * P:(m_ + 1) * P] for m_ in range(2) for h in range(2)])
            copied(pe, *[("xpT", t, g) for t in range(T) for g in range(2)], *[("xv", i, t, 0) for i in range(2) for t in range(T)])
            for h in range(XH):
                b = open_bank(pe, ("xo", h))
                for e in range(2):
                    for k in range(2):
                        c = h * XD + e * P
                        m = mm(b[:, e * S:(e + 1) * S], x_v[:, k, c:c + P], x_pT[:, k, h, :], start=(k == 0), stop=(k == 1))
                filled(m, ("xo", h))
            copied(pe, *[("xo", h) for h in range(XH)])
            gemm_rows(("wxo",), x_oT)

            norm_T(5)
            for i in range(8):
                gemm_T(("f1", i), hT, 2)
            pe.wait_ge(ev("h1_ready"), 16)
            gemm_rows(("f2",), h1T, 8)

        @block.vector
        def _(dve):
            V = nc.vector

            def v(ins, name="dve"):
                done(dve, ins, name)

            asked = [0]

            def rsqrt():
                asked[0] += 1
                dve.wait_ge(ev("rs_out"), asked[0])

            def normalise(i, src=None):
                src = x if src is None else src
                dve.wait_ge(ev("ssq_ready"), 2 * (i + 1))
                v(V.tensor_scalar(rin[:, 0:2], ssq[:, 0:2], 1.0 / D, EPS, ALU.mult, ALU.add), "rs_in")
                rsqrt()
                for t in range(T):
                    v(V.tensor_scalar(xn[:, t * D:(t + 1) * D], src[:, t, :], rout[:, t:t + 1], None, ALU.mult), "xn_ready")

            def add_x(tag):
                for t in range(T):
                    for h in range(2):
                        b = full(dve, (*tag, t, h))
                        dst = x[:, t, h * BANK:(h + 1) * BANK]
                        v(V.tensor_tensor(dst, dst, b, ALU.add), free((*tag, t, h)))

            def turned(i, r0, dst):
                for t in range(T):
                    for h in range(2):
                        n = ("xT", i, t, h)
                        b = full(dve, n).rearrange("p (k n) -> p k n", k=4)
                        v(V.tensor_tensor(dst[:, 4 * h:4 * h + 4, t * P:(t + 1) * P], b,
                                          bc(cols[:, r0 + 4 * h:r0 + 4 * h + 4], 2, P), ALU.mult), free(n))

            def rotary_tables():
                dve.wait_ge(ev("pos_in"), 16)
                v(V.tensor_copy(posf[:, :], posi[:, :]))
                for t in range(T):
                    v(V.tensor_scalar(ang[:, t, :], freq[:, :], posf[:, t:t + 1], None, ALU.mult))
                v(V.tensor_scalar(ang2, ang1, float(1.0 / TWO_PI), None, ALU.mult))
                v(V.tensor_scalar(ang2, ang2, ROUND, None, ALU.add))
                v(V.tensor_scalar(ang2, ang2, -ROUND, None, ALU.add))
                for part in (PI_A, PI_B, PI_C):
                    v(V.scalar_tensor_tensor(out=ang1, in0=ang2, scalar=-part, in1=ang1, op0=ALU.mult, op1=ALU.add))
                v(V.tensor_scalar(ang1, ang1, 3.1415925, -3.1415925, ALU.min, ALU.max))
                v(V.tensor_scalar(ang2, ang1, -1.0, None, ALU.mult))
                v(V.tensor_tensor(ang2, ang2, ang1, ALU.max))
                v(V.tensor_scalar(ang2, ang2, -1.0, float(np.pi / 2), ALU.mult, ALU.add), "angle_ready")

            for l in range(DEPTH):
                if l == 0:
                    dve.wait_ge(ev("const_ready"), 1)
                normalise(l)
                if l == 0:
                    v(V.tensor_copy(cols[:, :], full(dve, "cols")[:, 0:R_END]), free("cols"))
                turned(l, R_NORM + KD * l, hT)
                if l == 0:
                    rotary_tables()

                dve.wait_ge(ev("cssq_ready"), l + 1)
                v(V.tensor_scalar(rin[:, 0:2], ssq[:, 4:6], 1.0 / 256, EPS, ALU.mult, ALU.add))
                v(V.tensor_scalar(rin[:, 2:4], ssq[:, 6:8], 1.0 / 128, EPS, ALU.mult, ALU.add), "rs_in")
                rsqrt()
                for t in range(T):
                    v(V.tensor_scalar(cn[:, t, 0:256], proj[:, t, COL_CQ:COL_CQ + 256], rout[:, t:t + 1], None, ALU.mult))
                for t in range(T):
                    ins = V.tensor_scalar(cn[:, t, 256:384], proj[:, t, COL_CKV:COL_CKV + 128], rout[:, 2 + t:3 + t], None,
                                          ALU.mult)
                    v(ins, "cn_ready" if t else "dve")
                for t in range(T):
                    n = ("cT", l, t)
                    b = full(dve, n)
                    v(V.tensor_tensor(cT[:, 0:2, t * P:(t + 1) * P], b[:, 0:256].rearrange("p (k n) -> p k n", k=2),
                                      bc(cols[:, R_CQ + 2 * l:R_CQ + 2 * l + 2], 2, P), ALU.mult))
                    v(V.tensor_scalar(cT[:, 2, t * P:(t + 1) * P], b[:, 256:384], cols[:, R_CKV + l:R_CKV + l + 1], None,
                                      ALU.mult), free(n))
                for t in range(T):
                    v(V.tensor_copy(qk[:, t, MH:2 * MH, NOPE:MQK], bc(proj[:, t, COL_KR:COL_KR + ROPE], 1, MH)),
                      "kr_ready" if t else "dve")
                dve.wait_ge(ev("qsq_ready"), l + 1)
                dve.wait_ge(ev("layer_in"), 16 * N_LAYER_DMA * (l + 1))
                qk2 = at(arena, RA, 2 * T * MH, MQK)
                v(V.tensor_reduce(ssq[:, 0:32], at(tmp, 0, 32, MQK), X, ALU.add))
                v(V.tensor_scalar(rin[:, :], ssq[:, 0:32], 1.0 / MQK, EPS, ALU.mult, ALU.add), "rs_in")
                rsqrt()
                v(V.tensor_tensor(qk2, qk2, bc(rout[:, :], 2, MQK), ALU.mult))
                for t in range(T):
                    for z in range(2):
                        dst = qk[:, t, z * MH:(z + 1) * MH, :]
                        v(V.tensor_tensor(dst, dst, bc(qk_g[:, z, :], 1, MH), ALU.mult))
                if l == 0:
                    dve.wait_ge(ev("trig_ready"), 1)
                n = 2 * MH * HALF
                for t in range(T):
                    x1, x2 = qk[:, t, :, NOPE:NOPE + HALF], qk[:, t, :, NOPE + HALF:MQK]
                    cos, sin = bc(trig[:, 0, t, :], 1, 2 * MH), bc(trig[:, 1, t, :], 1, 2 * MH)
                    r = [at(tmp, k * n, 2 * MH, HALF) for k in range(4)]
                    v(V.tensor_tensor(r[0], x1, cos, ALU.mult))
                    v(V.tensor_tensor(r[1], x2, sin, ALU.mult))
                    v(V.tensor_tensor(r[2], x1, sin, ALU.mult))
                    v(V.tensor_tensor(r[3], x2, cos, ALU.mult))
                    v(V.tensor_tensor(x1, r[0], r[1], ALU.subtract))
                    v(V.tensor_tensor(x2, r[2], r[3], ALU.add), "qk_ready" if t else "dve")

                uv = proj[:, :, 0:1024]
                th = at(tmp, 0, T, 1024)
                dve.wait_ge(ev("uvsq_ready"), l + 1)
                v(V.tensor_scalar(th, th, 0.044715, 1.0, ALU.mult, ALU.add))
                v(V.tensor_tensor(th, th, uv, ALU.mult), "uvarg_ready")
                dve.wait_ge(ev("uvtanh_ready"), l + 1)
                v(V.scalar_tensor_tensor(out=uv, in0=th, scalar=1.0, in1=uv, op0=ALU.add, op1=ALU.mult))
                zz = proj[:, :, COL_Z:COL_Z + 512]
                tz = at(tmp, 2048, T, 512)
                v(V.scalar_tensor_tensor(out=zz, in0=tz, scalar=1.0, in1=zz, op0=ALU.add, op1=ALU.mult), "tmp_free")
                for t in range(T):
                    v(V.bn_stats(stat[:, t, 0:6], proj[:, t, COL_V:COL_V + 512]))
                    v(V.bn_aggr(stat[:, t, 6:8], stat[:, t, 0:6]))
                v(V.tensor_scalar(rin[:, 0:2], stat[:, :, 7], 4 * EPS, None, ALU.add), "rs_in")
                rsqrt()
                for t in range(T):
                    vt = proj[:, t, COL_V:COL_V + 512]
                    v(V.tensor_scalar(vt, vt, stat[:, t, 6:7], rout[:, t:t + 1], ALU.subtract, ALU.mult))
                vb = proj[:, :, COL_V:COL_V + 512]
                v(V.tensor_tensor(vb, vb, bc(ln_g, 1, T), ALU.mult))
                v(V.tensor_tensor(vb, vb, bc(ln_b, 1, T), ALU.add), "vn_ready")
                ub = proj[:, :, 0:512]
                v(V.tensor_tensor(ub, ub, zz, ALU.mult))

                for j, (t, h0, hn) in enumerate(SC):
                    n = P * (t + 1)
                    copied(dve, ("sc", l, j))
                    s3 = sc[:, j, :].rearrange("p (h n) -> p h n", n=n)
                    v(V.memset(s3[0:CH, :, n - CH:n], NEG))
                    v(V.tensor_reduce(smax[:, 0:hn], s3, X, ALU.max))
                    v(V.tensor_tensor(s3, s3, bc(smax[:, 0:hn], 2, n), ALU.subtract), "s_ready")
                for j, (t, h0, hn) in enumerate(SC):
                    n = P * (t + 1)
                    dve.wait_ge(ev("p_ready"), 3 * l + j + 1)
                    s3 = sc[:, j, :].rearrange("p (h n) -> p h n", n=n)
                    v(V.tensor_reduce(ssum[:, t * MH + h0:t * MH + h0 + hn], s3, X, ALU.add))
                v(V.reciprocal(ssum[:, :], ssum[:, :]))

                n = ("gg", l)
                dve.wait_ge(ev("gln_ready"), l + 1)
                b = full(dve, n).rearrange("p (t n) -> p t n", t=T)
                v(V.tensor_scalar(gl_la, b, 0.0, None, ALU.min), free(n))
                v(V.tensor_tensor(gl_la, gl_la, gl_b, ALU.subtract), "la_ready")

                for t in range(T):
                    n = ("pv", l, t)
                    b = full(dve, n).rearrange("p (h n) -> p h n", h=MH)
                    v(V.tensor_tensor(at(tmp, t * 512, MH, NOPE), b, bc(ssum[:, t * MH:(t + 1) * MH], 2, NOPE), ALU.mult), free(n))
                zb = proj[:, :, COL_ZB:COL_ZB + 512]
                zc = proj[:, :, COL_ZC:COL_ZC + 512]
                dve.wait_ge(ev("zb_ready"), l + 1)
                tb = at(tmp, 1024, T, 512)
                v(V.scalar_tensor_tensor(out=zb, in0=tb, scalar=1.0, in1=zb, op0=ALU.add, op1=ALU.mult))
                v(V.tensor_tensor(zb, zb, at(tmp, 0, T, 512), ALU.mult), "y0_ready")
                tc = at(tmp, 2048, T, 512)
                v(V.scalar_tensor_tensor(out=zc, in0=tc, scalar=1.0, in1=zc, op0=ALU.add, op1=ALU.mult))

                if l == 0:
                    dve.wait_ge(ev("const_ready"), 2)
                qc, kc = proj[:, :, COL_QC:COL_QC + 256], proj[:, :, COL_KC:COL_KC + 256]
                dve.wait_ge(ev("ge_ready"), l + 1)
                v(V.scalar_tensor_tensor(out=gl_qk[:, :, 0:256], in0=gl_e, scalar=GDK ** -0.5, in1=qc, op0=ALU.mult,
                                         op1=ALU.mult))
                v(V.tensor_tensor(gl_qk[:, :, 256:512], gl_e2, kc, ALU.mult))
                b = full(dve, ("gbl", l)).rearrange("p (t n) -> p t n", t=T)
                v(V.tensor_tensor(gl_b, b, gl_b, ALU.subtract), free(("gbl", l)))
                dve.wait_ge(ev("gks_ready"), l + 1)
                v(V.tensor_tensor(gl_ks, gl_b, kc, ALU.mult), "gqk_ready")
                copied(dve, ("gdec", l))
                b = full(dve, ("gu", l), 2)
                v(V.tensor_copy(gl_st[:, 0, :, :], b[:, 0:256].rearrange("p (a n) -> p a n", a=2)))
                for n in range(1, 3):
                    for pr in range(2):
                        c = 2 * (n - 1) + pr
                        c0 = (n % 2) * BANK + (n // 2) * 256 + pr * P
                        ins = V.scalar_tensor_tensor(out=gl_st[:, n, pr, :], in0=gl_st[:, n - 1, pr, :], scalar=gdec[:, c:c + 1],
                                                     in1=b[:, c0:c0 + P], op0=ALU.mult, op1=ALU.add)
                        v(ins, free(("gu", l)) if (n, pr) == (2, 1) else "dve")
                for t in range(T):
                    n = ("gatt", l, t)
                    b = full(dve, n, 2)
                    for z in range(2):
                        ins = V.tensor_tensor(gl_att[:, t, 2 * z:2 * z + 2, :],
                                              b[:, z * BANK:z * BANK + 256].rearrange("p (h n) -> p h n", h=2),
                                              bc(causal[:, 0, :], 1, 2), ALU.mult)
                        v(ins, free(n) if z else "dve")
                n = ("sgT", l)
                b = full(dve, n).rearrange("p (g n) -> p g n", g=4)
                v(V.tensor_copy(sgwT[:, :, :], b))
                v(V.memset(sgwT[CH:P, :, 0:CH], 0.0), free(n))
                for t in range(T):
                    n = ("sv", l, t)
                    b = full(dve, n)
                    for g in range(4):
                        u = proj[:, t, g * P:(g + 1) * P]
                        c = R_SGB + 4 * l + g
                        last_one = (t, g) == (T - 1, 3)
                        v(V.scalar_tensor_tensor(out=u, in0=b[:, g * P:(g + 1) * P], scalar=cols[:, c:c + 1], in1=u,
                                                 op0=ALU.add, op1=ALU.mult), free(n) if g == 3 else "dve")
                for t in range(T):
                    n = ("go", l, t)
                    b = full(dve, n, 2).rearrange("p (z n) -> p z n", z=2)
                    o4 = gl_o[:, t, :].rearrange("p (h z n) -> p z h n", h=2, z=2)
                    for z in range(2):
                        ins = V.tensor_copy(o4[:, z, :, :], b[:, z, 0:256].rearrange("p (h n) -> p h n", h=2))
                        v(ins, free(n) if z else "dve")
                v(V.tensor_tensor(gl_sq, gl_o, gl_o, ALU.mult))
                v(V.tensor_reduce(ssq[:, 0:8], at(arena, RC + 1024, 8, P), X, ALU.add))
                v(V.tensor_scalar(rin[:, 0:8], ssq[:, 0:8], 1.0 / GDV, EPS, ALU.mult, ALU.add), "rs_in")
                rsqrt()
                o3 = at(arena, RC, 8, P)
                v(V.tensor_tensor(o3, o3, bc(rout[:, 0:8], 2, P), ALU.mult))
                v(V.tensor_tensor(o3, o3, bc(o_g, 1, 8), ALU.mult))
                v(V.tensor_tensor(zc, zc, gl_o, ALU.mult), "y2_ready")

                for i in range(3):
                    g = BRANCHES[i]
                    for t in range(T):
                        for h in range(2):
                            n = ("br", l, i, t, h)
                            gt = gate[:, t, g * D + h * BANK:g * D + (h + 1) * BANK]
                            copied(dve, ("gate", l, 2 * g + h, t, 0))
                            b = full(dve, n)
                            dst = merged[:, t, h * BANK:(h + 1) * BANK] if i == 0 else gt
                            v(V.scalar_tensor_tensor(out=dst, in0=gt, scalar=1.0, in1=b, op0=ALU.add, op1=ALU.mult), free(n))
                    if i:
                        m = merged[:, :, :]
                        v(V.tensor_tensor(m, m, gate[:, :, g * D:(g + 1) * D], ALU.add), "merged_ready" if i == 2 else "dve")
                add_x(("wo", l))

            normalise(2)
            turned(2, R_MIX, hT)
            for j in range(9):
                n = ("cv", j)
                b = full(dve, n)[:, 0:S]
                dst = conv[:, j, :]

                def tap(k):
                    c = R_CONV + 9 * k + j
                    return cols[:, c:c + 1]

                v(V.tensor_scalar(dst, b, tap(2), None, ALU.mult))
                for k in (0, 1, 3, 4):
                    o = k - 2
                    lo, hi = max(0, -o), S - max(0, o)
                    ins = V.scalar_tensor_tensor(out=dst[:, lo:hi], in0=b[:, lo + o:hi + o], scalar=tap(k), in1=dst[:, lo:hi],
                                                 op0=ALU.mult, op1=ALU.add)
                    v(ins, free(n) if k == 4 else "dve")
            v(V.memset(ssq[:, 31:32], 0.0), "conv_done")
            copied(dve, *[("p2", i, t, 0) for i in range(2) for t in range(T)])
            dve.wait_ge(ev("second_in"), 16 * N_SECOND_DMA)
            v(V.tensor_tensor(ml_if, proj2[:, :, C_MLI:C_MLI + 16], bc(if_b, 1, T), ALU.add))
            v(V.tensor_copy(sp[:, :, 0:8], ml_if[:, :, 8:16]))
            v(V.tensor_tensor(sp[:, :, 8:20], proj2[:, :, K_GDA:K_GDA + 12], bc(dt_b, 1, T), ALU.add), "sp_ready")
            for q in range(3):
                dve.wait_ge(ev("convtanh_ready"), q + 1)
                c3 = conv[:, 3 * q:3 * q + 3, :]
                v(V.scalar_tensor_tensor(out=c3, in0=gd_th[:, 3 * q:3 * q + 3, :], scalar=1.0, in1=c3, op0=ALU.add, op1=ALU.mult),
                  "conv_ready")
            dve.wait_ge(ev("spln_ready"), 1)
            v(V.scalar_tensor_tensor(out=gd_g, in0=sp[:, :, 8:20], scalar=0.0, in1=spl[:, :, 8:20], op0=ALU.max, op1=ALU.add))
            v(V.tensor_scalar(gd_g, gd_g, -1.0, None, ALU.mult))
            v(V.tensor_tensor(gd_g, gd_g, bc(a_log, 1, T), ALU.mult))
            v(V.tensor_scalar(beta, beta, 0.5, 0.5, ALU.mult, ALU.add))
            v(V.scalar_tensor_tensor(out=sp[:, :, 0:8], in0=sp[:, :, 0:8], scalar=0.0, in1=spl[:, :, 0:8], op0=ALU.min,
                                     op1=ALU.subtract), "lfg_ready")
            copied(dve, "cum")
            v(V.tensor_tensor(ml_g, ml_if[:, :, 0:8], ml_b, ALU.subtract), "mlg_ready")
            z2 = proj2[:, :, K_GDZ:K_GDZ + 384]
            dve.wait_ge(ev("zt_ready"), 1)
            v(V.scalar_tensor_tensor(out=z2, in0=zt, scalar=1.0, in1=z2, op0=ALU.add, op1=ALU.mult))
            dve.wait_ge(ev("second_const"), 1)
            for t in range(T):
                for r in range(3):
                    n = ("nab", t, r)
                    b = full(dve, n).rearrange("p (z r n) -> p z r n", z=2, r=4)
                    dst = na_s[:, t, :, r, :].rearrange("p z (r n) -> p z r n", r=4)
                    v(V.tensor_tensor(dst, b, bc(bc(na_mask, 1, 4), 1, 2), ALU.add), free(n))
            copied(dve, "mlrow")
            v(V.memset(ml_m[0:MLH, :, :], 0.0))
            for j in range(4):
                for d in range(2):
                    n = j if d == 0 else 3 - j
                    src, dst = ml_row[0:MLH, 0, d, n * CH:(n + 1) * CH], ml_max[0:MLH, 0, d, n * CH:(n + 1) * CH]
                    if d:
                        src, dst = src[:, ::-1], dst[:, ::-1]
                    v(V.tensor_tensor_scan(dst, src, src, ml_m[0:MLH, d, j:j + 1], ALU.max, ALU.max))
                    e = n * CH + (0 if d else CH - 1)
                    v(V.tensor_tensor(ml_m[0:MLH, d, j + 1:j + 2], ml_max[0:MLH, 0, d, e:e + 1], ml_row[0:MLH, 1, d, e:e + 1], ALU.add))
            for q in range(2):
                for d in range(2):
                    src = ml_m[0:MLH, d, q:q + 4]
                    if d:
                        src = src[:, ::-1]
                    dst = ml_max[0:MLH, 1 + q, d, :].rearrange("p (a b) -> p a b", a=4)
                    v(V.tensor_copy(dst, bc(src, 2, CH)), "mlm_ready" if (q, d) == (1, 1) else "dve")
            for t in range(T):
                for z in range(2):
                    n = ("nas", t, z)
                    dst = na_s[:, t, z, :, :].rearrange("p r n -> p (r n)")
                    v(V.scalar_tensor_tensor(out=dst, in0=full(dve, n, 2)[:, 0:768], scalar=HD ** -0.5, in1=dst, op0=ALU.mult,
                                             op1=ALU.add), free(n))
                s3 = na_s[:, t, :, :, :].rearrange("p z r n -> p (z r) n")
                v(V.tensor_reduce(smax[:, 0:6], s3, X, ALU.max))
                v(V.tensor_tensor(s3, s3, bc(smax[:, 0:6], 2, S), ALU.subtract), "nas_ready")
            for t in range(T):
                for d in range(2):
                    n = ("mrow", t, d)
                    b = full(dve, n).rearrange("p (h n) -> p h n", h=MLH)
                    v(V.tensor_tensor(ml_p[:, t, d, :, :], bc(ml_g[:, t, d * 4:d * 4 + 4], 2, P), b, ALU.subtract), free(n))
            flat = ml_p[:, :, :, :, :].rearrange("p t d h n -> p (t d h n)")
            v(V.tensor_scalar(flat, flat, 0.0, None, ALU.min), "mld_ready")
            copied(dve, "mlcol")
            v(V.tensor_tensor(ml_e[:, 0, :, :], ml_col[:, 1, :, :], ml_col[:, 0, :, :], ALU.subtract))
            v(V.scalar_tensor_tensor(out=ml_e[:, 1, :, :], in0=ml_b, scalar=-1.0, in1=ml_col[:, 0, :, :], op0=ALU.mult,
                                     op1=ALU.subtract))
            v(V.tensor_tensor(ml_e[:, 2, :, :], ml_bl, ml_col[:, 2, :, :], ALU.subtract))
            v(V.tensor_tensor(ml_e[:, 3, :, :], ml_e[:, 2, :, :], ml_col[:, 1, :, :], ALU.add))
            v(V.tensor_tensor(ml_e[:, 2, :, :], ml_e[:, 2, :, :], ml_g, ALU.add), "mlarg_ready")
            v(V.tensor_copy(ml_v[:, :, :, 0:HD], proj2[:, :, C_MLV:C_MLV + 256].rearrange("p t (h n) -> p t h n", h=MLH)))
            v(V.memset(ml_v[:, :, :, HD:HD + 1], 1.0))
            v(V.memset(ml_c[:, :, 0, :, :], 0.0))
            for t in range(T):
                dve.wait_ge(ev("nap_ready"), t + 1)
                v(V.tensor_reduce(ssum[:, 6 * t:6 * t + 6], na_s[:, t, :, :, :].rearrange("p z r n -> p (z r) n"), X, ALU.add))
            v(V.reciprocal(ssum[:, 0:12], ssum[:, 0:12]))
            dve.wait_ge(ev("mle_ready"), 1)
            for t in range(T):
                for d in range(2):
                    k = proj2[:, t, C_MLK:C_MLK + 256].rearrange("p (h n) -> p h n", h=MLH)
                    v(V.scalar_tensor_tensor(out=ml_k[:, t, d, :, :], in0=k, scalar=HD ** -0.5,
                                             in1=bc(ml_e[:, 2, t, d * 4:d * 4 + 4], 2, HD), op0=ALU.mult, op1=ALU.mult),
                      "mlk_ready" if (t, d) == (1, 1) else "dve")
            dve.wait_ge(ev("mlx_ready"), 1)
            for t in range(T):
                for d in range(2):
                    p4 = ml_p[:, t, d, :, :]
                    v(V.tensor_tensor(p4, p4, bc(causal[:, d, :], 1, MLH), ALU.mult))
            for t in range(T):
                n = ("mqk", t)
                b = full(dve, n, 2).rearrange("p (z n) -> p z n", z=2)[:, :, 0:256].rearrange("p z (r n) -> p z r n", r=2)
                for d in range(2):
                    p4 = ml_p[:, t, d, :, :].rearrange("p (r z) n -> p z r n", z=2)
                    v(V.tensor_tensor(p4, p4, b, ALU.mult), free(n) if d else "dve")
            v(V.memset(ssq[:, 31:32], 0.0), "mlp_ready")
            copied(dve, "mldec")
            for d in range(2):
                n_ = ("mu", d)
                b = full(dve, n_, 2)
                v(V.tensor_copy(ml_c[:, d, 1, :, :], b[:, 0:130].rearrange("p (r n) -> p r n", r=2)))
                for j in range(1, 3):
                    n = j if d == 0 else 3 - j
                    c = BANK * (j % 2) + (j // 2) * 130
                    dst = ml_c[:, d, j + 1, :, :]
                    v(V.tensor_tensor(dst, ml_c[:, d, j, :, :], bc(ml_dec[:, n, d, :], 2, HD + 1), ALU.mult))
                    v(V.tensor_tensor(dst, dst, b[:, c:c + 130].rearrange("p (r n) -> p r n", r=2), ALU.add),
                      free(n_) if j == 2 else "dve")
            for t in range(T):
                n = ("napv", t)
                b = full(dve, n)[:, 0:384].rearrange("p (r z n) -> p r z n", r=3, z=2)
                dst = y2[:, t, 0:384].rearrange("p (r z n) -> p r z n", r=3, z=2)
                w = ssum[:, 6 * t:6 * t + 6].rearrange("p (z r) -> p r z", z=2)
                v(V.tensor_tensor(dst, b, bc(w, 3, HD), ALU.mult), free(n))
            for t in range(T):
                for d in range(2):
                    n = ("mint", t, d)
                    b = full(dve, n, 2).rearrange("p (z n) -> p z n", z=2)[:, :, 0:130].rearrange("p z (r n) -> p z r n", r=2)
                    dst = ml_n[:, t, d, :, :].rearrange("p (r z) n -> p z r n", z=2)
                    w = ml_e[:, 0, t, d * 4:d * 4 + 4].rearrange("p (r z) -> p z r", z=2)
                    v(V.tensor_tensor(dst, b, bc(w, 3, HD + 1), ALU.mult), free(n))
                    n = ("mia", t, d)
                    dst = ml_n[:, t, d, :, :].rearrange("p h n -> p (h n)")
                    v(V.tensor_tensor(dst, dst, full(dve, n)[:, 0:260], ALU.add), free(n))
            n16 = at(arena, 17688, 16, HD + 1)
            v(V.tensor_copy(rc_, n16[:, :, HD]))
            v(V.scalar_tensor_tensor(out=ssum[:, 0:16], in0=rc_, scalar=-1.0, in1=rc_, op0=ALU.mult, op1=ALU.max))
            v(V.tensor_tensor(ssum[:, 0:16], ssum[:, 0:16], at(tiny, 348, 16), ALU.max))
            v(V.reciprocal(ssum[:, 0:16], ssum[:, 0:16]))
            v(V.tensor_tensor(n16[:, :, 0:HD], n16[:, :, 0:HD], bc(ssum[:, 0:16], 2, HD), ALU.mult))

            def head_norm(src, heads, c0, w, gate_, twice):
                dst = y2[:, :, c0:c0 + heads * HD]
                d4 = dst.rearrange("p t (h n) -> p t h n", h=heads)
                for t in range(T):
                    v(V.tensor_tensor(d4[:, t, :, :], src[:, t, 0, :, 0:HD], src[:, t, 1, :, 0:HD], ALU.add))
                sq = src[:, :, 0, :, 0:HD]
                v(V.tensor_tensor(sq, d4, d4, ALU.mult))
                v(V.tensor_reduce(ssq[:, 0:T * heads].rearrange("p (t h) -> p t h", t=T), sq, X, ALU.add))
                v(V.tensor_scalar(rin[:, 0:T * heads], ssq[:, 0:T * heads], 1.0 / HD, EPS, ALU.mult, ALU.add), "rs_in")
                rsqrt()
                r = rout[:, 0:T * heads].rearrange("p (t h) -> p t h", t=T)
                v(V.tensor_tensor(d4, d4, bc(r, 3, HD), ALU.mult))
                v(V.tensor_tensor(dst, dst, bc(w, 1, T), ALU.mult))
                if twice:
                    v(V.scalar_tensor_tensor(out=gate_, in0=gate_, scalar=1.0, in1=dst, op0=ALU.add, op1=ALU.mult))
                else:
                    v(V.tensor_tensor(gate_, gate_, dst, ALU.mult))
                v(V.tensor_scalar(dst, gate_, 0.5, None, ALU.mult), "mixed_ready" if not twice else "dve")

            head_norm(ml_n, MLH, 640 - 256, ml_w, ot, True)
            v(V.memset(ssq[:, 31:32], 0.0), "ml_done")

            v(V.tensor_copy(gd_e[:, 0, :, :], gd_c))
            v(V.tensor_tensor(gd_e[:, 1, :, :], gd_cl, gd_c, ALU.subtract))
            v(V.tensor_copy(gd_e[:, 2, :, :], gd_cl), "gdarg_ready")
            dve.wait_ge(ev("gdsq_ready"), 1)
            sq = at(arena, 0, 24, HD)
            v(V.tensor_reduce(ssq[:, 0:24], sq, X, ALU.add))
            v(V.tensor_scalar(rin[:, 0:24], ssq[:, 0:24], 4 * EPS, None, ALU.add), "rs_in")
            rsqrt()
            qr = rout[:, 0:24].rearrange("p (t q h) -> p t q h", t=T, q=2)[:, :, 0, :]
            v(V.tensor_scalar(qr, qr, HD ** -0.5, None, ALU.mult))
            g4 = gd[:, :, 0:768].rearrange("p t (h n) -> p t h n", h=12)
            v(V.tensor_tensor(g4, g4, bc(rout[:, 0:24].rearrange("p (t h) -> p t h", t=T), 3, HD), ALU.mult), "gdqk_ready")
            dve.wait_ge(ev("gde_ready"), 1)
            k4 = gd[:, :, 384:768].rearrange("p t (h n) -> p t h n", h=GNH)
            for d in range(2):
                v(V.tensor_tensor(gd_kb[:, :, d, :, :], k4, bc(beta[:, :, d * 6:d * 6 + 6], 3, HD), ALU.mult),
                  "gdkb_ready" if d else "dve")
            for d in range(2):
                v(V.tensor_tensor(gd_kbe[:, :, d, :, :], gd_kb[:, :, d, :, :], bc(gd_e[:, 0, :, d * 6:d * 6 + 6], 3, HD), ALU.mult))
                v(V.tensor_tensor(gd_ks[:, :, d, :, :], k4, bc(gd_e[:, 1, :, d * 6:d * 6 + 6], 3, HD), ALU.mult))
                for t in range(T):
                    v(V.scalar_tensor_tensor(out=gd_vb[:, t, d, :, :], in0=gd[:, t, 768:1152].rearrange("p (h n) -> p h n", h=GNH),
                                             scalar=0.5, in1=bc(beta[:, t, d * 6:d * 6 + 6], 2, HD), op0=ALU.mult, op1=ALU.mult))
            for t in range(T):
                for d in range(2):
                    for z in range(2):
                        n = ("gl", t, d, z)
                        b = full(dve, n)[:, 0:384].rearrange("p (r n) -> p r n", r=3)
                        c = gd_c[:, t, d * 6 + z:d * 6 + 6:2]
                        v(V.tensor_tensor(gd_att[:, t, d, 3 * z:3 * z + 3, :], b, bc(c, 2, P), ALU.subtract), free(n))
                flat = gd_att[:, t, :, :, :].rearrange("p d h n -> p (d h n)")
                v(V.tensor_scalar(flat, flat, 0.0, None, ALU.min), "gdd_ready")
            for t in range(T):
                dve.wait_ge(ev("gdx_ready"), t + 1)
                for d in range(2):
                    v(V.tensor_tensor(gd_a[:, t, d, :, :], gd_att[:, t, d, :, :], bc(nstrict[:, d, :], 1, GNH), ALU.mult))
                    v(V.tensor_tensor(gd_att[:, t, d, :, :], gd_att[:, t, d, :, :], bc(causal[:, d, :], 1, GNH), ALU.mult))
            for t in range(T):
                for d in range(2):
                    for z in range(2):
                        n = ("kk", t, d, z)
                        b = full(dve, n)[:, 0:384].rearrange("p (r n) -> p r n", r=3)
                        a3 = gd_a[:, t, d, 3 * z:3 * z + 3, :]
                        v(V.tensor_tensor(a3, a3, b, ALU.mult), free(n))
            for t in range(T):
                for z in range(2):
                    n = ("kq", t, z)
                    b = full(dve, n)[:, 0:384].rearrange("p (r n) -> p r n", r=3)
                    for d in range(2):
                        a3 = gd_att[:, t, d, 3 * z:3 * z + 3, :]
                        v(V.tensor_tensor(a3, a3, b, ALU.mult), free(n) if d else "dve")
            for t in range(T):
                for d in range(2):
                    inv = gd_inv[1][:, t, d, :, :]
                    v(V.tensor_copy(inv, bc(ident[:, :], 1, GNH)))
                    v(V.copy_predicated(inv, bc(level[:, d, 0, :], 1, GNH), gd_a[:, t, d, :, :]),
                      "inv0_ready" if (t, d) == (1, 1) else "dve")
            GROUPS = [(t, d, z) for t in range(T) for d in range(2) for z in range(2)]
            for k in range(1, 6):
                for g in GROUPS:
                    t, d, z = g
                    for kind, which, side in (("ty", 0, 1 - d), ("tz", 1, d))[k == 5:]:
                        n = (kind, k, *g)
                        b = full(dve, n)[:, 0:384].rearrange("p (r n) -> p r n", r=3)
                        v(V.copy_predicated(gd_inv[which][:, t, d, 3 * z:3 * z + 3, :], bc(level[:, side, k, :], 1, 3), b), free(n))
            copied(dve, *[(n, t, d) for n in ("gu2", "gw") for t in range(T) for d in range(2)], "gdec2")
            v(V.memset(gd_st[:, 0, :, :, :], 0.0))
            for j in range(4):
                for d in range(2):
                    n = j if d == 0 else 3 - j
                    t, r = n // 2, CH * (n % 2)
                    dst, u = gd_vn[r:r + CH, t, d, :, :], gd_u[r:r + CH, t, d, :, :]
                    if j:
                        name = ("ws", j, d)
                        b = full(dve, name, 2).rearrange("p (z n) -> p z n", z=2)[r:r + CH, :, 0:192]
                        b = b.rearrange("p z (r n) -> p z r n", r=3)
                        by = "p (r z) n -> p z r n"
                        v(V.tensor_tensor(dst.rearrange(by, z=2), u.rearrange(by, z=2), b, ALU.subtract), free(name))
                    else:
                        v(V.tensor_copy(dst, u), "vn0_ready")
                for d in range(2):
                    n = j if d == 0 else 3 - j
                    if j < 3:
                        name = ("kv", j, d)
                        b = full(dve, name)[:, 0:192].rearrange("p (r n) -> p r n", r=3)
                        new = gd_st[:, j + 1, d, :, :]
                        if j:
                            v(V.tensor_tensor(new, gd_st[:, j, d, :, :], bc(gd_dec[:, n, d, :], 2, HD), ALU.mult))
                            v(V.tensor_tensor(new, new, b, ALU.add), free(name))
                        else:
                            v(V.tensor_copy(new, b), free(name))
            for t in range(T):
                for d in range(2):
                    n = ("oi", t, d)
                    b = full(dve, n, 2).rearrange("p (z n) -> p z n", z=2)[:, :, 0:192].rearrange("p z (r n) -> p z r n", r=3)
                    dst = gd_o[:, t, d, :, :].rearrange("p (r z) n -> p z r n", z=2)
                    w = gd_e[:, 0, t, d * 6:d * 6 + 6].rearrange("p (r z) -> p z r", z=2)
                    v(V.tensor_tensor(dst, b, bc(w, 3, HD), ALU.mult), free(n))
                    n = ("oa", t, d)
                    dst = gd_o[:, t, d, :, :].rearrange("p h n -> p (h n)")
                    v(V.tensor_tensor(dst, dst, full(dve, n)[:, 0:384], ALU.add), free(n))
            head_norm(gd_o, GNH, 640, gd_w, z2, False)

            copied(dve, *[("yT2", t, h) for t in range(T) for h in range(2)])
            normalise(3, mem)
            add_x(("wo2",))
            turned(3, R_MEM, memT)
            normalise(4)
            turned(4, R_XA, hT)
            for t in range(T):
                for g in range(2):
                    n = ("xs", t, g)
                    b = full(dve, n).rearrange("p (h n) -> p h n", h=2)
                    v(V.tensor_reduce(smax[:, 0:2], b, X, ALU.max))
                    v(V.tensor_tensor(x_s[:, t, 2 * g:2 * g + 2, :], b, bc(smax[:, 0:2], 2, S), ALU.subtract), free(n))
            for t in range(T):
                dve.wait_ge(ev("xe_ready"), t + 1)
                v(V.tensor_reduce(ssum[:, 0:XH], x_s[:, t, :, :], X, ALU.add))
                v(V.reciprocal(ssum[:, 0:XH], ssum[:, 0:XH]))
                v(V.tensor_tensor(x_s[:, t, :, :], x_s[:, t, :, :], bc(ssum[:, 0:XH], 2, S), ALU.mult), "xp_ready")
            add_x(("wxo",))
            normalise(5)
            turned(5, R_FFN, hT)
            for i in range(16):
                copied(dve, ("f1", i // 2, i % 2))
                hh = h1T[:, 2 * i:2 * i + 2, :]
                v(V.tensor_tensor(hh, hh, hh, ALU.mult), "h1_ready")
            add_x(("f2",))
            normalise(6)
            dve.wait_ge(ev("tail_in"), 32)
            for t in range(T):
                o = xn[:, t * D:(t + 1) * D]
                v(V.tensor_tensor(o, o, out_g, ALU.mult), "out_ready")

        @block.scalar
        def _(act):
            AC = nc.scalar.activation

            def a(ins, name="act"):
                done(act, ins, name)

            def quad(tag):
                return [(*tag, t, h) for t in range(T) for h in range(2)]

            def squares(src=None):
                src = x if src is None else src
                for t in range(T):
                    a(AC(tmp[:, 0:D], src[:, t, :], ACT.Square, accum_out=ssq[:, t:t + 1]), "ssq_ready")

            def copy_out(name, dst, n, shape=None, scale=1.0, func=ACT.Copy, rows_=P, banks=1):
                b = full(act, name, banks)[0:rows_, 0:n]
                if shape:
                    b = b.rearrange("p (a b) -> p a b", a=shape)
                a(AC(dst, b, func, scale=scale), free(name))

            for l in range(DEPTH):
                def p1(i):
                    c0, n, parts = SLOTS1[i]
                    n //= parts
                    for t in range(T):
                        for q in range(parts):
                            copy_out(("p1", l, i, t, q), proj[:, t, c0 + q * n:c0 + (q + 1) * n], n)

                def gates(i):
                    for t in range(T):
                        copy_out(("gate", l, i, t, 0), gate[:, t, i * BANK:(i + 1) * BANK], BANK, scale=0.5, func=ACT.Tanh)

                if l == 0:
                    act.wait_ge(ev("x_in"), 16 * T)
                else:
                    copied(act, *quad(("wo", l - 1)))
                squares()
                p1(0)
                for t in range(T):
                    a(AC(tmp[:, 0:256], proj[:, t, COL_CQ:COL_CQ + 256], ACT.Square, accum_out=ssq[:, 4 + t:5 + t]))
                for t in range(T):
                    a(AC(tmp[:, 0:128], proj[:, t, COL_CKV:COL_CKV + 128], ACT.Square, accum_out=ssq[:, 6 + t:7 + t]),
                      "cssq_ready" if t else "act")
                if l == 0:
                    act.wait_ge(ev("angle_ready"), 1)
                    a(AC(trig[:, 1, :, :], ang, ACT.Sin))
                    a(AC(trig[:, 0, :, :], at(arena, 64, T, HALF), ACT.Sin), "trig_ready")
                p1(1)
                p1(2)
                for t in range(T):
                    for h in range(2):
                        copy_out(("uq", l, t, h), qk[:, t, 4 * h:4 * h + 4, :], 384, shape=4)
                        n = ("ukv", l, t, h)
                        b = full(act, n).rearrange("p (h n) -> p h n", h=4)
                        a(AC(qk[:, t, MH + 4 * h:MH + 4 * h + 4, 0:NOPE], b[:, :, 0:NOPE], ACT.Copy))
                        a(AC(mv[:, t, h * 256:(h + 1) * 256].rearrange("p (h n) -> p h n", h=4), b[:, :, NOPE:2 * NOPE], ACT.Copy),
                          free(n))
                act.wait_ge(ev("kr_ready"), l + 1)
                a(AC(at(arena, RC, 32, MQK), at(arena, RA, 32, MQK), ACT.Square), "qsq_ready")
                p1(3)
                p1(4)
                act.wait_ge(ev("qk_ready"), l + 1)
                a(AC(at(tmp, 0, T, 1024), proj[:, :, 0:1024], ACT.Square), "uvsq_ready")
                p1(5)
                act.wait_ge(ev("uvarg_ready"), l + 1)
                a(AC(tmp[:, 0:2048], tmp[:, 0:2048], ACT.Tanh, scale=GELU_C))
                a(AC(at(tmp, 2048, T, 512), proj[:, :, COL_Z:COL_Z + 512], ACT.Tanh, scale=0.5), "uvtanh_ready")
                for t in range(T):
                    for g in range(4):
                        copy_out(("qkT", l, t, g), qkT[0:MQK, 4 * g:4 * g + 4, t * P:(t + 1) * P], BANK, shape=4, rows_=MQK)
                p1(6)
                p1(7)
                for j in range(3):
                    copy_out(("sc", l, j), sc[:, j, :], 1024, scale=MQK ** -0.5, banks=2)
                copy_out(("glrT", l), glrT[0:GRANK, :], S, rows_=GRANK)
                for j in range(3):
                    act.wait_ge(ev("s_ready"), 3 * l + j + 1)
                    a(AC(sc[:, j, :], sc[:, j, :], ACT.Exp), "p_ready")
                gates(0)
                b = full(act, ("gg", l))
                flat = xn[:, 1536:2048]
                a(AC(flat, b, ACT.Abs))
                a(AC(flat, flat, ACT.Exp, scale=-1.0))
                a(AC(flat, flat, ACT.Ln, bias=1.0), "gln_ready")
                for j in range(3):
                    for q in range(2):
                        copy_out(("pT", l, j, q), pT[:, j, 4 * q:4 * q + 4, :], BANK, shape=4)
                gates(1)
                act.wait_ge(ev("tmp_free"), l + 1)
                a(AC(at(tmp, 1024, T, 512), proj[:, :, COL_ZB:COL_ZB + 512], ACT.Tanh, scale=0.5))
                a(AC(at(tmp, 2048, T, 512), proj[:, :, COL_ZC:COL_ZC + 512], ACT.Tanh, scale=0.5), "zb_ready")
                copy_out(("gb", l), flat, BANK)
                a(AC(gl_e, gl_b, ACT.Exp, scale=1.0 / GTAU))
                a(AC(gl_e2, gl_b, ACT.Exp, scale=-1.0 / GTAU), "ge_ready")
                b = full(act, ("gdec", l), 2).rearrange("p (z n) -> p z n", z=2)[:, :, 0:2]
                a(AC(gdec[:, :].rearrange("p (z n) -> p z n", z=2), b, ACT.Exp, scale=1.0 / GTAU), free(("gdec", l)))
                copied(act, ("gbl", l))
                a(AC(gl_b, gl_b, ACT.Exp, scale=1.0 / GTAU), "gks_ready")
                gates(2)
                for t in range(T):
                    copy_out(("gqkT", l, t), gl_qkT[:, :, t * P:(t + 1) * P], BANK, shape=4)
                gates(3)
                gates(4)
                gates(5)
                for i, c in enumerate((0.5, 0.25, 0.5)):
                    for t in range(T):
                        copy_out(("yT", l, i, t), yT[:, i, :, t * P:(t + 1) * P], BANK, shape=4, scale=c)
                for t in range(T):
                    for h in range(2):
                        copy_out(("mT", l, t, h), hT[:, 4 * h:4 * h + 4, t * P:(t + 1) * P], BANK, shape=4, scale=0.5)

            def p2(i):
                _, n, c = SLOTS2T[i]
                for t in range(T):
                    copy_out(("p2", i, t, 0), proj2[:, t, c:c + n], n)

            copied(act, *quad(("wo", DEPTH - 1)))
            squares()
            act.wait_ge(ev("conv_done"), 1)
            for q in range(3):
                a(AC(gd_th[:, 3 * q:3 * q + 3, :], conv[:, 3 * q:3 * q + 3, :], ACT.Tanh, scale=0.5), "convtanh_ready")
            p2(0)
            p2(1)
            a(AC(beta, proj2[:, :, K_GDB:K_GDB + 12], ACT.Tanh, scale=0.5))
            a(AC(zt, proj2[:, :, K_GDZ:K_GDZ + 384], ACT.Tanh, scale=0.5), "zt_ready")
            act.wait_ge(ev("sp_ready"), 1)
            a(AC(a_log, a_log, ACT.Exp))
            a(AC(spl, sp, ACT.Abs))
            a(AC(spl, spl, ACT.Exp, scale=-1.0))
            a(AC(spl, spl, ACT.Ln, bias=1.0), "spln_ready")
            copy_out("cum", cum, 80)
            p2(2)
            copy_out("mlrow", ml_row[0:MLH, :, :, :].rearrange("p q d n -> p (q d n)"), 1024, rows_=MLH, banks=2)
            p2(3)
            for t in range(T):
                for q in range(2):
                    copy_out(("naT", t, q), na_T[:, 3 * q:3 * q + 3, t * P:(t + 1) * P], 384, shape=3)
            p2(4)
            p2(5)
            a(AC(ot, proj2[:, :, C_MLO:C_MLO + 256], ACT.Tanh, scale=0.5))
            copy_out("mlcol", ml_col[:, :, :, :].rearrange("p q t n -> p (q t n)"), 48)
            for t in range(T):
                n = ("mlT", t)
                b = full(act, n).rearrange("p (k n) -> p k n", k=4)
                a(AC(ml_T[:, 0:2, t * P:(t + 1) * P], b[:, 0:2, :], ACT.Copy))
                a(AC(ml_T[:, 2:4, t * P:(t + 1) * P], b[:, 2:4, :], ACT.Copy, scale=HD ** -0.5), free(n))
            for t in range(T):
                for q in range(3):
                    copy_out(("gT", t, q), gd[:, t, q * 384:(q + 1) * 384], 384)
            for t in range(T):
                act.wait_ge(ev("nas_ready"), t + 1)
                s1 = na_s[:, t, :, :, :].rearrange("p z r n -> p (z r n)")
                a(AC(s1, s1, ACT.Exp), "nap_ready")
            act.wait_ge(ev("mlarg_ready"), 1)
            e1 = ml_e[:, :, :, :].rearrange("p q t n -> p (q t n)")
            a(AC(e1, e1, ACT.Exp), "mle_ready")
            p1_ = ml_p[:, :, :, :, :].rearrange("p t d h n -> p (t d h n)")
            a(AC(p1_, p1_, ACT.Exp), "mlx_ready")
            for t in range(T):
                for q in range(3):
                    i = 12 * t + 4 * q
                    copy_out(("napT", t, q), na_pT[:, i:i + 4, :], BANK, shape=4)
            copy_out("mldec", ml_dec[:, :, :, :].rearrange("p a b c -> p (a b c)"), 16)
            act.wait_ge(ev("ml_done"), 1)
            a(AC(at(arena, 0, T, 12 * HD), gd[:, :, 0:768], ACT.Square), "gdsq_ready")
            act.wait_ge(ev("gdarg_ready"), 1)
            e1 = gd_e[:, :, :, :].rearrange("p q t n -> p (q t n)")
            a(AC(e1, e1, ACT.Exp), "gde_ready")
            for t in range(T):
                for q in range(2):
                    copy_out(("gqT", t, q), gd_T[:, 3 * q:3 * q + 3, t * P:(t + 1) * P], 384, shape=3)
            for t in range(T):
                for d in range(2):
                    copy_out(("gkT", t, d), gd_kbT[:, t, d, :, :], 384, shape=3)
            for t in range(T):
                act.wait_ge(ev("gdd_ready"), t + 1)
                e1 = gd_att[:, t, :, :, :].rearrange("p d h n -> p (d h n)")
                a(AC(e1, e1, ACT.Exp), "gdx_ready")
            GROUPS = [(t, d, z) for t in range(T) for d in range(2) for z in range(2)]
            for t, d, z in GROUPS:
                copy_out(("inv0", t, d, z), gd_inv[0][:, t, d, 3 * z:3 * z + 3, :], 384, shape=3)
            for k in range(1, 6):
                for n, g in enumerate(GROUPS):
                    copy_out(("tx", k, *g), gd_x[:, n % 4, :, :], 384, shape=3)
            copy_out("gdec2", stat_all[:, :], 24)
            for t in range(T):
                for d in range(2):
                    copy_out(("gu2", t, d), gd_u[:, t, d, :, :], 384, shape=6)
                    copy_out(("gw", t, d), gd_wk[:, t, d, :, :], 384, shape=3)
            act.wait_ge(ev("mixed_ready"), 1)
            act.wait_ge(ev("tail_in"), 32)
            squares(mem)
            for t in range(T):
                for h in range(2):
                    copy_out(("yT2", t, h), hT[:, 4 * h:4 * h + 4, t * P:(t + 1) * P], BANK, shape=4)
            copied(act, *quad(("wo2",)))
            squares()
            for i in range(2):
                for g in range(2):
                    copy_out(("xk", i, g), xk_T[:, 4 * i + 2 * g:4 * i + 2 * g + 2, :], BANK, shape=2)
            for i in range(2):
                for t in range(T):
                    copy_out(("xv", i, t, 0), x_v[:, t, i * BANK:(i + 1) * BANK], BANK)
            for i in range(2):
                for g in range(2):
                    copy_out(("xq", i, g), xq_T[:, 4 * i + 2 * g:4 * i + 2 * g + 2, :], BANK, shape=2)
            for t in range(T):
                copied(act, ("xs", t, 0), ("xs", t, 1))
                s1 = x_s[:, t, :, :].rearrange("p h n -> p (h n)")
                a(AC(s1, s1, ACT.Exp, scale=XD ** -0.5), "xe_ready")
            for t in range(T):
                for g in range(2):
                    n = ("xpT", t, g)
                    b = full(act, n).rearrange("p (m h n) -> p m h n", m=2, h=2)
                    a(AC(x_pT[:, :, 2 * g:2 * g + 2, t * P:(t + 1) * P], b, ACT.Copy), free(n))
            for h in range(XH):
                copy_out(("xo", h), x_oT[:, 2 * h:2 * h + 2, :], BANK, shape=2)
            copied(act, *quad(("wxo",)))
            squares()
            for i in range(8):
                for g in range(2):
                    k = 4 * i + 2 * g
                    n = ("f1", i, g)
                    b = full(act, n).rearrange("p (a b) -> p a b", a=2)
                    a(AC(h1T[:, k:k + 2, :], b, ACT.Relu), free(n))
            copied(act, *quad(("f2",)))
            squares()

        @block.gpsimd
        def _(pool):
            G = nc.gpsimd

            def g(ins, name="pool"):
                done(pool, ins, name)

            def across(ap, n):
                return bass.AP(tensor=ap.tensor, offset=ap.offset, ap=[[0, P], [1, n]])

            def powers(n):
                for _ in range(n):
                    k = made.get("rs_out", 0)
                    pool.wait_ge(ev("rs_in"), k + 1)
                    g(G.tensor_tensor(rout[:, :], rin[:, :], mhalf[:, :], ALU.pow), "rs_out")

            pool.dma_start(posi[:, :], A["positions"].rearrange("a (t p) -> p (a t)", p=P),
                           allow_slow_non_contiguous=True).then_inc(ev("pos_in"), 16)
            g(G.memset(ones[:, :], 1.0))
            g(G.memset(ident[:, :], 0.0))
            g(G.affine_select(out=ident[:, :], in_=ident[:, :], compare_op=ALU.not_equal, fill=1.0, base=0,
                              pattern=[[-1, P]], channel_multiplier=1))
            g(G.memset(mhalf[:, :], -0.5))
            g(G.memset(rin[:, :], 1.0))
            for i in range(HALF):
                f = np.float32(1.0) / np.power(np.float32(THETA), np.float32(i) * np.float32(2.0) / np.float32(ROPE))
                g(G.memset(freq[:, i:i + 1], float(np.float32(f))), "const_ready" if i == HALF - 1 else "pool")
            def masks():
                g(G.memset(blk[:, :], 0.0))
                for r in (0, CH):
                    g(G.memset(blk[r:r + CH, r:r + CH], 1.0))
                g(G.affine_select(out=causal[:, 0, :], in_=blk[:, :], compare_op=ALU.is_ge, fill=0.0, base=0,
                                  pattern=[[1, P]], channel_multiplier=-1))
                g(G.affine_select(out=causal[:, 1, :], in_=blk[:, :], compare_op=ALU.is_ge, fill=0.0, base=0,
                                  pattern=[[-1, P]], channel_multiplier=1))
                g(G.memset(sel[:, :, :], 0.0))
                g(G.affine_select(out=sel[:, :, :], in_=sel[:, :, :], compare_op=ALU.not_equal, fill=1.0, base=0,
                                  pattern=[[-1, 6], [0, P]], channel_multiplier=1))
                g(G.memset(level[:, :, :, :], 0))
                for k in range(6):
                    w = 2 ** k
                    for side in range(2):
                        m = level[:, side, k, :].rearrange("p (b w) -> p b w", w=2 * w)
                        m = m[:, :, w:2 * w] if side == 0 else m[:, :, 0:w]
                        g(G.memset(m, 1))
                        low = side * w
                        g(G.affine_select(out=m, in_=m, compare_op=ALU.is_ge, fill=0.0, base=-low, pattern=[[-2 * w, P // (2 * w)], [0, w]],
                                          channel_multiplier=1))
                        g(G.affine_select(out=m, in_=m, compare_op=ALU.is_ge, fill=0.0, base=low + w - 1,
                                          pattern=[[2 * w, P // (2 * w)], [0, w]], channel_multiplier=-1),
                          "const_ready" if (k, side) == (5, 1) else "pool")

            for l in range(DEPTH):
                powers(1)
                if l:
                    copied(pool, *[("wo", l - 1, t, h) for t in range(T) for h in range(2)])
                for dst, src in ((sgw, A["sg_w"][l].rearrange("g i j -> i g j")),
                                 (ln_g, across(A["sg_ln_g"][l], 512)),
                                 (ln_b, across(A["sg_ln_b"][l], 512)),
                                 (wuq, A["mla_w_uq"][l].rearrange("(k p) n -> p k n", p=P)),
                                 (wukv, A["mla_w_ukv"][l]),
                                 (qk_g[:, 0, :], across(A["mla_q_g"][l], MQK)),
                                 (qk_g[:, 1, :], across(A["mla_k_g"][l], MQK)),
                                 (o_g, across(A["gla_o_g"][l], GDV)),
                                 (wgu[0:GRANK, :], A["gla_w_gate"][l]),
                                 (bgu[0:1, :], A["gla_b_gate"][l:l + 1, :]),
                                 (bgate[0:6, :], A["b_gate"][l].rearrange("(a n) -> a n", n=BANK))):
                    pool.dma_start(dst, src).then_inc(ev("layer_in"), 16)
                powers(1)
                if l == 0:
                    masks()
                powers(3)

            powers(1)
            copied(pool, *[("wo", DEPTH - 1, t, h) for t in range(T) for h in range(2)])
            bias = A["na_rel_bias_2"]
            rows_n, cols_n = bias.shape[2], bias.shape[3]
            for t in range(T):
                for rl in range(2):
                    for h in range(NH):
                        off = h * rows_n * cols_n + (7 - 2 * t - rl) * cols_n + 15 - 63
                        src = bass.AP(tensor=bias.tensor, offset=bias.offset + off, ap=[[1, 64], [cols_n, 4], [1, GW]])
                        dst = na_raw[64 * rl:64 * rl + 64, t, h, :].rearrange("p (a b) -> p a b", a=4)
                        pool.dma_start(dst, src).then_inc(ev("second_in"), 16)
            for dst, src in ((ml_w, across(A["ml_norm_w_2"][0], 256)), (gd_w, across(A["gdn_norm_w_2"][0], 384)),
                             (if_b[:, 0:8], across(A["ml_i_bias_2"][0], 8)), (if_b[:, 8:16], across(A["ml_f_bias_2"][0], 8)),
                             (dt_b, across(A["gdn_dt_bias_2"][0], 12)), (a_log, across(A["gdn_a_log_2"][0], 12))):
                pool.dma_start(dst, src).then_inc(ev("second_in"), 16)
            g(G.memset(mirror, 0.0))
            for r in range(2):
                m64 = mirror[:, 64 * r:64 * r + 64]
                g(G.affine_select(out=m64, in_=m64, compare_op=ALU.not_equal, fill=1.0, base=-63 - 64 * r,
                                  pattern=[[1, 64]], channel_multiplier=1))
            g(G.memset(na_mask, 0.0))
            for r in range(2):
                lo, hi = na_mask[64 * r:64 * r + 64, 0:48], na_mask[64 * r:64 * r + 64, 16:64]
                g(G.affine_select(out=lo, in_=lo, compare_op=ALU.is_ge, fill=NEG, base=8, pattern=[[1, 48]], channel_multiplier=-1))
                g(G.affine_select(out=hi, in_=hi, compare_op=ALU.is_ge, fill=NEG, base=7 - 16, pattern=[[-1, 48]],
                                  channel_multiplier=1))
            for d in range(2):
                g(G.tensor_tensor(nstrict[:, d, :], ident[:, :], causal[:, d, :], ALU.subtract))
            g(G.memset(first[:, :, :], 0.0))
            for r in range(2):
                g(G.memset(first[64 * r:64 * r + 1, r, :], 1.0), "second_const" if r else "pool")
            powers(3)
            pool.wait_ge(ev("mixed_ready"), 1)
            pool.dma_start(mem[:, :, :], A["mem_2"][0].rearrange("(t p) d -> p t d", p=P)).then_inc(ev("tail_in"), 16)
            pool.dma_start(out_g, across(A["norm_out_w_2"], D)).then_inc(ev("tail_in"), 16)
            powers(4)

        @block.sync
        def _(sp_):
            for t in range(T):
                sp_.dma_start(x[:, t, :], A["x"][0, t * P:(t + 1) * P, :]).then_inc(ev("x_in"), 16)
            for r0, src in ((R_NORM, A["norm_g"].rearrange("l (k p) -> (l k) p", p=P)),
                            (R_MIX, A["norm_mix_w_2"].rearrange("l (k p) -> (l k) p", p=P)),
                            (R_XA, A["norm_xa_w_2"].rearrange("l (k p) -> (l k) p", p=P)),
                            (R_MEM, A["norm_mem_w_2"].rearrange("l (k p) -> (l k) p", p=P)),
                            (R_FFN, A["norm_ffn_w_2"].rearrange("l (k p) -> (l k) p", p=P)),
                            (R_CQ, A["mla_cq_g"].rearrange("l (k p) -> (l k) p", p=P)),
                            (R_CKV, A["mla_ckv_g"]),
                            (R_SGB, A["sg_b"].rearrange("l g p -> (l g) p")),
                            (R_CONV, A["gdn_conv_w_2"][0].rearrange("k (j p) -> (k j) p", p=P))):
                sp_.dma_start(rows[r0:r0 + src.shape[0], :], src).then_inc(ev("rows_in"), 16)
            for k, (src, kd, n) in enumerate(slots):
                if k >= RING:
                    sem, value = release[k - RING]
                    sp_.wait_ge(sem, value)
                dst = ring[:, k % RING, 0:kd * n].rearrange("p (k n) -> p k n", n=n)
                sp_.dma_start(dst, src).then_inc(ev(f"ring_full{k % RING}"), 16)
            for t in range(T):
                sp_.wait_ge(ev("out_ready"), t + 1)
                sp_.dma_start(out[0, t * P:(t + 1) * P, :], xn[:, t * D:(t + 1) * D]).then_inc(ev("stored"), 16)
            sp_.wait_ge(ev("stored"), 16 * T)


_INS = ['x', 'positions', 'norm_g', 'w_in', 'b_gate', 'sg_ln_g', 'sg_ln_b', 'sg_w', 'sg_b', 'mla_cq_g', 'mla_ckv_g',
        'mla_w_uq', 'mla_w_ukv', 'mla_q_g', 'mla_k_g', 'gla_w_gate', 'gla_b_gate', 'gla_o_g', 'w_branch', 'w_out',
        'mem_2', 'norm_mix_w_2', 'w_in_2', 'na_rel_bias_2', 'ml_i_bias_2', 'ml_f_bias_2', 'ml_norm_w_2',
        'gdn_conv_w_2', 'gdn_a_log_2', 'gdn_dt_bias_2', 'gdn_norm_w_2', 'w_out_2', 'norm_xa_w_2', 'norm_mem_w_2',
        'w_xq_2', 'w_xkv_2', 'w_xo_2', 'norm_ffn_w_2', 'w_ff1_2', 'w_ff2_2', 'norm_out_w_2']


def kernel(**inputs):
    import numpy as _np
    import concourse.bacc as _bacc
    from concourse import mybir as _mybir
    from concourse.bass_utils import run_bass_kernel_spmd as _run

    nc = _bacc.Bacc("TRN2", target_bir_lowering=False, num_devices=1)
    arrays, args = {}, {}
    for name in _INS:
        a = _np.ascontiguousarray(inputs[name])
        arrays[f"in_{name}"] = a
        args[name] = nc.dram_tensor(f"in_{name}", a.shape, _mybir.dt.from_np(a.dtype), kind="ExternalInput").ap()
    out = nc.dram_tensor("out_0", (1, S, D), F32, kind="ExternalOutput").ap()
    build(nc, args, out)
    r = _run(nc, [arrays], core_ids=[0])
    return r.results[0]["out_0"]
```

```python
from contextlib import ExitStack

import numpy as np
import concourse.bass as bass
from concourse import mybir
from concourse.alu_op_type import AluOpType as ALU

F32 = mybir.dt.float32
F32R = mybir.dt.float32r
I32 = mybir.dt.int32
I8 = mybir.dt.int8
ACT = mybir.ActivationFunctionType
X = mybir.AxisListType.X

P = 128
S = 256
T = S // P
D = 1024
KD = D // P
BANK = 512
EPS = 1e-6
NEG = -1e30
RSQRT_GUESS = 0x5F3759DF
DEPTH = 2
ARENA_W = 23488
CH = 64

COL_U, COL_V, COL_Z = 0, 512, 1024
COL_CQ, COL_CKV, COL_KR, COL_ZB = 1536, 1792, 1920, 1952
COL_QC, COL_KC, COL_VC, COL_GC, COL_ZC, COL_GATE = 2464, 2720, 2976, 3488, 3504, 4016
MH, MQK, NOPE, ROPE = 8, 96, 64, 32
HALF = ROPE // 2
THETA = 10000.0
GH, GDK, GDV, GRANK, GTAU = 4, 64, 128, 16, 16.0
GELU_C = float(np.sqrt(2.0 / np.pi))
SLOTS1 = [(COL_CQ, 416, 1), (COL_ZB, 512, 1), (COL_U, 512, 1), (COL_V, 512, 1), (COL_Z, 512, 1),
          (COL_QC, 512, 1), (COL_GC, 528, 2), (COL_VC, 512, 1)]
NGATE = 6
LOW_ROWS = 32
BRANCHES = (1, 0, 2)
BRANCH_SCALE = (0.5, 0.25, 0.5)
SC = [(0, 0, 8), (1, 0, 4), (1, 4, 4)]
TWO_PI = 2.0 * np.pi
PI_A = 6.28125
PI_B = float(np.float32(np.round((TWO_PI - PI_A) * 2.0 ** 22) / 2.0 ** 22))
PI_C = float(np.float32(TWO_PI - PI_A - PI_B))
ROUND = float(1.5 * 2 ** 23)

NH, HD, GW = 6, 64, 64
MLH = 4
GNH = 6
TAPS = 5
C_MLQ, C_MLK, C_MLV, C_MLO, C_MLI, C_MLF = 1152, 1408, 1664, 1920, 2176, 2184
C_GDQ, C_GDZ = 2192, 3344
SHIFT = C_GDZ - C_GDQ
K_GDZ, K_GDB, K_GDA = C_GDQ, C_GDQ + 384, C_GDQ + 396
SLOTS2 = [(C_GDQ, 512), (C_GDQ + 512, 512), (C_GDQ + 1024, 128)]
SLOTS2T = [(2048, 144, 2048), (C_GDZ, 408, K_GDZ), (0, 512, 0), (512, 512, 512), (1024, 512, 1024), (1536, 512, 1536)]
XH, XD = 4, 256
FF = 4096
CHUNKS = 4
CHUNK_W = KD // CHUNKS * 528
RAW, RING_HI, RING_LO = 3, 4, 3

LAYER_CHUNKS = CHUNKS * (len(SLOTS1) + NGATE + 3 + 2)
SPLITS1 = 2 * 3 + 4

R_NORM, R_MIX, R_XA, R_MEM, R_FFN, R_CQ, R_CKV, R_SGB, R_CONV, R_END = 0, 16, 24, 32, 40, 48, 52, 54, 62, 107


def bc(ap, pos, n):
    dims = [list(d) for d in ap.ap]
    dims.insert(pos, [0, n])
    return bass.AP(tensor=ap.tensor, offset=ap.offset, ap=dims)


def build(nc, A, out):
    ctx = ExitStack()
    with ctx:
        def sb(name, shape, dt=F32):
            return ctx.enter_context(nc.sbuf_tensor(name, shape, dt))

        sems = {}
        made = {}

        def ev(name):
            if name not in sems:
                sems[name] = ctx.enter_context(nc.semaphore(name))
            return sems[name]

        def done(eng, ins, name):
            if isinstance(name, tuple):
                sem, value = name
            else:
                made[name] = made.get(name, 0) + 1
                sem, value = ev(name), made[name]
            ins.then_inc(sem, 1)
            eng.wait_ge(sem, value)

        x = sb("x", [P, T, D])
        xn = sb("xn", [P, T * D])
        hT = sb("hT", [P, 2, KD, S], F32R)
        ring = sb("ring", [P, RAW, CHUNK_W])
        ring_hi = sb("ring_hi", [P, RING_HI, CHUNK_W], F32R)
        ring_lo = sb("ring_lo", [P, RING_LO, CHUNK_W], F32R)
        proj_all = sb("proj", [P, T * COL_GATE])
        arena = sb("arena", [P, ARENA_W])
        arena_r = nc.alloc_sbuf_tensor_at("arena_r", [P, ARENA_W], F32R, offset=nc.sbuf_base - 4 * ARENA_W)
        tiny = sb("tiny", [P, 544])
        ident = sb("ident", [P, P])
        blk = sb("blk", [P, P])
        causal = sb("causal", [P, 2, P])
        ones = sb("ones", [P, P])
        sel = sb("sel", [LOW_ROWS + 32, NGATE, P])
        cols = sb("cols", [P, R_END])
        rin = sb("rin", [P, 32])
        rout = sb("rout", [P, 32])
        rtmp = sb("rtmp", [P, 32])
        ssq = sb("ssq", [P, 32])
        posi = sb("posi", [P, T], I32)
        posf = sb("posf", [P, T])
        freq = sb("freq", [P, HALF])
        trig = sb("trig", [P, 2, T, HALF])
        stat_all = sb("stat_all", [P, 24])
        smax = sb("smax", [P, 16])
        ssum = sb("ssum", [P, 16])
        stat = sb("stat", [P, T, 8])
        gdec = sb("gdec", [P, 4])
        level = sb("level", [P, 2, 6, P], I8)
        psum = ctx.enter_context(nc.psum_tensor("psum", [P, 8, BANK], F32))

        def at(where, off, *shape):
            n = int(np.prod(shape))
            ap = where[:, off:off + n]
            if len(shape) == 1:
                return ap
            names = "abcde"[:len(shape)]
            return ap.rearrange("p (%s) -> p %s" % (" ".join(names), " ".join(names)),
                                **dict(zip(names[1:], shape[1:])))

        proj = at(proj_all, 0, T, COL_GATE)
        gate = at(arena, 0, T, 3 * D)
        RA, RB, RC, PB = 6144, 9216, 13312, 17408
        qk = at(arena, RA, T, 2 * MH, MQK)
        sc = at(arena, RA, 3, 1024)
        qkT = at(arena, RB, 2 * MH, S)
        pT = at(arena, RB, 3, MH, P)
        tmp = at(arena, RC, 3072)
        mv = at(arena, RC + 3072, T, MH * NOPE)
        yT = at(arena_r, RB, 2, 2, 4, S)
        sgw = at(arena, PB, 4, P)
        sgwT = at(arena, PB + 512, 4, P)
        ln_g = at(arena, PB + 1024, 512)
        ln_b = at(arena, PB + 1536, 512)
        wuq = at(arena, PB + 2048, 2, MH * MQK)
        wukv = at(arena, PB + 3584, 1024)
        qk_g = at(arena, PB + 4608, 2, MQK)
        o_g = at(arena, PB + 4800, GDV)
        wgu = at(arena, PB + 4928, 256)
        bgu = at(arena, PB + 5184, 256)
        bgate = at(arena, PB + 5440, 512)
        rows = at(arena, PB + 5952, P)
        bias_r = at(arena_r, PB + 2048, BANK)
        sel_r = at(arena_r, PB + 2560, NGATE, P)
        N_LAYER_DMA = 12
        N_ROWS_DMA = 9
        N_SECOND_DMA = 30
        merged = at(arena, RA, T, D)
        normT = at(arena, RC, KD, S)
        flag = sb("flag", [P, 1])
        ang, ang1, ang2 = at(arena, 0, T, HALF), at(arena, 0, T * HALF), at(arena, 64, T * HALF)
        cn = at(xn, 0, T, 384)
        cT = at(xn, 768, 3, S)
        glrT = at(xn, 0, S)
        gl_la = at(xn, 1024, T, 256)
        gl_b = at(xn, 1536, T, 256)
        gl_qk = at(arena, RA, T, 512)
        gl_ks = at(arena, RA + 1024, T, 256)
        gl_e = at(arena, RA + 1536, T, 256)
        gl_st = at(arena, RA + 2048, 3, 2, P)
        gl_e2 = at(xn, 512, T, 256)
        gl_qkT = at(arena, RB, 4, S)
        gl_att = at(arena, RB + 1024, T, 4, P)
        gl_o = at(arena, RC, T, 512)
        gl_sq = at(arena, RC + 1024, T, 512)

        proj2 = at(proj_all, 0, T, 2600)
        gd = at(proj_all, 5200, T, 1152)
        gd_th = at(proj_all, 5200, 9, S)
        nstrict = at(proj_all, 7504, 2, P)
        first = at(proj_all, 7760, 2, 64)
        mirror = at(proj_all, 7888, P)
        conv = at(arena, 20352, 9, S)
        PC = 22656
        ml_w, gd_w = at(arena, PC, 256), at(arena, PC + 256, 384)
        if_b, dt_b, a_log = at(arena, PC + 640, 16), at(arena, PC + 656, 12), at(arena, PC + 668, 12)
        na_s = at(arena, 0, T, 2, 3, S)
        na_pT = at(arena, 3072, 24, P)
        na_T = at(arena, 6144, 6, S)
        na_raw = at(arena, 7680, T, NH, S)
        ml_row = at(arena, 7680, 2, 2, S)
        ml_max = at(arena, 8704, 3, 2, S)
        ml_T = at(arena, 10752, 4, S)
        ml_v = at(arena, 11776, T, MLH, HD + 1)
        ml_k = at(arena, 12296, T, 2, MLH, HD)
        ml_p = at(arena, 13320, T, 2, MLH, P)
        zt = at(arena, 15368, T, 384)
        ot = at(arena, 16136, T, 256)
        ml_c = at(arena, 16648, 2, 4, 2, HD + 1)
        ml_n = at(arena, 17688, T, 2, MLH, HD + 1)
        gd_kb = at(arena, 0, T, 2, GNH, HD)
        gd_kbe = at(arena, 1536, T, 2, GNH, HD)
        gd_ks = at(arena, 3072, T, 2, GNH, HD)
        gd_vb = at(arena, 4608, T, 2, GNH, HD)
        gd_T = at(arena, 6144, 6, S)
        gd_kbT = at(arena, 7680, T, 2, 3, P)
        gd_x = at(arena, 7680, 4, 3, P)
        gd_a = at(arena, 9216, T, 2, GNH, P)
        gd_att = at(arena, 12288, T, 2, GNH, P)
        gd_inv = [at(arena, 19584, T, 2, GNH, P), at(arena, 16512, T, 2, GNH, P)]
        gd_u = at(arena, 0, T, 2, GNH, HD)
        gd_wk = at(arena, 19584, T, 2, 3, P)
        gd_vn = at(arena, 21120, T, 2, GNH, HD)
        gd_st = at(arena, 9216, 4, 2, 3, HD)
        gd_o = at(arena, 10752, T, 2, GNH, HD)
        y2 = at(xn, 0, T, D)
        na_mask = at(tiny, 0, GW)
        ml_if = at(tiny, 64, T, 16)
        sp = at(tiny, 96, T, 20)
        spl = at(tiny, 136, T, 20)
        cum = at(tiny, 176, 80)
        ml_b, ml_bl = at(tiny, 176, T, 8), at(tiny, 192, T, 8)
        gd_c, gd_cl = at(tiny, 208, T, 12), at(tiny, 232, T, 12)
        ml_g = at(tiny, 256, T, 8)
        ml_m = at(tiny, 272, 2, 5)
        ml_col = at(tiny, 284, 3, T, 8)
        ml_e = at(tiny, 332, 4, T, 8)
        ml_dec = at(tiny, 396, 4, 2, 2)
        beta = at(tiny, 412, T, 12)
        gd_g = at(tiny, 436, T, 12)
        gd_e = at(tiny, 460, 3, T, 12)
        rc_ = at(tiny, 256, 16)
        gd_dec = at(stat_all, 0, 4, 2, 3)
        mem = at(xn, 0, T, D)
        mem_normT = at(xn, 0, KD, S)
        xk_T = proj2[:, :, 0:D]
        x_v = proj2[:, :, D:2 * D]
        x_s = at(arena, 10240, T, XH, S)
        x_pT = at(arena, 12288, T, XH, S)
        x_oT = at(arena_r, 14336, 2, KD, S)
        out_g = at(arena, 18432, D)
        xq_T = at(arena, 19456, KD, S)
        h1T = at(arena_r, 0, 2, FF // P, S)
        h1 = at(proj_all, 5200, 4, 2, S)

        bank_full = [ev(f"bank_full{b}") for b in range(8)]
        bank_free = [ev(f"bank_free{b}") for b in range(8)]
        uses = [0] * 8
        last = [None] * 8
        where = {}
        turn = [0]

        def open_bank(pe, name, n=1):
            if turn[0] % 8 + n > 8:
                turn[0] += 8 - turn[0] % 8
            b = turn[0] % 8
            turn[0] += n
            for lead, use in sorted({last[c] for c in range(b, b + n) if last[c]}):
                pe.wait_ge(bank_free[lead], use)
            uses[b] += 1
            for c in range(b, b + n):
                last[c] = (b, uses[b])
            assert name not in where, name
            where[name] = (b, uses[b])
            return bank_view(b, n)

        def bank_view(b, n):
            return psum[:, b, :] if n == 1 else psum[:, b:b + n, :].rearrange("p b n -> p (b n)")

        def filled(ins, name):
            ins.then_inc(bank_full[where[name][0]], 1)

        def full(eng, name, n=1):
            b, u = where[name]
            eng.wait_ge(bank_full[b], u)
            return bank_view(b, n)

        def copied(eng, *names):
            for b in sorted({where[n][0] for n in names}):
                eng.wait_ge(bank_free[b], max(where[n][1] for n in names if where[n][0] == b))

        def free(name):
            return bank_free[where[name][0]], where[name][1]

        def across(ap, n):
            return bass.AP(tensor=ap.tensor, offset=ap.offset, ap=[[0, P], [1, n]])

        chunks = []
        release = []

        def w_cols(w, c0, n):
            rows_ = KD // CHUNKS
            for c in range(CHUNKS):
                chunks.append((w[c * rows_ * P:(c + 1) * rows_ * P, c0:c0 + n].rearrange("(k p) n -> p k n", p=P), rows_, n))

        def w_rows(w, r0):
            for c in range(CHUNKS):
                chunks.append((w[r0 + c * P:r0 + (c + 1) * P, :].rearrange("(k p) n -> p k n", p=P), 1, D))

        def chunk_view(where_, places, c):
            _, k, n = chunks[c]
            return where_[:, c % places, 0:k * n].rearrange("p (k n) -> p k n", n=n)

        def plain(view):
            return view.bitcast(F32)

        for l in range(DEPTH):
            for c0, n, _ in SLOTS1:
                w_cols(A["w_in"][l], c0, n)
            for i in range(NGATE):
                w_cols(A["w_in"][l], COL_GATE + BANK * i, BANK)
            for i in BRANCHES:
                w_rows(A["w_branch"][l, i], 0)
            for i in range(2):
                w_rows(A["w_out"][l], 4 * P * i)
        for c0, n in SLOTS2:
            w_cols(A["w_in_2"][0], c0, n)
        for c0, n, _ in SLOTS2T:
            w_cols(A["w_in_2"][0], c0, n)
        for i in range(4):
            w_cols(A["w_xkv_2"][0], BANK * i, BANK)
        for i in range(2):
            w_rows(A["w_out_2"][0], 4 * P * i)
        for i in range(2):
            w_cols(A["w_xq_2"][0], BANK * i, BANK)
        for i in range(2):
            w_rows(A["w_xo_2"][0], 4 * P * i)
        for i in range(8):
            w_cols(A["w_ff1_2"][0], BANK * i, BANK)
        for i in range(8):
            w_rows(A["w_ff2_2"][0], 4 * P * i)


        block = ctx.enter_context(nc.Block())

        @block.tensor
        def _(pe):
            mm = nc.tensor.matmul
            turn_ = nc.tensor.transpose
            used = [0]

            norm_wait = [0]

            def take_chunk():
                c = used[0]
                used[0] += 1
                if c % CHUNKS == 2 and norm_wait[0]:
                    pe.wait_ge(ev("normT_ready"), norm_wait[0])
                    norm_wait[0] = 0
                pe.wait_ge(ev("wlo_ready"), c + 1)
                return chunk_view(ring_hi, RING_HI, c), chunk_view(ring_lo, RING_LO, c)

            def chunk_used(m):
                m.then_inc(ev("chunk_used"), 1)
                made["chunk_used"] = made.get("chunk_used", 0) + 1
                release.append((ev("chunk_used"), made["chunk_used"]))

            def slot_done(name):
                release.append((bank_full[where[name][0]], where[name][1]))

            def split_mm(b, lhs, rhs, start, stop, **how):
                mm(b, lhs[0], rhs[0], start=start, stop=False, **how)
                mm(b, lhs[0], rhs[1], start=False, stop=False, **how)
                return mm(b, lhs[1], rhs[0], start=False, stop=stop, **how)

            def parts_of(x_, *where_):
                return [x_[(slice(None), z, *where_)] for z in range(2)]

            def norm_T(i, wait=True):
                for h in range(2):
                    for t in range(T):
                        if h == 0:
                            pe.wait_ge(ev("xn_ready"), T * i + t + 1)
                        b = open_bank(pe, ("xT", i, t, h))
                        for k in range(4):
                            c = t * D + (4 * h + k) * P
                            m = turn_(b[:, k * P:(k + 1) * P], xn[:, c:c + P], ident[:, :])
                        filled(m, ("xT", i, t, h))
                if wait:
                    norm_T_wait(i)

            def norm_T_wait(i):
                pe.wait_ge(ev("normT_ready"), 4 * i + 2)
                norm_wait[0] = 4 * (i + 1)

            def gemm_cols(tag, lhs, parts=1, bias=None):
                banks = {(t, q): open_bank(pe, (*tag, t, q)) for t in range(T) for q in range(parts)}
                for c in range(CHUNKS):
                    w = take_chunk()
                    n = w[0].shape[2] // parts
                    for t in range(T):
                        for q in range(parts):
                            b = banks[t, q]
                            for j in range(KD // CHUNKS):
                                k = KD // CHUNKS * c + j
                                m = split_mm(b[:, 0:n], parts_of(lhs, k, slice(t * P, (t + 1) * P)),
                                            [z[:, j, q * n:(q + 1) * n] for z in w],
                                            start=(k == 0), stop=(k == KD - 1 and bias is None))
                            if c == CHUNKS - 1:
                                if bias is not None:
                                    m = mm(b[:, 0:n], sel_r[0:64, bias, :], bias_r[0:64, :], start=False, stop=True)
                                filled(m, (*tag, t, q))
                    if c < CHUNKS - 1:
                        chunk_used(m)
                slot_done((*tag, T - 1, parts - 1))

            def gemm_rows(tag, lhs, parts=2, ready=None):
                banks = [open_bank(pe, (*tag, t, h)) for t in range(T) for h in range(2)]
                for part in range(parts):
                    if ready:
                        ready(part)
                    for k in range(4):
                        w = take_chunk()
                        final = part == parts - 1 and k == 3
                        for t in range(T):
                            for h in range(2):
                                m = split_mm(banks[2 * t + h], parts_of(lhs, 4 * part + k, slice(t * P, (t + 1) * P)),
                                            [z[:, 0, h * BANK:(h + 1) * BANK] for z in w],
                                            start=(part == 0 and k == 0), stop=final)
                                if final:
                                    filled(m, (*tag, t, h))
                        if not final:
                            chunk_used(m)
                slot_done((*tag, 1, 1))

            def gemm_T(tag, rhs, tiles=4):
                pairs = (tiles + 1) // 2
                banks = [open_bank(pe, (*tag, g)) for g in range(pairs)]
                for c in range(CHUNKS):
                    w = take_chunk()
                    for f in range(tiles):
                        b = banks[f // 2][:, (f % 2) * S:(f % 2 + 1) * S]
                        for j in range(KD // CHUNKS):
                            k = KD // CHUNKS * c + j
                            m = split_mm(b, [z[:, j, f * P:(f + 1) * P] for z in w], parts_of(rhs, k, slice(None)),
                                        start=(k == 0 and f % 2 == 0), stop=(k == KD - 1), skip_group_check=True)
                        if c == CHUNKS - 1 and (f % 2 or f == tiles - 1):
                            filled(m, (*tag, f // 2))
                    if c < CHUNKS - 1:
                        chunk_used(m)
                slot_done((*tag, pairs - 1))

            def rows_product(name_T, name, src, n, ready, count):
                for h in range(2):
                    for t in range(T):
                        if h == 0:
                            pe.wait_ge(ev(ready), count[t])
                        b = open_bank(pe, (*name_T, t, h))
                        for k in range(4):
                            m = turn_(b[:, k * P:(k + 1) * P], src[:, t, (4 * h + k) * P:(4 * h + k + 1) * P], ident[:, :])
                        filled(m, (*name_T, t, h))
                gemm_rows(name, hT, 2, lambda part: pe.wait_ge(ev("lo_made"), n - T * (1 - part)))

            pe.wait_ge(ev("const_ready"), 1)
            pe.wait_ge(ev("rows_in"), 16 * N_ROWS_DMA)
            b = open_bank(pe, "cols")
            filled(turn_(b[:, 0:R_END], rows[0:R_END, :], ident[0:R_END, 0:R_END]), "cols")

            for l in range(DEPTH):
                def p1(i):
                    gemm_cols(("p1", l, i), hT, parts=SLOTS1[i][2])

                def gates(i):
                    gemm_cols(("gate", l, i), hT, bias=i)

                norm_T(l)
                p1(0)
                p1(1)
                p1(2)
                pe.wait_ge(ev("cn_ready"), l + 1)
                for t in range(T):
                    b = open_bank(pe, ("cT", l, t))
                    for k in range(3):
                        m = turn_(b[:, k * P:(k + 1) * P], cn[:, t, k * P:(k + 1) * P], ident[:, :])
                    filled(m, ("cT", l, t))
                copied(pe, ("cT", l, 0), ("cT", l, 1))
                pe.wait_ge(ev("layer_in"), 16 * N_LAYER_DMA * (l + 1))
                for t in range(T):
                    for h in range(2):
                        b = open_bank(pe, ("uq", l, t, h))
                        for k in range(2):
                            m = mm(b[:, 0:384], cT[:, k, t * P:(t + 1) * P], wuq[:, k, h * 384:(h + 1) * 384],
                                   start=(k == 0), stop=(k == 1))
                        filled(m, ("uq", l, t, h))
                        b = open_bank(pe, ("ukv", l, t, h))
                        filled(mm(b, cT[:, 2, t * P:(t + 1) * P], wukv[:, h * BANK:(h + 1) * BANK], start=True, stop=True),
                               ("ukv", l, t, h))
                p1(3)
                p1(4)
                p1(5)
                pe.wait_ge(ev("qk_ready"), l + 1)
                for t in range(T):
                    for g in range(4):
                        b = open_bank(pe, ("qkT", l, t, g))
                        for k in range(4):
                            m = turn_(b[0:MQK, k * P:(k + 1) * P], qk[:, t, 4 * g + k, :], ident[:, :])
                        filled(m, ("qkT", l, t, g))
                p1(6)
                p1(7)
                copied(pe, *[("qkT", l, t, g) for t in range(T) for g in range(4)])
                for j, (t, h0, hn) in enumerate(SC):
                    n = P * (t + 1)
                    b = open_bank(pe, ("sc", l, j), 2)
                    for h in range(hn):
                        m = mm(b[:, h * n:(h + 1) * n], qkT[0:MQK, h0 + h, t * P:(t + 1) * P], qkT[0:MQK, MH + h0 + h, 0:n],
                               start=True, stop=True)
                    filled(m, ("sc", l, j))
                b = open_bank(pe, ("glrT", l))
                copied(pe, ("p1", l, 6, 0, 0), ("p1", l, 6, 1, 0))
                for t in range(T):
                    m = turn_(b[0:GRANK, t * P:(t + 1) * P], proj[:, t, COL_GC:COL_GC + GRANK], ident[:, :])
                filled(m, ("glrT", l))
                pe.wait_ge(ev("const_ready"), 2)
                pe.wait_ge(ev("bias_ready"), l + 1)
                gates(0)
                copied(pe, ("glrT", l))
                b = open_bank(pe, ("gg", l))
                for t in range(T):
                    mm(b[:, t * 256:(t + 1) * 256], glrT[0:GRANK, t * P:(t + 1) * P], wgu[0:GRANK, :], start=True, stop=False)
                    m = mm(b[:, t * 256:(t + 1) * 256], ones[0:1, :], bgu[0:1, :], start=False, stop=True)
                filled(m, ("gg", l))
                for j in range(3):
                    pe.wait_ge(ev("p_ready"), 3 * l + j + 1)
                    for q in range(2):
                        b = open_bank(pe, ("pT", l, j, q))
                        for k in range(4):
                            m = turn_(b[:, k * P:(k + 1) * P], sc[:, j, (4 * q + k) * P:(4 * q + k + 1) * P], ident[:, :])
                        filled(m, ("pT", l, j, q))
                gates(1)
                copied(pe, *[("pT", l, j, q) for j in range(3) for q in range(2)])
                for t in range(T):
                    b = open_bank(pe, ("pv", l, t))
                    for h in range(MH):
                        for k in range(t + 1):
                            src = pT[:, 0, h, :] if t == 0 else pT[:, 1 + h // 4, 2 * (h % 4) + k, :]
                            m = mm(b[:, h * NOPE:(h + 1) * NOPE], src, mv[:, k, h * NOPE:(h + 1) * NOPE],
                                   start=(k == 0), stop=(k == t))
                    filled(m, ("pv", l, t))
                pe.wait_ge(ev("la_ready"), l + 1)
                for name, mat in (("gb", causal[:, 0, :]), ("gbl", blk[:, :])):
                    b = open_bank(pe, (name, l))
                    for t in range(T):
                        m = mm(b[:, t * 256:(t + 1) * 256], mat, gl_la[:, t, :], start=True, stop=True)
                    filled(m, (name, l))
                b = open_bank(pe, ("gdec", l), 2)
                for n in range(1, 3):
                    r = CH * (n % 2)
                    for pr in range(2):
                        c = BANK * (n - 1) + pr
                        m = mm(b[:, c:c + 1], gl_la[r:r + CH, n // 2, pr * P:(pr + 1) * P], ones[r:r + CH, 0:1],
                               start=True, stop=True)
                filled(m, ("gdec", l))
                gates(2)
                pe.wait_ge(ev("gqk_ready"), l + 1)
                for t in range(T):
                    b = open_bank(pe, ("gqkT", l, t))
                    for k in range(4):
                        m = turn_(b[:, k * P:(k + 1) * P], gl_qk[:, t, k * P:(k + 1) * P], ident[:, :])
                    filled(m, ("gqkT", l, t))
                copied(pe, ("p1", l, 7, 0, 0), ("p1", l, 7, 1, 0))
                b = open_bank(pe, ("gu", l), 2)
                for n in range(3):
                    r = CH * (n % 2)
                    for h in range(GH):
                        o = 64 * (h % 2)
                        c = (n % 2) * BANK + (n // 2) * 256 + (h // 2) * P
                        m = mm(b[o:o + 64, c:c + P], gl_ks[r:r + CH, n // 2, h * 64:(h + 1) * 64],
                               proj[r:r + CH, n // 2, COL_VC + h * P:COL_VC + (h + 1) * P], start=True, stop=True)
                filled(m, ("gu", l))
                gates(3)
                copied(pe, ("gqkT", l, 0), ("gqkT", l, 1))
                for t in range(T):
                    b = open_bank(pe, ("gatt", l, t), 2)
                    for h in range(GH):
                        o = 64 * (h % 2)
                        c = BANK * (h % 2) + (h // 2) * P
                        m = mm(b[:, c:c + P], gl_qkT[o:o + 64, 2 + h // 2, t * P:(t + 1) * P],
                               gl_qkT[o:o + 64, h // 2, t * P:(t + 1) * P], start=True, stop=True)
                    filled(m, ("gatt", l, t))
                b = open_bank(pe, ("sgT", l))
                for g in range(4):
                    m = turn_(b[:, g * P:(g + 1) * P], sgw[:, g, :], ident[:, :])
                filled(m, ("sgT", l))
                gates(4)
                pe.wait_ge(ev("vn_ready"), l + 1)
                copied(pe, ("sgT", l))
                for t in range(T):
                    b = open_bank(pe, ("sv", l, t))
                    for g in range(4):
                        m = mm(b[:, g * P:(g + 1) * P], sgwT[:, g, :], proj[:, t, COL_V + g * P:COL_V + (g + 1) * P],
                               start=True, stop=True)
                    filled(m, ("sv", l, t))
                copied(pe, ("gatt", l, 0), ("gatt", l, 1))
                copied(pe, ("gu", l))
                for t in range(T):
                    b = open_bank(pe, ("go", l, t), 2)
                    for h in range(GH):
                        o = 64 * (h % 2)
                        c = BANK * (h % 2) + (h // 2) * P
                        mm(b[:, c:c + P], gl_att[:, t, 2 * (h % 2) + h // 2, :], proj[:, t, COL_VC + h * P:COL_VC + (h + 1) * P],
                           start=True, stop=True, skip_group_check=True)
                        for n in range(max(1, 2 * t), 2 * t + 2):
                            r = CH * (n % 2)
                            m = mm(b[r:r + CH, c:c + P], gl_qkT[o:o + 64, h // 2, n * CH:(n + 1) * CH],
                                   gl_st[o:o + 64, n - 1, h // 2, :], start=False, stop=True, skip_group_check=True)
                    filled(m, ("go", l, t))
                gates(5)

                def turn_branch(i):
                    if i == 1:
                        copied(pe, ("sv", l, 0), ("sv", l, 1))
                    else:
                        pe.wait_ge(ev(f"y{i}_ready"), l + 1)
                    c0 = (COL_ZB, COL_U, COL_ZC)[i]
                    for t in range(T):
                        b = open_bank(pe, ("yT", l, i, t))
                        for k in range(4):
                            m = turn_(b[:, k * P:(k + 1) * P], proj[:, t, c0 + k * P:c0 + (k + 1) * P], ident[:, :])
                        filled(m, ("yT", l, i, t))

                def branch(i):
                    pe.wait_ge(ev("lo_made"), SPLITS1 * l + 2 * (i + 1))
                    banks = [open_bank(pe, ("br", l, i, t, h)) for t in range(T) for h in range(2)]
                    for k in range(4):
                        w = take_chunk()
                        for t in range(T):
                            for h in range(2):
                                m = split_mm(banks[2 * t + h], [yT[:, i % 2, z, k, t * P:(t + 1) * P] for z in range(2)],
                                            [z[:, 0, h * BANK:(h + 1) * BANK] for z in w], start=(k == 0), stop=(k == 3))
                                if k == 3:
                                    filled(m, ("br", l, i, t, h))
                        if k < 3:
                            chunk_used(m)
                    slot_done(("br", l, i, T - 1, 1))

                turn_branch(0)
                turn_branch(1)
                branch(0)
                turn_branch(2)
                branch(1)
                branch(2)
                rows_product(("mT", l), ("wo", l), merged, SPLITS1 * (l + 1), "merged_ready", [T * l + 1, T * l + 2])

            def turns(name, pieces, rows_=P):
                b = open_bank(pe, name)
                for k, piece in enumerate(pieces):
                    m = turn_(b[0:rows_, k * P:(k + 1) * P], piece, ident[:, :])
                filled(m, name)

            def p2(i):
                gemm_cols(("p2", i), hT)

            norm_T(2)
            for i, (c0, n) in enumerate(SLOTS2):
                gemm_T(("cv", i), hT, n // P)
            p2(0)
            p2(1)
            pe.wait_ge(ev("lfg_ready"), 1)
            b = open_bank(pe, "cum")
            for t in range(T):
                for d in range(2):
                    mm(b[:, t * 8 + d * 4:t * 8 + d * 4 + 4], causal[:, d, :], sp[:, t, d * 4:d * 4 + 4], start=True, stop=True)
                    c = 32 + t * 12 + d * 6
                    mm(b[:, c:c + 6], causal[:, d, :], gd_g[:, t, d * 6:d * 6 + 6], start=True, stop=True)
                mm(b[:, 16 + t * 8:24 + t * 8], blk[:, :], sp[:, t, 0:8], start=True, stop=True)
                m = mm(b[:, 56 + t * 12:68 + t * 12], blk[:, :], gd_g[:, t, :], start=True, stop=True)
            filled(m, "cum")
            p2(2)
            pe.wait_ge(ev("second_in"), 16 * N_SECOND_DMA)
            pe.wait_ge(ev("second_const"), 1)
            for t in range(T):
                for r in range(3):
                    b = open_bank(pe, ("nab", t, r))
                    filled(mm(b, mirror[:, :], na_raw[:, t, 2 * r:2 * r + 2, :].rearrange("p h n -> p (h n)"), start=True, stop=True), ("nab", t, r))
            pe.wait_ge(ev("mlg_ready"), 1)
            copied(pe, "cum")
            b = open_bank(pe, "mlrow", 2)
            for q, src in enumerate((ml_g, ml_bl)):
                for d in range(2):
                    for t in range(T):
                        c = ((q * 2 + d) * 2 + t) * P
                        m = turn_(b[0:MLH, c:c + P], src[:, t, d * 4:d * 4 + 4], ident[:, :])
            filled(m, "mlrow")
            p2(3)
            for t in range(T):
                copied(pe, ("p2", 2, t, 0), ("p2", 3, t, 0))
                for q in range(2):
                    turns(("naT", t, q), [proj2[:, t, (3 * q + k) * P:(3 * q + k + 1) * P] for k in range(3)])
            p2(4)
            copied(pe, *[("naT", t, q) for t in range(T) for q in range(2)])
            for t in range(T):
                for z in range(2):
                    b = open_bank(pe, ("nas", t, z), 2)
                    o = 64 * z
                    for r in range(3):
                        m = mm(b[:, r * S:(r + 1) * S], na_T[o:o + 64, r, t * P:(t + 1) * P], na_T[o:o + 64, 3 + r, :],
                               start=True, stop=True)
                    filled(m, ("nas", t, z))
            p2(5)
            norm_T(3, wait=False)
            pe.wait_ge(ev("mlm_ready"), 1)
            b = open_bank(pe, "mlcol")
            for q in range(3):
                for t in range(T):
                    for d in range(2):
                        c = (q * 2 + t) * 8 + d * 4
                        m = turn_(b[:, c:c + 4], ml_max[0:MLH, q, d, t * P:(t + 1) * P], ident[0:MLH, 0:MLH])
            filled(m, "mlcol")
            for t in range(T):
                for d in range(2):
                    b = open_bank(pe, ("mrow", t, d))
                    for h in range(MLH):
                        m = mm(b[:, h * P:(h + 1) * P], sel[0:MLH, h, :], ml_max[0:MLH, 0, d, t * P:(t + 1) * P],
                               start=True, stop=True)
                    filled(m, ("mrow", t, d))
            for t in range(T):
                copied(pe, ("p2", 4, t, 0), ("p2", 5, t, 0))
                turns(("mlT", t), [proj2[:, t, C_MLQ + k * P:C_MLQ + (k + 1) * P] for k in range(4)])
            for t in range(T):
                for q in range(3):
                    pe.wait_ge(ev("conv_ready"), q + 1)
                    turns(("gT", t, q), [conv[:, 3 * q + k, t * P:(t + 1) * P] for k in range(3)])
            copied(pe, ("mlT", 0), ("mlT", 1))
            for t in range(T):
                b = open_bank(pe, ("mqk", t), 2)
                for h in range(MLH):
                    o, c = 64 * (h % 2), BANK * (h % 2) + (h // 2) * P
                    m = mm(b[:, c:c + P], ml_T[o:o + 64, 2 + h // 2, t * P:(t + 1) * P], ml_T[o:o + 64, h // 2, t * P:(t + 1) * P],
                           start=True, stop=True)
                filled(m, ("mqk", t))
            for t in range(T):
                pe.wait_ge(ev("nap_ready"), t + 1)
                for q in range(3):
                    flat = na_s[:, t, :, :, :].rearrange("p z r n -> p (z r n)")
                    turns(("napT", t, q), [flat[:, (4 * q + k) * P:(4 * q + k + 1) * P] for k in range(4)])
            pe.wait_ge(ev("mle_ready"), 1)
            b = open_bank(pe, "mldec")
            for n in range(4):
                for z in range(2):
                    m = mm(b[64 * z:64 * z + 64, n * 4:n * 4 + 4], first[:, n % 2, :], ml_e[:, 3, n // 2, z::2], start=True, stop=True)
            filled(m, "mldec")
            pe.wait_ge(ev("mlk_ready"), 1)
            for d in range(2):
                b = open_bank(pe, ("mu", d), 2)
                for j in range(3):
                    n = j if d == 0 else 3 - j
                    r = CH * (n % 2)
                    for h in range(MLH):
                        o, c = 64 * (h % 2), BANK * (j % 2) + (j // 2) * 130 + (h // 2) * 65
                        m = mm(b[o:o + 64, c:c + 65], ml_k[r:r + CH, n // 2, d, h, :], ml_v[r:r + CH, n // 2, h, :],
                               start=True, stop=True)
                filled(m, ("mu", d))
            copied(pe, *[("napT", t, q) for t in range(T) for q in range(3)])
            for t in range(T):
                b = open_bank(pe, ("napv", t))
                for h in range(NH):
                    for k in range(2):
                        i = ((t * 2 + h % 2) * 3 + h // 2) * 2 + k
                        m = mm(b[:, h * HD:(h + 1) * HD], na_pT[:, i, :], proj2[:, k, 768 + h * HD:768 + (h + 1) * HD],
                               start=(k == 0), stop=(k == 1))
                filled(m, ("napv", t))
            copied(pe, ("mu", 0), ("mu", 1))
            pe.wait_ge(ev("mlp_ready"), 1)
            for t in range(T):
                for d in range(2):
                    b = open_bank(pe, ("mint", t, d), 2)
                    for h in range(MLH):
                        o, c = 64 * (h % 2), BANK * (h % 2) + (h // 2) * 65
                        for n in (2 * t, 2 * t + 1):
                            j = n if d == 0 else 3 - n
                            r = CH * (n % 2)
                            m = mm(b[r:r + CH, c:c + 65], ml_T[o:o + 64, h // 2, n * CH:(n + 1) * CH], ml_c[o:o + 64, d, j, h // 2, :],
                                   start=True, stop=True)
                    filled(m, ("mint", t, d))
                    b = open_bank(pe, ("mia", t, d))
                    for h in range(MLH):
                        m = mm(b[:, h * 65:(h + 1) * 65], ml_p[:, t, d, h, :], ml_v[:, t, h, :], start=True, stop=True)
                    filled(m, ("mia", t, d))

            norm_T_wait(3)
            gemm_T(("xk", 0), hT)
            pe.wait_ge(ev("gdqk_ready"), 1)
            for t in range(T):
                for q in range(2):
                    turns(("gqT", t, q), [gd[:, t, (3 * q + k) * P:(3 * q + k + 1) * P] for k in range(3)])
            pe.wait_ge(ev("gdkb_ready"), 1)
            for t in range(T):
                for d in range(2):
                    flat = gd_kb[:, t, d, :, :].rearrange("p h n -> p (h n)")
                    turns(("gkT", t, d), [flat[:, k * P:(k + 1) * P] for k in range(3)])
            for t in range(T):
                for d in range(2):
                    for z in range(2):
                        b = open_bank(pe, ("gl", t, d, z))
                        for r in range(3):
                            c = d * 6 + 2 * r + z
                            m = mm(b[:, r * P:(r + 1) * P], gd_g[:, t, c:c + 1].to_broadcast([P, P]), causal[:, d, :],
                                   start=True, stop=True)
                        filled(m, ("gl", t, d, z))
            copied(pe, *[("gqT", t, q) for t in range(T) for q in range(2)], *[("gkT", t, d) for t in range(T) for d in range(2)])
            for t in range(T):
                for d in range(2):
                    for z in range(2):
                        o = 64 * z
                        b = open_bank(pe, ("kk", t, d, z))
                        for r in range(3):
                            m = mm(b[:, r * P:(r + 1) * P], gd_T[o:o + 64, 3 + r, t * P:(t + 1) * P], gd_kbT[o:o + 64, t, d, r, :],
                                   start=True, stop=True)
                        filled(m, ("kk", t, d, z))
            for t in range(T):
                for z in range(2):
                    o = 64 * z
                    b = open_bank(pe, ("kq", t, z))
                    for r in range(3):
                        m = mm(b[:, r * P:(r + 1) * P], gd_T[o:o + 64, 3 + r, t * P:(t + 1) * P], gd_T[o:o + 64, r, t * P:(t + 1) * P],
                               start=True, stop=True)
                    filled(m, ("kq", t, z))
            GROUPS = [(t, d, z) for t in range(T) for d in range(2) for z in range(2)]
            gemm_T(("xk", 1), hT)
            gemm_cols(("xv", 0), hT)
            pe.wait_ge(ev("inv0_ready"), 1)
            for t, d, z in GROUPS:
                turns(("inv0", t, d, z), [gd_inv[1][:, t, d, 3 * z + r, :] for r in range(3)])
            for k in range(1, 6):
                def product(g):
                    t, d, z = g
                    copied(pe, ("inv0", *g) if k == 1 else ("ty", k - 1, *g))
                    b = open_bank(pe, ("tx", k, *g))
                    for r in range(3):
                        i = 3 * z + r
                        m = mm(b[:, r * P:(r + 1) * P], gd_a[:, t, d, i, :], gd_inv[0][:, t, d, i, :], start=True, stop=True)
                    filled(m, ("tx", k, *g))

                def update(n, g):
                    t, d, z = g
                    copied(pe, ("tx", k, *g))
                    if k > 1:
                        copied(pe, ("tz", k - 1, *g))
                    for kind in ("ty", "tz")[k == 5:]:
                        b = open_bank(pe, (kind, k, *g))
                        for r in range(3):
                            xr, rr = gd_x[:, n % 4, r, :], gd_inv[1][:, t, d, 3 * z + r, :]
                            if kind == "ty":
                                m = mm(b[:, r * P:(r + 1) * P], rr, xr, start=True, stop=True)
                            else:
                                m = mm(b[:, r * P:(r + 1) * P], xr, rr, start=True, stop=True)
                        filled(m, (kind, k, *g))

                for n, g in enumerate(GROUPS):
                    product(g)
                    if n >= 2:
                        update(n - 2, GROUPS[n - 2])
                for n in (6, 7):
                    update(n, GROUPS[n])
            b = open_bank(pe, "gdec2")
            for n in range(4):
                for z in range(2):
                    m = mm(b[64 * z:64 * z + 64, n * 6:n * 6 + 6], first[:, n % 2, :], gd_e[:, 2, n // 2, z::2], start=True, stop=True)
            filled(m, "gdec2")
            for t in range(T):
                for d in range(2):
                    copied(pe, ("tz", 5, t, d, 0), ("tz", 5, t, d, 1))
                    b = open_bank(pe, ("gu2", t, d))
                    for h in range(GNH):
                        m = mm(b[:, h * HD:(h + 1) * HD], gd_inv[1][:, t, d, 3 * (h % 2) + h // 2, :], gd_vb[:, t, d, h, :],
                               start=True, stop=True)
                    filled(m, ("gu2", t, d))
                    b = open_bank(pe, ("gw", t, d))
                    for h in range(GNH):
                        o, c = 64 * (h % 2), (h // 2) * P
                        m = mm(b[o:o + 64, c:c + P], gd_kbe[:, t, d, h, :], gd_inv[1][:, t, d, 3 * (h % 2) + h // 2, :],
                               start=True, stop=True)
                    filled(m, ("gw", t, d))
            gemm_cols(("xv", 1), hT)
            copied(pe, *[(n, t, d) for n in ("gu2", "gw") for t in range(T) for d in range(2)])
            for j in range(4):
                for d in range(2):
                    n = j if d == 0 else 3 - j
                    t, r = n // 2, CH * (n % 2)
                    if j:
                        copied(pe, ("kv", j - 1, d))
                        b = open_bank(pe, ("ws", j, d), 2)
                        for h in range(GNH):
                            o, c = 64 * (h % 2), BANK * (h % 2) + (h // 2) * HD
                            m = mm(b[r:r + CH, c:c + HD], gd_wk[o:o + 64, t, d, h // 2, r:r + CH], gd_st[o:o + 64, j, d, h // 2, :],
                                   start=True, stop=True)
                        filled(m, ("ws", j, d))
                for d in range(2):
                    n = j if d == 0 else 3 - j
                    t, r = n // 2, CH * (n % 2)
                    if j < 3:
                        if j:
                            copied(pe, ("ws", j, d))
                        else:
                            pe.wait_ge(ev("vn0_ready"), d + 1)
                        b = open_bank(pe, ("kv", j, d))
                        for h in range(GNH):
                            o, c = 64 * (h % 2), (h // 2) * HD
                            m = mm(b[o:o + 64, c:c + HD], gd_ks[r:r + CH, t, d, h, :], gd_vn[r:r + CH, t, d, h, :],
                                   start=True, stop=True)
                        filled(m, ("kv", j, d))
            copied(pe, ("ws", 3, 0), ("ws", 3, 1))
            for t in range(T):
                for d in range(2):
                    b = open_bank(pe, ("oi", t, d), 2)
                    for h in range(GNH):
                        o, c = 64 * (h % 2), BANK * (h % 2) + (h // 2) * HD
                        for n in (2 * t, 2 * t + 1):
                            j = n if d == 0 else 3 - n
                            r = CH * (n % 2)
                            m = mm(b[r:r + CH, c:c + HD], gd_T[o:o + 64, h // 2, n * CH:(n + 1) * CH], gd_st[o:o + 64, j, d, h // 2, :],
                                   start=True, stop=True)
                    filled(m, ("oi", t, d))
                    b = open_bank(pe, ("oa", t, d))
                    for h in range(GNH):
                        m = mm(b[:, h * HD:(h + 1) * HD], gd_att[:, t, d, 3 * (h % 2) + h // 2, :], gd_vn[:, t, d, h, :],
                               start=True, stop=True)
                    filled(m, ("oa", t, d))
            rows_product(("yT2",), ("wo2",), y2, SPLITS1 * DEPTH + 4, "mixed_ready", [1, 1])

            norm_T(4)
            for i in range(2):
                gemm_T(("xq", i), hT)
            copied(pe, *[(n, i, g) for n in ("xk", "xq") for i in range(2) for g in range(2)])
            for t in range(T):
                for g in range(2):
                    b = open_bank(pe, ("xs", t, g))
                    for h in range(2):
                        for k in range(2):
                            i = 2 * (2 * g + h) + k
                            m = mm(b[:, h * S:(h + 1) * S], xq_T[:, i, t * P:(t + 1) * P], xk_T[:, i // 4, i % 4 * S:(i % 4 + 1) * S], start=(k == 0), stop=(k == 1))
                    filled(m, ("xs", t, g))
            for t in range(T):
                pe.wait_ge(ev("xp_ready"), t + 1)
                for g in range(2):
                    turns(("xpT", t, g), [x_s[:, t, 2 * g + h, m_ * P:(m_ + 1) * P] for m_ in range(2) for h in range(2)])
            copied(pe, *[("xpT", t, g) for t in range(T) for g in range(2)], *[("xv", i, t, 0) for i in range(2) for t in range(T)])
            for h in range(XH):
                b = open_bank(pe, ("xo", h))
                for e in range(2):
                    for k in range(2):
                        c = h * XD + e * P
                        m = mm(b[:, e * S:(e + 1) * S], x_v[:, k, c:c + P], x_pT[:, k, h, :], start=(k == 0), stop=(k == 1))
                filled(m, ("xo", h))
            pe.wait_ge(ev("lo_made"), SPLITS1 * DEPTH + 4 + XH)
            gemm_rows(("wxo",), x_oT)

            norm_T(5)
            for i in range(8):
                gemm_T(("f1", i), hT)
            gemm_rows(("f2",), h1T, 8, lambda part: pe.wait_ge(ev("h1_ready"), 2 * (part + 1)))

        @block.vector
        def _(dve):
            V = nc.vector

            def v(ins, name="dve"):
                done(dve, ins, name)

            def rsqrt(n):
                r, y, z = rin[:, 0:n], rout[:, 0:n], rtmp[:, 0:n]
                v(V.tensor_scalar(y.bitcast(I32), r.bitcast(I32), 1, None, ALU.arith_shift_right))
                v(V.tensor_scalar(y.bitcast(I32), y.bitcast(I32), -1.0, float(RSQRT_GUESS), ALU.mult, ALU.add))
                for _ in range(3):
                    v(V.tensor_tensor(z, y, y, ALU.mult))
                    v(V.scalar_tensor_tensor(out=z, in0=z, scalar=-0.5, in1=r, op0=ALU.mult, op1=ALU.mult))
                    v(V.scalar_tensor_tensor(out=y, in0=z, scalar=1.5, in1=y, op0=ALU.add, op1=ALU.mult))

            def inverse_rms(i):
                dve.wait_ge(ev("ssq_ready"), 2 * (i + 1))
                v(V.tensor_scalar(rin[:, 0:2], ssq[:, 0:2], 1.0 / D, EPS, ALU.mult, ALU.add))
                rsqrt(2)

            def normalise(i, src=None):
                src = x if src is None else src
                inverse_rms(i)
                for t in range(T):
                    v(V.tensor_scalar(xn[:, t * D:(t + 1) * D], src[:, t, :], rout[:, t:t + 1], None, ALU.mult), "xn_ready")

            def add_x(tag):
                for t in range(T):
                    for h in range(2):
                        b = full(dve, (*tag, t, h))
                        dst = x[:, t, h * BANK:(h + 1) * BANK]
                        v(V.tensor_tensor(dst, dst, b, ALU.add), free((*tag, t, h)))

            def turned(i, r0, dst, normT=normT):
                def piece(ap, t, h):
                    return ap[:, 4 * h:4 * h + 4, t * P:(t + 1) * P]

                if i == 3:
                    full(dve, ("xT", i, T - 1, 1))
                for h in range(2):
                    for t in range(T):
                        n = ("xT", i, t, h)
                        b = full(dve, n).rearrange("p (k n) -> p k n", k=4)
                        v(V.tensor_tensor(piece(normT, t, h), b, bc(cols[:, r0 + 4 * h:r0 + 4 * h + 4], 2, P), ALU.mult), free(n))
                    for t in range(T):
                        dve.wait_ge(ev("normhi_ready"), 4 * i + 2 * h + t + 1)
                        v(V.tensor_tensor(piece(dst[:, 1, :, :], t, h), piece(normT, t, h), plain(piece(dst[:, 0, :, :], t, h)),
                                          ALU.subtract), "normT_ready")

            hi_seen = [0]

            def low(name, b, dst_lo, dst_hi, scale):
                hi_seen[0] += 1
                dve.wait_ge(ev("hi_made"), hi_seen[0])
                ins = V.scalar_tensor_tensor(out=dst_lo, in0=b, scalar=scale, in1=plain(dst_hi), op0=ALU.mult, op1=ALU.subtract)
                ins.then_inc(*free(name)[:1], 1)
                dve.wait_ge(*free(name))
                v(V.memset(flag[:, :], 0.0), "lo_made")

            def low_rows(tag, scale):
                for h in range(2):
                    for t in range(T):
                        n = (*tag, t, h)
                        b = full(dve, n).rearrange("p (k n) -> p k n", k=4)
                        cols_ = slice(t * P, (t + 1) * P)
                        low(n, b, hT[:, 1, 4 * h:4 * h + 4, cols_], hT[:, 0, 4 * h:4 * h + 4, cols_], scale)

            def rotary_tables():
                dve.wait_ge(ev("pos_in"), 16)
                v(V.tensor_copy(posf[:, :], posi[:, :]))
                for t in range(T):
                    v(V.tensor_scalar(ang[:, t, :], freq[:, :], posf[:, t:t + 1], None, ALU.mult))
                v(V.tensor_scalar(ang2, ang1, float(1.0 / TWO_PI), None, ALU.mult))
                v(V.tensor_scalar(ang2, ang2, ROUND, None, ALU.add))
                v(V.tensor_scalar(ang2, ang2, -ROUND, None, ALU.add))
                for part in (PI_A, PI_B, PI_C):
                    v(V.scalar_tensor_tensor(out=ang1, in0=ang2, scalar=-part, in1=ang1, op0=ALU.mult, op1=ALU.add))
                v(V.tensor_scalar(ang1, ang1, 3.1415925, -3.1415925, ALU.min, ALU.max))
                v(V.tensor_scalar(ang2, ang1, -1.0, None, ALU.mult))
                v(V.tensor_tensor(ang2, ang2, ang1, ALU.max))
                v(V.tensor_scalar(ang2, ang2, -1.0, float(np.pi / 2), ALU.mult, ALU.add), "angle_ready")

            for l in range(DEPTH):
                if l == 0:
                    dve.wait_ge(ev("const_ready"), 1)
                normalise(l)
                if l == 0:
                    v(V.tensor_copy(cols[:, :], full(dve, "cols")[:, 0:R_END]), free("cols"))
                turned(l, R_NORM + KD * l, hT)
                if l == 0:
                    rotary_tables()

                dve.wait_ge(ev("cssq_ready"), l + 1)
                v(V.tensor_scalar(rin[:, 0:2], ssq[:, 4:6], 1.0 / 256, EPS, ALU.mult, ALU.add))
                v(V.tensor_scalar(rin[:, 2:4], ssq[:, 6:8], 1.0 / 128, EPS, ALU.mult, ALU.add))
                rsqrt(4)
                for t in range(T):
                    v(V.tensor_scalar(cn[:, t, 0:256], proj[:, t, COL_CQ:COL_CQ + 256], rout[:, t:t + 1], None, ALU.mult))
                for t in range(T):
                    ins = V.tensor_scalar(cn[:, t, 256:384], proj[:, t, COL_CKV:COL_CKV + 128], rout[:, 2 + t:3 + t], None,
                                          ALU.mult)
                    v(ins, "cn_ready" if t else "dve")
                for t in range(T):
                    n = ("cT", l, t)
                    b = full(dve, n)
                    v(V.tensor_tensor(cT[:, 0:2, t * P:(t + 1) * P], b[:, 0:256].rearrange("p (k n) -> p k n", k=2),
                                      bc(cols[:, R_CQ + 2 * l:R_CQ + 2 * l + 2], 2, P), ALU.mult))
                    v(V.tensor_scalar(cT[:, 2, t * P:(t + 1) * P], b[:, 256:384], cols[:, R_CKV + l:R_CKV + l + 1], None,
                                      ALU.mult), free(n))
                for t in range(T):
                    v(V.tensor_copy(qk[:, t, MH:2 * MH, NOPE:MQK], bc(proj[:, t, COL_KR:COL_KR + ROPE], 1, MH)),
                      "kr_ready" if t else "dve")
                dve.wait_ge(ev("biashi_ready"), l + 1)
                low_bias = bias_r[LOW_ROWS:64, :]
                v(V.tensor_tensor(low_bias, bgate[LOW_ROWS:64, :], plain(low_bias), ALU.subtract), "bias_ready")
                dve.wait_ge(ev("qsq_ready"), l + 1)
                dve.wait_ge(ev("layer_in"), 16 * N_LAYER_DMA * (l + 1))
                qk2 = at(arena, RA, 2 * T * MH, MQK)
                v(V.tensor_reduce(ssq[:, 0:32], at(tmp, 0, 32, MQK), X, ALU.add))
                v(V.tensor_scalar(rin[:, :], ssq[:, 0:32], 1.0 / MQK, EPS, ALU.mult, ALU.add))
                rsqrt(32)
                v(V.tensor_tensor(qk2, qk2, bc(rout[:, :], 2, MQK), ALU.mult))
                for t in range(T):
                    for z in range(2):
                        dst = qk[:, t, z * MH:(z + 1) * MH, :]
                        v(V.tensor_tensor(dst, dst, bc(qk_g[:, z, :], 1, MH), ALU.mult))
                if l == 0:
                    dve.wait_ge(ev("trig_ready"), 1)
                n = 2 * MH * HALF
                for t in range(T):
                    x1, x2 = qk[:, t, :, NOPE:NOPE + HALF], qk[:, t, :, NOPE + HALF:MQK]
                    cos, sin = bc(trig[:, 0, t, :], 1, 2 * MH), bc(trig[:, 1, t, :], 1, 2 * MH)
                    r = [at(tmp, k * n, 2 * MH, HALF) for k in range(4)]
                    v(V.tensor_tensor(r[0], x1, cos, ALU.mult))
                    v(V.tensor_tensor(r[1], x2, sin, ALU.mult))
                    v(V.tensor_tensor(r[2], x1, sin, ALU.mult))
                    v(V.tensor_tensor(r[3], x2, cos, ALU.mult))
                    v(V.tensor_tensor(x1, r[0], r[1], ALU.subtract))
                    v(V.tensor_tensor(x2, r[2], r[3], ALU.add), "qk_ready" if t else "dve")

                uv = proj[:, :, 0:1024]
                th = at(tmp, 0, T, 1024)
                dve.wait_ge(ev("uvsq_ready"), l + 1)
                v(V.tensor_scalar(th, th, 0.044715, 1.0, ALU.mult, ALU.add))
                v(V.tensor_tensor(th, th, uv, ALU.mult), "uvarg_ready")
                dve.wait_ge(ev("uvtanh_ready"), l + 1)
                v(V.scalar_tensor_tensor(out=uv, in0=th, scalar=1.0, in1=uv, op0=ALU.add, op1=ALU.mult))
                zz = proj[:, :, COL_Z:COL_Z + 512]
                tz = at(tmp, 2048, T, 512)
                v(V.scalar_tensor_tensor(out=zz, in0=tz, scalar=1.0, in1=zz, op0=ALU.add, op1=ALU.mult), "tmp_free")
                for t in range(T):
                    v(V.bn_stats(stat[:, t, 0:6], proj[:, t, COL_V:COL_V + 512]))
                    v(V.bn_aggr(stat[:, t, 6:8], stat[:, t, 0:6]))
                v(V.tensor_scalar(rin[:, 0:2], stat[:, :, 7], 4 * EPS, None, ALU.add))
                rsqrt(2)
                for t in range(T):
                    vt = proj[:, t, COL_V:COL_V + 512]
                    v(V.tensor_scalar(vt, vt, stat[:, t, 6:7], rout[:, t:t + 1], ALU.subtract, ALU.mult))
                vb = proj[:, :, COL_V:COL_V + 512]
                v(V.tensor_tensor(vb, vb, bc(ln_g, 1, T), ALU.mult))
                v(V.tensor_tensor(vb, vb, bc(ln_b, 1, T), ALU.add), "vn_ready")
                ub = proj[:, :, 0:512]
                v(V.tensor_tensor(ub, ub, zz, ALU.mult))

                for j, (t, h0, hn) in enumerate(SC):
                    n = P * (t + 1)
                    copied(dve, ("sc", l, j))
                    s3 = sc[:, j, :].rearrange("p (h n) -> p h n", n=n)
                    v(V.memset(s3[0:CH, :, n - CH:n], NEG))
                    v(V.tensor_reduce(smax[:, 0:hn], s3, X, ALU.max))
                    v(V.tensor_tensor(s3, s3, bc(smax[:, 0:hn], 2, n), ALU.subtract), "s_ready")
                for j, (t, h0, hn) in enumerate(SC):
                    n = P * (t + 1)
                    dve.wait_ge(ev("p_ready"), 3 * l + j + 1)
                    s3 = sc[:, j, :].rearrange("p (h n) -> p h n", n=n)
                    v(V.tensor_reduce(ssum[:, t * MH + h0:t * MH + h0 + hn], s3, X, ALU.add))
                v(V.reciprocal(ssum[:, :], ssum[:, :]))

                n = ("gg", l)
                dve.wait_ge(ev("gln_ready"), l + 1)
                b = full(dve, n).rearrange("p (t n) -> p t n", t=T)
                v(V.tensor_scalar(gl_la, b, 0.0, None, ALU.min), free(n))
                v(V.tensor_tensor(gl_la, gl_la, gl_b, ALU.subtract), "la_ready")

                for t in range(T):
                    n = ("pv", l, t)
                    b = full(dve, n).rearrange("p (h n) -> p h n", h=MH)
                    v(V.tensor_tensor(at(tmp, t * 512, MH, NOPE), b, bc(ssum[:, t * MH:(t + 1) * MH], 2, NOPE), ALU.mult), free(n))
                zb = proj[:, :, COL_ZB:COL_ZB + 512]
                zc = proj[:, :, COL_ZC:COL_ZC + 512]
                dve.wait_ge(ev("zb_ready"), l + 1)
                tb = at(tmp, 1024, T, 512)
                v(V.scalar_tensor_tensor(out=zb, in0=tb, scalar=1.0, in1=zb, op0=ALU.add, op1=ALU.mult))
                v(V.tensor_tensor(zb, zb, at(tmp, 0, T, 512), ALU.mult), "y0_ready")
                tc = at(tmp, 2048, T, 512)
                v(V.scalar_tensor_tensor(out=zc, in0=tc, scalar=1.0, in1=zc, op0=ALU.add, op1=ALU.mult))

                if l == 0:
                    dve.wait_ge(ev("const_ready"), 2)
                qc, kc = proj[:, :, COL_QC:COL_QC + 256], proj[:, :, COL_KC:COL_KC + 256]
                dve.wait_ge(ev("ge_ready"), l + 1)
                v(V.scalar_tensor_tensor(out=gl_qk[:, :, 0:256], in0=gl_e, scalar=GDK ** -0.5, in1=qc, op0=ALU.mult,
                                         op1=ALU.mult))
                v(V.tensor_tensor(gl_qk[:, :, 256:512], gl_e2, kc, ALU.mult))
                b = full(dve, ("gbl", l)).rearrange("p (t n) -> p t n", t=T)
                v(V.tensor_tensor(gl_b, b, gl_b, ALU.subtract), free(("gbl", l)))
                dve.wait_ge(ev("gks_ready"), l + 1)
                v(V.tensor_tensor(gl_ks, gl_b, kc, ALU.mult), "gqk_ready")
                copied(dve, ("gdec", l))
                b = full(dve, ("gu", l), 2)
                v(V.tensor_copy(gl_st[:, 0, :, :], b[:, 0:256].rearrange("p (a n) -> p a n", a=2)))
                for n in range(1, 3):
                    for pr in range(2):
                        c = 2 * (n - 1) + pr
                        c0 = (n % 2) * BANK + (n // 2) * 256 + pr * P
                        ins = V.scalar_tensor_tensor(out=gl_st[:, n, pr, :], in0=gl_st[:, n - 1, pr, :], scalar=gdec[:, c:c + 1],
                                                     in1=b[:, c0:c0 + P], op0=ALU.mult, op1=ALU.add)
                        v(ins, free(("gu", l)) if (n, pr) == (2, 1) else "dve")
                for t in range(T):
                    n = ("gatt", l, t)
                    b = full(dve, n, 2)
                    for z in range(2):
                        ins = V.tensor_tensor(gl_att[:, t, 2 * z:2 * z + 2, :],
                                              b[:, z * BANK:z * BANK + 256].rearrange("p (h n) -> p h n", h=2),
                                              bc(causal[:, 0, :], 1, 2), ALU.mult)
                        v(ins, free(n) if z else "dve")
                n = ("sgT", l)
                b = full(dve, n).rearrange("p (g n) -> p g n", g=4)
                v(V.tensor_copy(sgwT[:, :, :], b))
                v(V.memset(sgwT[CH:P, :, 0:CH], 0.0), free(n))
                for t in range(T):
                    n = ("sv", l, t)
                    b = full(dve, n)
                    for g in range(4):
                        u = proj[:, t, g * P:(g + 1) * P]
                        c = R_SGB + 4 * l + g
                        last_one = (t, g) == (T - 1, 3)
                        v(V.scalar_tensor_tensor(out=u, in0=b[:, g * P:(g + 1) * P], scalar=cols[:, c:c + 1], in1=u,
                                                 op0=ALU.add, op1=ALU.mult), free(n) if g == 3 else "dve")
                for t in range(T):
                    n = ("go", l, t)
                    b = full(dve, n, 2).rearrange("p (z n) -> p z n", z=2)
                    o4 = gl_o[:, t, :].rearrange("p (h z n) -> p z h n", h=2, z=2)
                    for z in range(2):
                        ins = V.tensor_copy(o4[:, z, :, :], b[:, z, 0:256].rearrange("p (h n) -> p h n", h=2))
                        v(ins, free(n) if z else "dve")
                v(V.tensor_tensor(gl_sq, gl_o, gl_o, ALU.mult))
                v(V.tensor_reduce(ssq[:, 0:8], at(arena, RC + 1024, 8, P), X, ALU.add))
                v(V.tensor_scalar(rin[:, 0:8], ssq[:, 0:8], 1.0 / GDV, EPS, ALU.mult, ALU.add))
                rsqrt(8)
                o3 = at(arena, RC, 8, P)
                v(V.tensor_tensor(o3, o3, bc(rout[:, 0:8], 2, P), ALU.mult))
                v(V.tensor_tensor(o3, o3, bc(o_g, 1, 8), ALU.mult))
                v(V.tensor_tensor(zc, zc, gl_o, ALU.mult), "y2_ready")

                def low_branch(i):
                    for t in range(T):
                        n = ("yT", l, i, t)
                        b = full(dve, n).rearrange("p (k n) -> p k n", k=4)
                        low(n, b, yT[:, i % 2, 1, :, t * P:(t + 1) * P], yT[:, i % 2, 0, :, t * P:(t + 1) * P], BRANCH_SCALE[i])

                low_branch(0)
                low_branch(1)
                for i in range(3):
                    g = BRANCHES[i]
                    for t in range(T):
                        for h in range(2):
                            n = ("br", l, i, t, h)
                            gt = gate[:, t, g * D + h * BANK:g * D + (h + 1) * BANK]
                            copied(dve, ("gate", l, 2 * g + h, t, 0))
                            b = full(dve, n)
                            dst = merged[:, t, h * BANK:(h + 1) * BANK] if i == 0 else gt
                            v(V.scalar_tensor_tensor(out=dst, in0=gt, scalar=1.0, in1=b, op0=ALU.add, op1=ALU.mult), free(n))
                        if i:
                            m = merged[:, t, :]
                            v(V.tensor_tensor(m, m, gate[:, t, g * D:(g + 1) * D], ALU.add), "merged_ready" if i == 2 else "dve")
                    if i == 0:
                        low_branch(2)
                low_rows(("mT", l), 0.5)
                add_x(("wo", l))

            normalise(2)
            turned(2, R_MIX, hT)
            for j in range(9):
                n = ("cv", j // 4, j % 4 // 2)
                b = full(dve, n)[:, (j % 2) * S:(j % 2 + 1) * S]
                dst = conv[:, j, :]

                def tap(k):
                    c = R_CONV + 9 * k + j
                    return cols[:, c:c + 1]

                v(V.tensor_scalar(dst, b, tap(2), None, ALU.mult))
                for k in (0, 1, 3, 4):
                    o = k - 2
                    lo, hi = max(0, -o), S - max(0, o)
                    ins = V.scalar_tensor_tensor(out=dst[:, lo:hi], in0=b[:, lo + o:hi + o], scalar=tap(k), in1=dst[:, lo:hi],
                                                 op0=ALU.mult, op1=ALU.add)
                    v(ins, free(n) if k == 4 and (j % 2 or j == 8) else "dve")
            v(V.memset(ssq[:, 31:32], 0.0), "conv_done")
            copied(dve, *[("p2", i, t, 0) for i in range(2) for t in range(T)])
            dve.wait_ge(ev("second_in"), 16 * N_SECOND_DMA)
            v(V.tensor_tensor(ml_if, proj2[:, :, C_MLI:C_MLI + 16], bc(if_b, 1, T), ALU.add))
            v(V.tensor_copy(sp[:, :, 0:8], ml_if[:, :, 8:16]))
            v(V.tensor_tensor(sp[:, :, 8:20], proj2[:, :, K_GDA:K_GDA + 12], bc(dt_b, 1, T), ALU.add), "sp_ready")
            for q in range(3):
                dve.wait_ge(ev("convtanh_ready"), q + 1)
                c3 = conv[:, 3 * q:3 * q + 3, :]
                v(V.scalar_tensor_tensor(out=c3, in0=gd_th[:, 3 * q:3 * q + 3, :], scalar=1.0, in1=c3, op0=ALU.add, op1=ALU.mult),
                  "conv_ready")
            dve.wait_ge(ev("spln_ready"), 1)
            v(V.scalar_tensor_tensor(out=gd_g, in0=sp[:, :, 8:20], scalar=0.0, in1=spl[:, :, 8:20], op0=ALU.max, op1=ALU.add))
            v(V.tensor_scalar(gd_g, gd_g, -1.0, None, ALU.mult))
            v(V.tensor_tensor(gd_g, gd_g, bc(a_log, 1, T), ALU.mult))
            v(V.tensor_scalar(beta, beta, 0.5, 0.5, ALU.mult, ALU.add))
            v(V.scalar_tensor_tensor(out=sp[:, :, 0:8], in0=sp[:, :, 0:8], scalar=0.0, in1=spl[:, :, 0:8], op0=ALU.min,
                                     op1=ALU.subtract), "lfg_ready")
            copied(dve, "cum")
            v(V.tensor_tensor(ml_g, ml_if[:, :, 0:8], ml_b, ALU.subtract), "mlg_ready")
            z2 = proj2[:, :, K_GDZ:K_GDZ + 384]
            dve.wait_ge(ev("zt_ready"), 1)
            v(V.scalar_tensor_tensor(out=z2, in0=zt, scalar=1.0, in1=z2, op0=ALU.add, op1=ALU.mult))
            normalise(3, mem)
            dve.wait_ge(ev("second_const"), 1)
            for t in range(T):
                for r in range(3):
                    n = ("nab", t, r)
                    b = full(dve, n).rearrange("p (z r n) -> p z r n", z=2, r=4)
                    dst = na_s[:, t, :, r, :].rearrange("p z (r n) -> p z r n", r=4)
                    v(V.tensor_tensor(dst, b, bc(bc(na_mask, 1, 4), 1, 2), ALU.add), free(n))
            copied(dve, "mlrow")
            v(V.memset(ml_m[0:MLH, :, :], 0.0))
            for j in range(4):
                for d in range(2):
                    n = j if d == 0 else 3 - j
                    src, dst = ml_row[0:MLH, 0, d, n * CH:(n + 1) * CH], ml_max[0:MLH, 0, d, n * CH:(n + 1) * CH]
                    if d:
                        src, dst = src[:, ::-1], dst[:, ::-1]
                    v(V.tensor_tensor_scan(dst, src, src, ml_m[0:MLH, d, j:j + 1], ALU.max, ALU.max))
                    e = n * CH + (0 if d else CH - 1)
                    v(V.tensor_tensor(ml_m[0:MLH, d, j + 1:j + 2], ml_max[0:MLH, 0, d, e:e + 1], ml_row[0:MLH, 1, d, e:e + 1], ALU.add))
            for q in range(2):
                for d in range(2):
                    src = ml_m[0:MLH, d, q:q + 4]
                    if d:
                        src = src[:, ::-1]
                    dst = ml_max[0:MLH, 1 + q, d, :].rearrange("p (a b) -> p a b", a=4)
                    v(V.tensor_copy(dst, bc(src, 2, CH)), "mlm_ready" if (q, d) == (1, 1) else "dve")
            for t in range(T):
                for z in range(2):
                    n = ("nas", t, z)
                    dst = na_s[:, t, z, :, :].rearrange("p r n -> p (r n)")
                    v(V.scalar_tensor_tensor(out=dst, in0=full(dve, n, 2)[:, 0:768], scalar=HD ** -0.5, in1=dst, op0=ALU.mult,
                                             op1=ALU.add), free(n))
                s3 = na_s[:, t, :, :, :].rearrange("p z r n -> p (z r) n")
                v(V.tensor_reduce(smax[:, 0:6], s3, X, ALU.max))
                v(V.tensor_tensor(s3, s3, bc(smax[:, 0:6], 2, S), ALU.subtract), "nas_ready")
            turned(3, R_MEM, hT, mem_normT)
            for t in range(T):
                for d in range(2):
                    n = ("mrow", t, d)
                    b = full(dve, n).rearrange("p (h n) -> p h n", h=MLH)
                    v(V.tensor_tensor(ml_p[:, t, d, :, :], bc(ml_g[:, t, d * 4:d * 4 + 4], 2, P), b, ALU.subtract), free(n))
            flat = ml_p[:, :, :, :, :].rearrange("p t d h n -> p (t d h n)")
            v(V.tensor_scalar(flat, flat, 0.0, None, ALU.min), "mld_ready")
            copied(dve, "mlcol")
            v(V.tensor_tensor(ml_e[:, 0, :, :], ml_col[:, 1, :, :], ml_col[:, 0, :, :], ALU.subtract))
            v(V.scalar_tensor_tensor(out=ml_e[:, 1, :, :], in0=ml_b, scalar=-1.0, in1=ml_col[:, 0, :, :], op0=ALU.mult,
                                     op1=ALU.subtract))
            v(V.tensor_tensor(ml_e[:, 2, :, :], ml_bl, ml_col[:, 2, :, :], ALU.subtract))
            v(V.tensor_tensor(ml_e[:, 3, :, :], ml_e[:, 2, :, :], ml_col[:, 1, :, :], ALU.add))
            v(V.tensor_tensor(ml_e[:, 2, :, :], ml_e[:, 2, :, :], ml_g, ALU.add), "mlarg_ready")
            v(V.tensor_copy(ml_v[:, :, :, 0:HD], proj2[:, :, C_MLV:C_MLV + 256].rearrange("p t (h n) -> p t h n", h=MLH)))
            v(V.memset(ml_v[:, :, :, HD:HD + 1], 1.0))
            v(V.memset(ml_c[:, :, 0, :, :], 0.0))
            for t in range(T):
                dve.wait_ge(ev("nap_ready"), t + 1)
                v(V.tensor_reduce(ssum[:, 6 * t:6 * t + 6], na_s[:, t, :, :, :].rearrange("p z r n -> p (z r) n"), X, ALU.add))
            v(V.reciprocal(ssum[:, 0:12], ssum[:, 0:12]))
            dve.wait_ge(ev("mle_ready"), 1)
            for t in range(T):
                for d in range(2):
                    k = proj2[:, t, C_MLK:C_MLK + 256].rearrange("p (h n) -> p h n", h=MLH)
                    v(V.scalar_tensor_tensor(out=ml_k[:, t, d, :, :], in0=k, scalar=HD ** -0.5,
                                             in1=bc(ml_e[:, 2, t, d * 4:d * 4 + 4], 2, HD), op0=ALU.mult, op1=ALU.mult),
                      "mlk_ready" if (t, d) == (1, 1) else "dve")
            dve.wait_ge(ev("mlx_ready"), 1)
            for t in range(T):
                for d in range(2):
                    p4 = ml_p[:, t, d, :, :]
                    v(V.tensor_tensor(p4, p4, bc(causal[:, d, :], 1, MLH), ALU.mult))
            for t in range(T):
                n = ("mqk", t)
                b = full(dve, n, 2).rearrange("p (z n) -> p z n", z=2)[:, :, 0:256].rearrange("p z (r n) -> p z r n", r=2)
                for d in range(2):
                    p4 = ml_p[:, t, d, :, :].rearrange("p (r z) n -> p z r n", z=2)
                    v(V.tensor_tensor(p4, p4, b, ALU.mult), free(n) if d else "dve")
            v(V.memset(ssq[:, 31:32], 0.0), "mlp_ready")
            copied(dve, "mldec")
            for d in range(2):
                n_ = ("mu", d)
                b = full(dve, n_, 2)
                v(V.tensor_copy(ml_c[:, d, 1, :, :], b[:, 0:130].rearrange("p (r n) -> p r n", r=2)))
                for j in range(1, 3):
                    n = j if d == 0 else 3 - j
                    c = BANK * (j % 2) + (j // 2) * 130
                    dst = ml_c[:, d, j + 1, :, :]
                    v(V.tensor_tensor(dst, ml_c[:, d, j, :, :], bc(ml_dec[:, n, d, :], 2, HD + 1), ALU.mult))
                    v(V.tensor_tensor(dst, dst, b[:, c:c + 130].rearrange("p (r n) -> p r n", r=2), ALU.add),
                      free(n_) if j == 2 else "dve")
            for t in range(T):
                n = ("napv", t)
                b = full(dve, n)[:, 0:384].rearrange("p (r z n) -> p r z n", r=3, z=2)
                dst = y2[:, t, 0:384].rearrange("p (r z n) -> p r z n", r=3, z=2)
                w = ssum[:, 6 * t:6 * t + 6].rearrange("p (z r) -> p r z", z=2)
                v(V.tensor_tensor(dst, b, bc(w, 3, HD), ALU.mult), free(n))
            for t in range(T):
                for d in range(2):
                    n = ("mint", t, d)
                    b = full(dve, n, 2).rearrange("p (z n) -> p z n", z=2)[:, :, 0:130].rearrange("p z (r n) -> p z r n", r=2)
                    dst = ml_n[:, t, d, :, :].rearrange("p (r z) n -> p z r n", z=2)
                    w = ml_e[:, 0, t, d * 4:d * 4 + 4].rearrange("p (r z) -> p z r", z=2)
                    v(V.tensor_tensor(dst, b, bc(w, 3, HD + 1), ALU.mult), free(n))
                    n = ("mia", t, d)
                    dst = ml_n[:, t, d, :, :].rearrange("p h n -> p (h n)")
                    v(V.tensor_tensor(dst, dst, full(dve, n)[:, 0:260], ALU.add), free(n))
            n16 = at(arena, 17688, 16, HD + 1)
            v(V.tensor_copy(rc_, n16[:, :, HD]))
            v(V.scalar_tensor_tensor(out=ssum[:, 0:16], in0=rc_, scalar=-1.0, in1=rc_, op0=ALU.mult, op1=ALU.max))
            v(V.tensor_tensor(ssum[:, 0:16], ssum[:, 0:16], at(tiny, 348, 16), ALU.max))
            v(V.reciprocal(ssum[:, 0:16], ssum[:, 0:16]))
            v(V.tensor_tensor(n16[:, :, 0:HD], n16[:, :, 0:HD], bc(ssum[:, 0:16], 2, HD), ALU.mult))

            def head_norm(src, heads, c0, w, gate_, twice):
                dst = y2[:, :, c0:c0 + heads * HD]
                d4 = dst.rearrange("p t (h n) -> p t h n", h=heads)
                for t in range(T):
                    v(V.tensor_tensor(d4[:, t, :, :], src[:, t, 0, :, 0:HD], src[:, t, 1, :, 0:HD], ALU.add))
                sq = src[:, :, 0, :, 0:HD]
                v(V.tensor_tensor(sq, d4, d4, ALU.mult))
                v(V.tensor_reduce(ssq[:, 0:T * heads].rearrange("p (t h) -> p t h", t=T), sq, X, ALU.add))
                v(V.tensor_scalar(rin[:, 0:T * heads], ssq[:, 0:T * heads], 1.0 / HD, EPS, ALU.mult, ALU.add))
                rsqrt(T * heads)
                r = rout[:, 0:T * heads].rearrange("p (t h) -> p t h", t=T)
                v(V.tensor_tensor(d4, d4, bc(r, 3, HD), ALU.mult))
                v(V.tensor_tensor(dst, dst, bc(w, 1, T), ALU.mult))
                if twice:
                    v(V.scalar_tensor_tensor(out=gate_, in0=gate_, scalar=1.0, in1=dst, op0=ALU.add, op1=ALU.mult))
                else:
                    v(V.tensor_tensor(gate_, gate_, dst, ALU.mult))
                v(V.tensor_scalar(dst, gate_, 0.5, None, ALU.mult), "mixed_ready" if not twice else "dve")

            head_norm(ml_n, MLH, 640 - 256, ml_w, ot, True)
            v(V.memset(ssq[:, 31:32], 0.0), "ml_done")

            v(V.tensor_copy(gd_e[:, 0, :, :], gd_c))
            v(V.tensor_tensor(gd_e[:, 1, :, :], gd_cl, gd_c, ALU.subtract))
            v(V.tensor_copy(gd_e[:, 2, :, :], gd_cl), "gdarg_ready")
            dve.wait_ge(ev("gdsq_ready"), 1)
            sq = at(arena, 0, 24, HD)
            v(V.tensor_reduce(ssq[:, 0:24], sq, X, ALU.add))
            v(V.tensor_scalar(rin[:, 0:24], ssq[:, 0:24], 4 * EPS, None, ALU.add))
            rsqrt(24)
            qr = rout[:, 0:24].rearrange("p (t q h) -> p t q h", t=T, q=2)[:, :, 0, :]
            v(V.tensor_scalar(qr, qr, HD ** -0.5, None, ALU.mult))
            g4 = gd[:, :, 0:768].rearrange("p t (h n) -> p t h n", h=12)
            v(V.tensor_tensor(g4, g4, bc(rout[:, 0:24].rearrange("p (t h) -> p t h", t=T), 3, HD), ALU.mult), "gdqk_ready")
            dve.wait_ge(ev("gde_ready"), 1)
            k4 = gd[:, :, 384:768].rearrange("p t (h n) -> p t h n", h=GNH)
            for d in range(2):
                v(V.tensor_tensor(gd_kb[:, :, d, :, :], k4, bc(beta[:, :, d * 6:d * 6 + 6], 3, HD), ALU.mult),
                  "gdkb_ready" if d else "dve")
            for d in range(2):
                v(V.tensor_tensor(gd_kbe[:, :, d, :, :], gd_kb[:, :, d, :, :], bc(gd_e[:, 0, :, d * 6:d * 6 + 6], 3, HD), ALU.mult))
                v(V.tensor_tensor(gd_ks[:, :, d, :, :], k4, bc(gd_e[:, 1, :, d * 6:d * 6 + 6], 3, HD), ALU.mult))
                for t in range(T):
                    v(V.scalar_tensor_tensor(out=gd_vb[:, t, d, :, :], in0=gd[:, t, 768:1152].rearrange("p (h n) -> p h n", h=GNH),
                                             scalar=0.5, in1=bc(beta[:, t, d * 6:d * 6 + 6], 2, HD), op0=ALU.mult, op1=ALU.mult))
            for t in range(T):
                for d in range(2):
                    for z in range(2):
                        n = ("gl", t, d, z)
                        b = full(dve, n)[:, 0:384].rearrange("p (r n) -> p r n", r=3)
                        c = gd_c[:, t, d * 6 + z:d * 6 + 6:2]
                        v(V.tensor_tensor(gd_att[:, t, d, 3 * z:3 * z + 3, :], b, bc(c, 2, P), ALU.subtract), free(n))
                flat = gd_att[:, t, :, :, :].rearrange("p d h n -> p (d h n)")
                v(V.tensor_scalar(flat, flat, 0.0, None, ALU.min), "gdd_ready")
            for t in range(T):
                dve.wait_ge(ev("gdx_ready"), t + 1)
                for d in range(2):
                    v(V.tensor_tensor(gd_a[:, t, d, :, :], gd_att[:, t, d, :, :], bc(nstrict[:, d, :], 1, GNH), ALU.mult))
                    v(V.tensor_tensor(gd_att[:, t, d, :, :], gd_att[:, t, d, :, :], bc(causal[:, d, :], 1, GNH), ALU.mult))
            for t in range(T):
                for d in range(2):
                    for z in range(2):
                        n = ("kk", t, d, z)
                        b = full(dve, n)[:, 0:384].rearrange("p (r n) -> p r n", r=3)
                        a3 = gd_a[:, t, d, 3 * z:3 * z + 3, :]
                        v(V.tensor_tensor(a3, a3, b, ALU.mult), free(n))
            for t in range(T):
                for z in range(2):
                    n = ("kq", t, z)
                    b = full(dve, n)[:, 0:384].rearrange("p (r n) -> p r n", r=3)
                    for d in range(2):
                        a3 = gd_att[:, t, d, 3 * z:3 * z + 3, :]
                        v(V.tensor_tensor(a3, a3, b, ALU.mult), free(n) if d else "dve")
            dve.wait_ge(ev("level_ready"), 1)
            for t in range(T):
                for d in range(2):
                    inv = gd_inv[1][:, t, d, :, :]
                    v(V.tensor_copy(inv, bc(ident[:, :], 1, GNH)))
                    v(V.copy_predicated(inv, bc(level[:, d, 0, :], 1, GNH), gd_a[:, t, d, :, :]),
                      "inv0_ready" if (t, d) == (1, 1) else "dve")
            GROUPS = [(t, d, z) for t in range(T) for d in range(2) for z in range(2)]
            for k in range(1, 6):
                for g in GROUPS:
                    t, d, z = g
                    for kind, which, side in (("ty", 0, 1 - d), ("tz", 1, d))[k == 5:]:
                        n = (kind, k, *g)
                        b = full(dve, n)[:, 0:384].rearrange("p (r n) -> p r n", r=3)
                        v(V.copy_predicated(gd_inv[which][:, t, d, 3 * z:3 * z + 3, :], bc(level[:, side, k, :], 1, 3), b), free(n))
            copied(dve, *[(n, t, d) for n in ("gu2", "gw") for t in range(T) for d in range(2)], "gdec2")
            v(V.memset(gd_st[:, 0, :, :, :], 0.0))
            for j in range(4):
                for d in range(2):
                    n = j if d == 0 else 3 - j
                    t, r = n // 2, CH * (n % 2)
                    dst, u = gd_vn[r:r + CH, t, d, :, :], gd_u[r:r + CH, t, d, :, :]
                    if j:
                        name = ("ws", j, d)
                        b = full(dve, name, 2).rearrange("p (z n) -> p z n", z=2)[r:r + CH, :, 0:192]
                        b = b.rearrange("p z (r n) -> p z r n", r=3)
                        by = "p (r z) n -> p z r n"
                        v(V.tensor_tensor(dst.rearrange(by, z=2), u.rearrange(by, z=2), b, ALU.subtract), free(name))
                    else:
                        v(V.tensor_copy(dst, u), "vn0_ready")
                for d in range(2):
                    n = j if d == 0 else 3 - j
                    if j < 3:
                        name = ("kv", j, d)
                        b = full(dve, name)[:, 0:192].rearrange("p (r n) -> p r n", r=3)
                        new = gd_st[:, j + 1, d, :, :]
                        if j:
                            v(V.tensor_tensor(new, gd_st[:, j, d, :, :], bc(gd_dec[:, n, d, :], 2, HD), ALU.mult))
                            v(V.tensor_tensor(new, new, b, ALU.add), free(name))
                        else:
                            v(V.tensor_copy(new, b), free(name))
            for t in range(T):
                for d in range(2):
                    n = ("oi", t, d)
                    b = full(dve, n, 2).rearrange("p (z n) -> p z n", z=2)[:, :, 0:192].rearrange("p z (r n) -> p z r n", r=3)
                    dst = gd_o[:, t, d, :, :].rearrange("p (r z) n -> p z r n", z=2)
                    w = gd_e[:, 0, t, d * 6:d * 6 + 6].rearrange("p (r z) -> p z r", z=2)
                    v(V.tensor_tensor(dst, b, bc(w, 3, HD), ALU.mult), free(n))
                    n = ("oa", t, d)
                    dst = gd_o[:, t, d, :, :].rearrange("p h n -> p (h n)")
                    v(V.tensor_tensor(dst, dst, full(dve, n)[:, 0:384], ALU.add), free(n))
            head_norm(gd_o, GNH, 640, gd_w, z2, False)

            low_rows(("yT2",), 1.0)
            add_x(("wo2",))
            normalise(4)
            turned(4, R_XA, hT)
            for t in range(T):
                for g in range(2):
                    n = ("xs", t, g)
                    b = full(dve, n).rearrange("p (h n) -> p h n", h=2)
                    v(V.tensor_reduce(smax[:, 0:2], b, X, ALU.max))
                    v(V.tensor_tensor(x_s[:, t, 2 * g:2 * g + 2, :], b, bc(smax[:, 0:2], 2, S), ALU.subtract), free(n))
            for t in range(T):
                dve.wait_ge(ev("xe_ready"), t + 1)
                v(V.tensor_reduce(ssum[:, 0:XH], x_s[:, t, :, :], X, ALU.add))
                v(V.reciprocal(ssum[:, 0:XH], ssum[:, 0:XH]))
                v(V.tensor_tensor(x_s[:, t, :, :], x_s[:, t, :, :], bc(ssum[:, 0:XH], 2, S), ALU.mult), "xp_ready")
            for h in range(XH):
                b = full(dve, ("xo", h)).rearrange("p (a b) -> p a b", a=2)
                low(("xo", h), b, x_oT[:, 1, 2 * h:2 * h + 2, :], x_oT[:, 0, 2 * h:2 * h + 2, :], 1.0)
            add_x(("wxo",))
            normalise(5)
            turned(5, R_FFN, hT)
            for i in range(16):
                dve.wait_ge(ev("h1hi_ready"), i + 1)
                v(V.tensor_tensor(h1T[:, 1, 2 * i:2 * i + 2, :], h1[:, i % 4, :, :], plain(h1T[:, 0, 2 * i:2 * i + 2, :]),
                                  ALU.subtract), "h1_ready")
            add_x(("f2",))
            inverse_rms(6)
            dve.wait_ge(ev("tail_in"), 16)
            for t in range(T):
                v(V.scalar_tensor_tensor(out=xn[:, t * D:(t + 1) * D], in0=x[:, t, :], scalar=rout[:, t:t + 1], in1=out_g,
                                         op0=ALU.mult, op1=ALU.mult), "out_ready")

        @block.scalar
        def _(act):
            AC = nc.scalar.activation

            def a(ins, name="act"):
                done(act, ins, name)

            def quad(tag):
                return [(*tag, t, h) for t in range(T) for h in range(2)]

            def squares(src=None, added=None):
                src = x if src is None else src
                norms = made.get("ssq_ready", 0) // T
                if norms:
                    act.wait_ge(ev("normT_ready"), 4 * norms)
                for t in range(T):
                    if not norms:
                        act.wait_ge(ev("x_in"), 16 * T)
                    if added:
                        copied(act, (*added, t, 0), (*added, t, 1))
                    a(AC(tmp[:, 0:D], src[:, t, :], ACT.Square, accum_out=ssq[:, t:t + 1]), "ssq_ready")

            hi_next = [0]

            def weights_hi(n=CHUNKS):
                for _ in range(n):
                    c = hi_next[0]
                    hi_next[0] += 1
                    act.wait_ge(ev(f"raw_full{c % RAW}"), 16 * (c // RAW + 1))
                    if c >= RING_HI:
                        act.wait_ge(*release[c - RING_HI])
                    AC(chunk_view(ring_hi, RING_HI, c), chunk_view(ring, RAW, c), ACT.Copy).then_inc(ev("whi_ready"), 1)

            def norm_hi(i, dst, normT=normT):
                for h in range(2):
                    for t in range(T):
                        copied(act, ("xT", i, t, h))
                        a(AC(dst[:, 0, 4 * h:4 * h + 4, t * P:(t + 1) * P], normT[:, 4 * h:4 * h + 4, t * P:(t + 1) * P], ACT.Copy),
                          "normhi_ready")

            def high(name, dst, shape, scale=1.0):
                b = full(act, name).rearrange("p (a b) -> p a b", a=shape)
                a(AC(dst, b, ACT.Copy, scale=scale), "hi_made")

            def copy_out(name, dst, n, shape=None, scale=1.0, func=ACT.Copy, rows_=P, banks=1):
                b = full(act, name, banks)[0:rows_, 0:n]
                if shape:
                    b = b.rearrange("p (a b) -> p a b", a=shape)
                a(AC(dst, b, func, scale=scale), free(name))

            for l in range(DEPTH):
                def p1(i):
                    c0, n, parts = SLOTS1[i]
                    n //= parts
                    for t in range(T):
                        for q in range(parts):
                            copy_out(("p1", l, i, t, q), proj[:, t, c0 + q * n:c0 + (q + 1) * n], n)

                def gates(i):
                    for t in range(T):
                        copy_out(("gate", l, i, t, 0), gate[:, t, i * BANK:(i + 1) * BANK], BANK, scale=0.5, func=ACT.Tanh)

                if l == 0:
                    squares()
                else:
                    weights_hi(3)
                    squares(added=("wo", l - 1))
                weights_hi(1 if l else CHUNKS)
                norm_hi(l, hT)
                weights_hi()
                p1(0)
                for t in range(T):
                    a(AC(tmp[:, 0:256], proj[:, t, COL_CQ:COL_CQ + 256], ACT.Square, accum_out=ssq[:, 4 + t:5 + t]))
                for t in range(T):
                    a(AC(tmp[:, 0:128], proj[:, t, COL_CKV:COL_CKV + 128], ACT.Square, accum_out=ssq[:, 6 + t:7 + t]),
                      "cssq_ready" if t else "act")
                if l == 0:
                    act.wait_ge(ev("angle_ready"), 1)
                    a(AC(trig[:, 1, :, :], ang, ACT.Sin))
                    a(AC(trig[:, 0, :, :], at(arena, 64, T, HALF), ACT.Sin), "trig_ready")
                weights_hi()
                p1(1)
                weights_hi()
                p1(2)
                for t in range(T):
                    for h in range(2):
                        copy_out(("uq", l, t, h), qk[:, t, 4 * h:4 * h + 4, :], 384, shape=4)
                        n = ("ukv", l, t, h)
                        b = full(act, n).rearrange("p (h n) -> p h n", h=4)
                        a(AC(qk[:, t, MH + 4 * h:MH + 4 * h + 4, 0:NOPE], b[:, :, 0:NOPE], ACT.Copy))
                        a(AC(mv[:, t, h * 256:(h + 1) * 256].rearrange("p (h n) -> p h n", h=4), b[:, :, NOPE:2 * NOPE], ACT.Copy),
                          free(n))
                act.wait_ge(ev("layer_in"), 16 * N_LAYER_DMA * (l + 1))
                act.wait_ge(ev("const_ready"), 2)
                a(AC(bias_r[0:64, :], bgate[0:64, :], ACT.Copy))
                a(AC(sel_r[0:64, :, :], sel[:, :, :], ACT.Copy), "biashi_ready")
                act.wait_ge(ev("kr_ready"), l + 1)
                a(AC(at(arena, RC, 32, MQK), at(arena, RA, 32, MQK), ACT.Square), "qsq_ready")
                weights_hi()
                p1(3)
                weights_hi()
                p1(4)
                act.wait_ge(ev("qk_ready"), l + 1)
                a(AC(at(tmp, 0, T, 1024), proj[:, :, 0:1024], ACT.Square), "uvsq_ready")
                weights_hi()
                p1(5)
                act.wait_ge(ev("uvarg_ready"), l + 1)
                a(AC(tmp[:, 0:2048], tmp[:, 0:2048], ACT.Tanh, scale=GELU_C))
                a(AC(at(tmp, 2048, T, 512), proj[:, :, COL_Z:COL_Z + 512], ACT.Tanh, scale=0.5), "uvtanh_ready")
                for t in range(T):
                    for g in range(4):
                        copy_out(("qkT", l, t, g), qkT[0:MQK, 4 * g:4 * g + 4, t * P:(t + 1) * P], BANK, shape=4, rows_=MQK)
                weights_hi()
                p1(6)
                weights_hi()
                p1(7)
                for j in range(3):
                    copy_out(("sc", l, j), sc[:, j, :], 1024, scale=MQK ** -0.5, banks=2)
                copy_out(("glrT", l), glrT[0:GRANK, :], S, rows_=GRANK)
                for j in range(3):
                    act.wait_ge(ev("s_ready"), 3 * l + j + 1)
                    a(AC(sc[:, j, :], sc[:, j, :], ACT.Exp), "p_ready")
                weights_hi()
                gates(0)
                b = full(act, ("gg", l))
                flat = xn[:, 1536:2048]
                a(AC(flat, b, ACT.Abs))
                a(AC(flat, flat, ACT.Exp, scale=-1.0))
                a(AC(flat, flat, ACT.Ln, bias=1.0), "gln_ready")
                for j in range(3):
                    for q in range(2):
                        copy_out(("pT", l, j, q), pT[:, j, 4 * q:4 * q + 4, :], BANK, shape=4)
                weights_hi()
                gates(1)
                act.wait_ge(ev("tmp_free"), l + 1)
                a(AC(at(tmp, 1024, T, 512), proj[:, :, COL_ZB:COL_ZB + 512], ACT.Tanh, scale=0.5))
                a(AC(at(tmp, 2048, T, 512), proj[:, :, COL_ZC:COL_ZC + 512], ACT.Tanh, scale=0.5), "zb_ready")
                copy_out(("gb", l), flat, BANK)
                a(AC(gl_e, gl_b, ACT.Exp, scale=1.0 / GTAU))
                a(AC(gl_e2, gl_b, ACT.Exp, scale=-1.0 / GTAU), "ge_ready")
                b = full(act, ("gdec", l), 2).rearrange("p (z n) -> p z n", z=2)[:, :, 0:2]
                a(AC(gdec[:, :].rearrange("p (z n) -> p z n", z=2), b, ACT.Exp, scale=1.0 / GTAU), free(("gdec", l)))
                copied(act, ("gbl", l))
                a(AC(gl_b, gl_b, ACT.Exp, scale=1.0 / GTAU), "gks_ready")
                weights_hi()
                gates(2)
                for t in range(T):
                    copy_out(("gqkT", l, t), gl_qkT[:, :, t * P:(t + 1) * P], BANK, shape=4)
                weights_hi()
                gates(3)
                weights_hi()
                gates(4)
                weights_hi()
                gates(5)
                def branch_hi(i):
                    for t in range(T):
                        high(("yT", l, i, t), yT[:, i % 2, 0, :, t * P:(t + 1) * P], 4, BRANCH_SCALE[i])

                branch_hi(0)
                branch_hi(1)
                weights_hi()
                full(act, ("br", l, 0, T - 1, 1))
                branch_hi(2)
                weights_hi()
                weights_hi()
                for h in range(2):
                    for t in range(T):
                        high(("mT", l, t, h), hT[:, 0, 4 * h:4 * h + 4, t * P:(t + 1) * P], 4, 0.5)
                weights_hi()

            def p2(i):
                _, n, c = SLOTS2T[i]
                for t in range(T):
                    copy_out(("p2", i, t, 0), proj2[:, t, c:c + n], n)

            weights_hi(3)
            squares(added=("wo", DEPTH - 1))
            weights_hi(1)
            norm_hi(2, hT)
            for _ in SLOTS2:
                weights_hi()
            act.wait_ge(ev("conv_done"), 1)
            for q in range(3):
                a(AC(gd_th[:, 3 * q:3 * q + 3, :], conv[:, 3 * q:3 * q + 3, :], ACT.Tanh, scale=0.5), "convtanh_ready")
            weights_hi()
            p2(0)
            weights_hi()
            p2(1)
            a(AC(beta, proj2[:, :, K_GDB:K_GDB + 12], ACT.Tanh, scale=0.5))
            a(AC(zt, proj2[:, :, K_GDZ:K_GDZ + 384], ACT.Tanh, scale=0.5), "zt_ready")
            act.wait_ge(ev("sp_ready"), 1)
            a(AC(a_log, a_log, ACT.Exp))
            a(AC(spl, sp, ACT.Abs))
            a(AC(spl, spl, ACT.Exp, scale=-1.0))
            a(AC(spl, spl, ACT.Ln, bias=1.0), "spln_ready")
            copy_out("cum", cum, 80)
            act.wait_ge(ev("mem_in"), 16)
            squares(mem)
            weights_hi()
            p2(2)
            copy_out("mlrow", ml_row[0:MLH, :, :, :].rearrange("p q d n -> p (q d n)"), 1024, rows_=MLH, banks=2)
            weights_hi()
            p2(3)
            for t in range(T):
                for q in range(2):
                    copy_out(("naT", t, q), na_T[:, 3 * q:3 * q + 3, t * P:(t + 1) * P], 384, shape=3)
            weights_hi()
            p2(4)
            weights_hi()
            p2(5)
            a(AC(ot, proj2[:, :, C_MLO:C_MLO + 256], ACT.Tanh, scale=0.5))
            norm_hi(3, hT, mem_normT)
            copy_out("mlcol", ml_col[:, :, :, :].rearrange("p q t n -> p (q t n)"), 48)
            for t in range(T):
                n = ("mlT", t)
                b = full(act, n).rearrange("p (k n) -> p k n", k=4)
                a(AC(ml_T[:, 0:2, t * P:(t + 1) * P], b[:, 0:2, :], ACT.Copy))
                a(AC(ml_T[:, 2:4, t * P:(t + 1) * P], b[:, 2:4, :], ACT.Copy, scale=HD ** -0.5), free(n))
            for t in range(T):
                for q in range(3):
                    copy_out(("gT", t, q), gd[:, t, q * 384:(q + 1) * 384], 384)
            for t in range(T):
                act.wait_ge(ev("nas_ready"), t + 1)
                s1 = na_s[:, t, :, :, :].rearrange("p z r n -> p (z r n)")
                a(AC(s1, s1, ACT.Exp), "nap_ready")
            act.wait_ge(ev("mlarg_ready"), 1)
            e1 = ml_e[:, :, :, :].rearrange("p q t n -> p (q t n)")
            a(AC(e1, e1, ACT.Exp), "mle_ready")
            p1_ = ml_p[:, :, :, :, :].rearrange("p t d h n -> p (t d h n)")
            a(AC(p1_, p1_, ACT.Exp), "mlx_ready")
            for t in range(T):
                for q in range(3):
                    i = 12 * t + 4 * q
                    copy_out(("napT", t, q), na_pT[:, i:i + 4, :], BANK, shape=4)
            copy_out("mldec", ml_dec[:, :, :, :].rearrange("p a b c -> p (a b c)"), 16)
            act.wait_ge(ev("ml_done"), 1)
            a(AC(at(arena, 0, T, 12 * HD), gd[:, :, 0:768], ACT.Square), "gdsq_ready")
            act.wait_ge(ev("gdarg_ready"), 1)
            e1 = gd_e[:, :, :, :].rearrange("p q t n -> p (q t n)")
            a(AC(e1, e1, ACT.Exp), "gde_ready")

            def memory_k(i):
                weights_hi()
                for g in range(2):
                    copy_out(("xk", i, g), xk_T[:, i, g * BANK:(g + 1) * BANK], BANK)

            def memory_v(i):
                weights_hi()
                for t in range(T):
                    copy_out(("xv", i, t, 0), x_v[:, t, i * BANK:(i + 1) * BANK], BANK)

            memory_k(0)
            for t in range(T):
                for q in range(2):
                    copy_out(("gqT", t, q), gd_T[:, 3 * q:3 * q + 3, t * P:(t + 1) * P], 384, shape=3)
            for t in range(T):
                for d in range(2):
                    copy_out(("gkT", t, d), gd_kbT[:, t, d, :, :], 384, shape=3)
            for t in range(T):
                act.wait_ge(ev("gdd_ready"), t + 1)
                e1 = gd_att[:, t, :, :, :].rearrange("p d h n -> p (d h n)")
                a(AC(e1, e1, ACT.Exp), "gdx_ready")
            memory_k(1)
            memory_v(0)
            GROUPS = [(t, d, z) for t in range(T) for d in range(2) for z in range(2)]
            for t, d, z in GROUPS:
                copy_out(("inv0", t, d, z), gd_inv[0][:, t, d, 3 * z:3 * z + 3, :], 384, shape=3)
            for k in range(1, 6):
                for n, g in enumerate(GROUPS):
                    copy_out(("tx", k, *g), gd_x[:, n % 4, :, :], 384, shape=3)
            copy_out("gdec2", stat_all[:, :], 24)
            for t in range(T):
                for d in range(2):
                    copy_out(("gu2", t, d), gd_u[:, t, d, :, :], 384, shape=6)
                    copy_out(("gw", t, d), gd_wk[:, t, d, :, :], 384, shape=3)
            memory_v(1)
            act.wait_ge(ev("mixed_ready"), 1)
            for h in range(2):
                for t in range(T):
                    high(("yT2", t, h), hT[:, 0, 4 * h:4 * h + 4, t * P:(t + 1) * P], 4)
            weights_hi()
            weights_hi(3)
            squares(added=("wo2",))
            weights_hi(1)
            norm_hi(4, hT)
            for i in range(2):
                weights_hi()
                for g in range(2):
                    copy_out(("xq", i, g), xq_T[:, 4 * i + 2 * g:4 * i + 2 * g + 2, :], BANK, shape=2)
            for t in range(T):
                copied(act, ("xs", t, 0), ("xs", t, 1))
                s1 = x_s[:, t, :, :].rearrange("p h n -> p (h n)")
                a(AC(s1, s1, ACT.Exp, scale=XD ** -0.5), "xe_ready")
            for t in range(T):
                for g in range(2):
                    n = ("xpT", t, g)
                    b = full(act, n).rearrange("p (m h n) -> p m h n", m=2, h=2)
                    a(AC(x_pT[:, :, 2 * g:2 * g + 2, t * P:(t + 1) * P], b, ACT.Copy), free(n))
            for h in range(XH):
                high(("xo", h), x_oT[:, 0, 2 * h:2 * h + 2, :], 2)
            weights_hi()
            weights_hi(3)
            squares(added=("wxo",))
            weights_hi(1)
            norm_hi(5, hT)
            for i in range(8):
                weights_hi()
                for g in range(2):
                    k = 2 * i + g
                    if k >= 4:
                        act.wait_ge(ev("h1_ready"), k - 3)
                    n = ("f1", i, g)
                    b = full(act, n).rearrange("p (a b) -> p a b", a=2)
                    a(AC(h1[:, k % 4, :, :], b, ACT.Relu), free(n))
                    a(AC(h1[:, k % 4, :, :], h1[:, k % 4, :, :], ACT.Square))
                    a(AC(h1T[:, 0, 2 * k:2 * k + 2, :], h1[:, k % 4, :, :], ACT.Copy), "h1hi_ready")
            for _ in range(7):
                weights_hi()
            squares(added=("f2",))

        @block.gpsimd
        def _(pool):
            G = nc.gpsimd

            def g(ins, name="pool"):
                done(pool, ins, name)

            lo_next = [0]

            def weights_lo(upto):
                for c in range(lo_next[0], upto):
                    pool.wait_ge(ev("whi_ready"), c + 1)
                    if c >= RING_LO:
                        pool.wait_ge(*release[c - RING_LO])
                    G.tensor_tensor(chunk_view(ring_lo, RING_LO, c), chunk_view(ring, RAW, c), plain(chunk_view(ring_hi, RING_HI, c)),
                                    ALU.subtract).then_inc(ev("wlo_ready"), 1)
                lo_next[0] = upto

            pool.dma_start(posi[:, :], A["positions"].rearrange("a (t p) -> p (a t)", p=P),
                           allow_slow_non_contiguous=True).then_inc(ev("pos_in"), 16)
            g(G.memset(ones[:, :], 1.0))
            g(G.memset(bgate[:, :], 0.0))
            g(G.memset(ident[:, :], 0.0))
            g(G.affine_select(out=ident[:, :], in_=ident[:, :], compare_op=ALU.not_equal, fill=1.0, base=0,
                              pattern=[[-1, P]], channel_multiplier=1))
            for i in range(HALF):
                f = np.float32(1.0) / np.power(np.float32(THETA), np.float32(i) * np.float32(2.0) / np.float32(ROPE))
                g(G.memset(freq[:, i:i + 1], float(np.float32(f))), "const_ready" if i == HALF - 1 else "pool")
            def masks():
                g(G.memset(blk[:, :], 0.0))
                for r in (0, CH):
                    g(G.memset(blk[r:r + CH, r:r + CH], 1.0))
                g(G.affine_select(out=causal[:, 0, :], in_=blk[:, :], compare_op=ALU.is_ge, fill=0.0, base=0,
                                  pattern=[[1, P]], channel_multiplier=-1))
                g(G.affine_select(out=causal[:, 1, :], in_=blk[:, :], compare_op=ALU.is_ge, fill=0.0, base=0,
                                  pattern=[[-1, P]], channel_multiplier=1))
                g(G.memset(sel[:, :, :], 0.0))
                for r in (0, LOW_ROWS):
                    g(G.affine_select(out=sel[:, :, :], in_=sel[:, :, :], compare_op=ALU.not_equal, fill=1.0, base=-r,
                                      pattern=[[-1, NGATE], [0, P]], channel_multiplier=1))
                g(G.memset(level[:, :, :, :], 0), "const_ready")

            def levels():
                for k in range(6):
                    w = 2 ** k
                    for side in range(2):
                        m = level[:, side, k, :].rearrange("p (b w) -> p b w", w=2 * w)
                        m = m[:, :, w:2 * w] if side == 0 else m[:, :, 0:w]
                        g(G.memset(m, 1))
                        low = side * w
                        g(G.affine_select(out=m, in_=m, compare_op=ALU.is_ge, fill=0.0, base=-low, pattern=[[-2 * w, P // (2 * w)], [0, w]],
                                          channel_multiplier=1))
                        g(G.affine_select(out=m, in_=m, compare_op=ALU.is_ge, fill=0.0, base=low + w - 1,
                                          pattern=[[2 * w, P // (2 * w)], [0, w]], channel_multiplier=-1),
                          "level_ready" if (k, side) == (5, 1) else "pool")

            masks()
            FIRST2 = LAYER_CHUNKS * DEPTH
            weights_lo(FIRST2 + 3)
            copied(pool, *[("wo", DEPTH - 1, t, h) for t in range(T) for h in range(2)])
            g(G.memset(mirror, 0.0))
            for r in range(2):
                m64 = mirror[:, 64 * r:64 * r + 64]
                g(G.affine_select(out=m64, in_=m64, compare_op=ALU.not_equal, fill=1.0, base=-63 - 64 * r,
                                  pattern=[[1, 64]], channel_multiplier=1))
            g(G.memset(na_mask, 0.0))
            for r in range(2):
                lo, hi = na_mask[64 * r:64 * r + 64, 0:48], na_mask[64 * r:64 * r + 64, 16:64]
                g(G.affine_select(out=lo, in_=lo, compare_op=ALU.is_ge, fill=NEG, base=8, pattern=[[1, 48]], channel_multiplier=-1))
                g(G.affine_select(out=hi, in_=hi, compare_op=ALU.is_ge, fill=NEG, base=7 - 16, pattern=[[-1, 48]],
                                  channel_multiplier=1))
            for d in range(2):
                g(G.tensor_tensor(nstrict[:, d, :], ident[:, :], causal[:, d, :], ALU.subtract))
            g(G.memset(first[:, :, :], 0.0))
            for r in range(2):
                g(G.memset(first[64 * r:64 * r + 1, r, :], 1.0), "second_const" if r else "pool")
            mixed = FIRST2 + CHUNKS * (len(SLOTS2) + len(SLOTS2T))
            weights_lo(mixed)
            levels()
            weights_lo(mixed + 4 * CHUNKS + 3)
            pool.wait_ge(ev("mixed_ready"), 1)
            pool.dma_start(out_g, across(A["norm_out_w_2"], D)).then_inc(ev("tail_in"), 16)
            weights_lo(len(chunks))

        @block.sync
        def _(sp_):
            for t in range(T):
                sp_.dma_start(x[:, t, :], A["x"][0, t * P:(t + 1) * P, :]).then_inc(ev("x_in"), 16)
            for r0, src in ((R_NORM, A["norm_g"].rearrange("l (k p) -> (l k) p", p=P)),
                            (R_MIX, A["norm_mix_w_2"].rearrange("l (k p) -> (l k) p", p=P)),
                            (R_XA, A["norm_xa_w_2"].rearrange("l (k p) -> (l k) p", p=P)),
                            (R_MEM, A["norm_mem_w_2"].rearrange("l (k p) -> (l k) p", p=P)),
                            (R_FFN, A["norm_ffn_w_2"].rearrange("l (k p) -> (l k) p", p=P)),
                            (R_CQ, A["mla_cq_g"].rearrange("l (k p) -> (l k) p", p=P)),
                            (R_CKV, A["mla_ckv_g"]),
                            (R_SGB, A["sg_b"].rearrange("l g p -> (l g) p")),
                            (R_CONV, A["gdn_conv_w_2"][0].rearrange("k (j p) -> (k j) p", p=P))):
                sp_.dma_start(rows[r0:r0 + src.shape[0], :], src).then_inc(ev("rows_in"), 16)
            def layer_vectors(l):
                if l:
                    copied(sp_, *[("wo", l - 1, t, h) for t in range(T) for h in range(2)])
                else:
                    sp_.wait_ge(ev("const_ready"), 1)
                for dst, src in ((sgw, A["sg_w"][l].rearrange("g i j -> i g j")),
                                 (ln_g, across(A["sg_ln_g"][l], 512)),
                                 (ln_b, across(A["sg_ln_b"][l], 512)),
                                 (wuq, A["mla_w_uq"][l].rearrange("(k p) n -> p k n", p=P)),
                                 (wukv, A["mla_w_ukv"][l]),
                                 (qk_g[:, 0, :], across(A["mla_q_g"][l], MQK)),
                                 (qk_g[:, 1, :], across(A["mla_k_g"][l], MQK)),
                                 (o_g, across(A["gla_o_g"][l], GDV)),
                                 (wgu[0:GRANK, :], A["gla_w_gate"][l]),
                                 (bgu[0:1, :], A["gla_b_gate"][l:l + 1, :]),
                                 (bgate[0:NGATE, :], A["b_gate"][l].rearrange("(a n) -> a n", n=BANK)),
                                 (bgate[LOW_ROWS:LOW_ROWS + NGATE, :], A["b_gate"][l].rearrange("(a n) -> a n", n=BANK))):
                    sp_.dma_start(dst, src).then_inc(ev("layer_in"), 16)

            def second_vectors():
                copied(sp_, *[("wo", DEPTH - 1, t, h) for t in range(T) for h in range(2)])
                for dst, src in ((ml_w, across(A["ml_norm_w_2"][0], 256)), (gd_w, across(A["gdn_norm_w_2"][0], 384)),
                                 (if_b[:, 0:8], across(A["ml_i_bias_2"][0], 8)), (if_b[:, 8:16], across(A["ml_f_bias_2"][0], 8)),
                                 (dt_b, across(A["gdn_dt_bias_2"][0], 12)), (a_log, across(A["gdn_a_log_2"][0], 12))):
                    sp_.dma_start(dst, src).then_inc(ev("second_in"), 16)

            def relative_bias(t):
                bias = A["na_rel_bias_2"]
                rows_n, cols_n = bias.shape[2], bias.shape[3]
                for rl in range(2):
                    for h in range(NH):
                        off = h * rows_n * cols_n + (7 - 2 * t - rl) * cols_n + 15 - 63
                        src = bass.AP(tensor=bias.tensor, offset=bias.offset + off, ap=[[1, 64], [cols_n, 4], [1, GW]])
                        dst = na_raw[64 * rl:64 * rl + 64, t, h, :].rearrange("p (a b) -> p a b", a=4)
                        sp_.dma_start(dst, src).then_inc(ev("second_in"), 16)

            def memory():
                sp_.wait_ge(ev("normT_ready"), 4 * 3)
                sp_.dma_start(mem, A["mem_2"][0].rearrange("(t p) d -> p t d", p=P)).then_inc(ev("mem_in"), 16)

            first2 = LAYER_CHUNKS * DEPTH
            also = {3: lambda: layer_vectors(0), LAYER_CHUNKS + 3: lambda: layer_vectors(1), first2 + 3: second_vectors,
                    first2 + 14: memory,
                    first2 + 7: lambda: relative_bias(0), first2 + 11: lambda: relative_bias(1)}
            for c, (src, k, n) in enumerate(chunks):
                if c in also:
                    also[c]()
                if c >= RAW:
                    sp_.wait_ge(ev("wlo_ready"), c - RAW + 1)
                sp_.dma_start(chunk_view(ring, RAW, c), src).then_inc(ev(f"raw_full{c % RAW}"), 16)
            for t in range(T):
                sp_.wait_ge(ev("out_ready"), t + 1)
                sp_.dma_start(out[0, t * P:(t + 1) * P, :], xn[:, t * D:(t + 1) * D]).then_inc(ev("stored"), 16)
            sp_.wait_ge(ev("stored"), 16 * T)


_INS = ['x', 'positions', 'norm_g', 'w_in', 'b_gate', 'sg_ln_g', 'sg_ln_b', 'sg_w', 'sg_b', 'mla_cq_g', 'mla_ckv_g',
        'mla_w_uq', 'mla_w_ukv', 'mla_q_g', 'mla_k_g', 'gla_w_gate', 'gla_b_gate', 'gla_o_g', 'w_branch', 'w_out',
        'mem_2', 'norm_mix_w_2', 'w_in_2', 'na_rel_bias_2', 'ml_i_bias_2', 'ml_f_bias_2', 'ml_norm_w_2',
        'gdn_conv_w_2', 'gdn_a_log_2', 'gdn_dt_bias_2', 'gdn_norm_w_2', 'w_out_2', 'norm_xa_w_2', 'norm_mem_w_2',
        'w_xq_2', 'w_xkv_2', 'w_xo_2', 'norm_ffn_w_2', 'w_ff1_2', 'w_ff2_2', 'norm_out_w_2']


def kernel(**inputs):
    import numpy as _np
    import concourse.bacc as _bacc
    from concourse import mybir as _mybir
    from concourse.bass_utils import run_bass_kernel_spmd as _run

    nc = _bacc.Bacc("TRN2", target_bir_lowering=False, num_devices=1)
    arrays, args = {}, {}
    for name in _INS:
        a = _np.ascontiguousarray(inputs[name])
        arrays[f"in_{name}"] = a
        args[name] = nc.dram_tensor(f"in_{name}", a.shape, _mybir.dt.from_np(a.dtype), kind="ExternalInput").ap()
    out = nc.dram_tensor("out_0", (1, S, D), F32, kind="ExternalOutput").ap()
    build(nc, args, out)
    r = _run(nc, [arrays], core_ids=[0])
    return r.results[0]["out_0"]
```
